# Optimizing a Trainium2 kernel written in Bass

```python
import math
import jax
import jax.numpy as jnp
from jax import lax
import numpy as np
import jax, jax.numpy as jnp

D_MODEL = 2048
BATCH = 1
SEQ = 256
DEPTH = 1

HYENA_WIDTH = 1024
HYENA_ORDER = 2
HYENA_EMB = 33
HYENA_FILTER_HIDDEN = 64
HYENA_FAST_DECAY = 0.3
HYENA_SLOW_DECAY = 1.5
HYENA_TARGET = 1e-2
MLSTM_WIDTH = 1024
MLSTM_HEADS = 4
MLSTM_HEAD_DIM = MLSTM_WIDTH // MLSTM_HEADS
MLSTM_CHUNK = 128
N_MLSTM_GATES = 4 * MLSTM_HEADS
SHORT_CONV = 3
SHORT_CONV_CH = 3 * HYENA_WIDTH + 2 * MLSTM_WIDTH
IN_COLS = SHORT_CONV_CH + 2 * MLSTM_WIDTH + N_MLSTM_GATES + 2 * D_MODEL
FFN_HIDDEN = -(-8 * D_MODEL // (3 * 256)) * 256
RMS_EPS = 1e-6


def rmsnorm(x, w):
    xf = x.astype(jnp.float32)
    y = xf * lax.rsqrt(jnp.mean(xf * xf, axis=-1, keepdims=True) + RMS_EPS)
    return (y * w.astype(jnp.float32)).astype(x.dtype)

def centred_depthwise_conv(u, w, b):
    K = w.shape[0]
    pad = K // 2
    L = u.shape[1]
    up = jnp.pad(u, ((0, 0), (pad, pad), (0, 0)))
    out = up[:, 0:L] * w[0] + b
    for j in range(1, K):
        out = out + up[:, j:j + L] * w[j]
    return out

def hyena_filters(L, w1, b1, f1, w2, b2, f2, w3):
    f32 = jnp.float32
    t = jnp.linspace(0.0, 1.0, L, dtype=f32)[:, None]
    bands = (HYENA_EMB - 1) // 2
    omega = 2.0 * math.pi * jnp.arange(L, dtype=f32) / L
    freqs = jnp.linspace(1e-4, bands - 1, bands, dtype=f32)
    ang = omega[:, None] * freqs[None, :]
    z = jnp.concatenate([t, jnp.cos(ang), -jnp.sin(ang)], axis=-1)
    h = jnp.sin(f1.astype(f32) * (z @ w1.astype(f32) + b1.astype(f32)))
    h = jnp.sin(f2.astype(f32) * (h @ w2.astype(f32) + b2.astype(f32)))
    h = h @ w3.astype(f32)
    max_decay = math.log(HYENA_TARGET) / HYENA_FAST_DECAY
    min_decay = math.log(HYENA_TARGET) / HYENA_SLOW_DECAY
    deltas = jnp.linspace(min_decay, max_decay, HYENA_WIDTH, dtype=f32)
    window = jnp.exp(-t * jnp.abs(deltas)[None, :])
    return h.reshape(L, HYENA_ORDER, 2, HYENA_WIDTH) * window[:, None, None, :]

def two_sided_spectrum(h):
    h_fwd = h[:, :, 0]
    h_bwd = h[:, :, 1]
    kern = jnp.concatenate([h_fwd, jnp.zeros_like(h_fwd[:1]), h_bwd[:0:-1]], axis=0)
    return jnp.fft.rfft(kern, axis=0)

def long_conv(u, kf, bias):
    L = u.shape[1]
    uf = jnp.fft.rfft(u, n=2 * L, axis=1)
    y = jnp.fft.irfft(uf * kf[None], n=2 * L, axis=1)[:, :L]
    return y + u * bias

def mlstm_direction(q, k, v, i_pre, f_pre):
    B, L, H, dh = q.shape
    nc = L // MLSTM_CHUNK

    def to_chunks(t):
        return t.reshape(B, nc, MLSTM_CHUNK, H, -1).transpose(0, 3, 1, 2, 4)

    qc = to_chunks(q)
    kc = to_chunks(k) * (dh ** -0.5)
    vc = to_chunks(v)
    ig = to_chunks(i_pre[..., None])[..., 0]
    logf = to_chunks(jax.nn.log_sigmoid(f_pre)[..., None])[..., 0]
    b = jnp.cumsum(logf, axis=-1)
    b_last = b[..., -1]
    a = b_last[..., None] - b + ig
    m_loc = jnp.max(a, axis=-1)

    def step(carry, xs):
        C, n, m = carry
        bl, a_c, ml, k_c, v_c = xs
        m_new = jnp.maximum(bl + m, ml)
        keep = jnp.exp(bl + m - m_new)
        w = jnp.exp(a_c - m_new[..., None])
        C_new = keep[..., None, None] * C + jnp.einsum('bhsv,bhsk->bhvk', v_c * w[..., None], k_c)
        n_new = keep[..., None] * n + jnp.einsum('bhs,bhsk->bhk', w, k_c)
        return (C_new, n_new, m_new), (C, n, m)

    xs = tuple(jnp.moveaxis(t, 2, 0) for t in (b_last, a, m_loc, kc, vc))
    init = (jnp.zeros((B, H, dh, dh), jnp.float32),
            jnp.zeros((B, H, dh), jnp.float32),
            jnp.zeros((B, H), jnp.float32))
    _, (C_prev, n_prev, m_prev) = lax.scan(step, init, xs)
    C_prev = jnp.moveaxis(C_prev, 0, 2)
    n_prev = jnp.moveaxis(n_prev, 0, 2)
    m_prev = jnp.moveaxis(m_prev, 0, 2)

    pos = jnp.arange(MLSTM_CHUNK)
    lower = pos[:, None] >= pos[None, :]
    dlog = b[..., :, None] - b[..., None, :] + ig[..., None, :]
    dlog = jnp.where(lower, dlog, -jnp.inf)
    inter = b + m_prev[..., None]
    m_j = jnp.maximum(inter, jnp.max(dlog, axis=-1))
    s = jnp.einsum('bhcjd,bhcsd->bhcjs', qc, kc) * jnp.exp(dlog - m_j[..., None])
    inter_w = jnp.exp(inter - m_j)
    num = (jnp.einsum('bhcjs,bhcsv->bhcjv', s, vc)
           + inter_w[..., None] * jnp.einsum('bhcjk,bhcvk->bhcjv', qc, C_prev))
    den = jnp.sum(s, axis=-1) + inter_w * jnp.einsum('bhcjk,bhck->bhcj', qc, n_prev)
    h = num / jnp.maximum(jnp.abs(den), jnp.exp(-m_j))[..., None]
    return h.transpose(0, 2, 3, 1, 4).reshape(B, L, H, dh)

def first_inputs(seed: int = 0) -> dict:
    key = jax.random.key(seed)
    ks = jax.random.split(key, 24)
    f32 = jnp.float32

    def nrm(k, shape, scale):
        return jax.random.normal(k, shape, f32) * scale

    Ld = DEPTH
    H = MLSTM_HEADS
    FH = HYENA_FILTER_HIDDEN
    x = nrm(ks[0], (BATCH, SEQ, D_MODEL), 1.0)
    norm1_w = 1.0 + nrm(ks[1], (Ld, D_MODEL), 0.05)
    w_in = nrm(ks[2], (Ld, D_MODEL, IN_COLS), D_MODEL ** -0.5)
    conv_w = nrm(ks[3], (Ld, SHORT_CONV, SHORT_CONV_CH), SHORT_CONV ** -0.5)
    conv_b = nrm(ks[4], (Ld, SHORT_CONV_CH), 0.02)
    filt_w1 = nrm(ks[5], (Ld, HYENA_EMB, FH), HYENA_EMB ** -0.5)
    filt_b1 = nrm(ks[6], (Ld, FH), 0.1)
    filt_freq1 = 1.0 + nrm(ks[7], (Ld, FH), 0.05)
    filt_w2 = nrm(ks[8], (Ld, FH, FH), FH ** -0.5)
    filt_b2 = nrm(ks[9], (Ld, FH), 0.1)
    filt_freq2 = 1.0 + nrm(ks[10], (Ld, FH), 0.05)
    filt_w3 = nrm(ks[11], (Ld, FH, HYENA_ORDER * 2 * HYENA_WIDTH), 0.5 * SEQ ** -0.5)
    hyena_bias = nrm(ks[12], (Ld, HYENA_ORDER, HYENA_WIDTH), 0.5)
    f_base = jnp.linspace(3.0, 6.0, H, dtype=f32)
    zero_h = jnp.zeros((H,), f32)
    gate_base = jnp.stack([zero_h, f_base, zero_h, f_base])
    mlstm_gate_bias = gate_base[None] + nrm(ks[13], (Ld, 4, H), 0.1)
    w_branch_a = nrm(ks[14], (Ld, HYENA_WIDTH, D_MODEL), HYENA_WIDTH ** -0.5)
    w_branch_b = nrm(ks[15], (Ld, MLSTM_WIDTH, D_MODEL), MLSTM_WIDTH ** -0.5)
    w_out = nrm(ks[16], (Ld, D_MODEL, D_MODEL), D_MODEL ** -0.5)
    norm2_w = 1.0 + nrm(ks[17], (Ld, D_MODEL), 0.05)
    w_gate_up = nrm(ks[18], (Ld, D_MODEL, 2 * FFN_HIDDEN), D_MODEL ** -0.5)
    w_down = nrm(ks[19], (Ld, FFN_HIDDEN, D_MODEL), FFN_HIDDEN ** -0.5)
    norm_f_w = 1.0 + nrm(ks[20], (D_MODEL,), 0.05)
    return {'x': x, 'norm1_w': norm1_w, 'w_in': w_in, 'conv_w': conv_w, 'conv_b': conv_b,
            'filt_w1': filt_w1, 'filt_b1': filt_b1, 'filt_freq1': filt_freq1,
            'filt_w2': filt_w2, 'filt_b2': filt_b2, 'filt_freq2': filt_freq2, 'filt_w3': filt_w3,
            'hyena_bias': hyena_bias, 'mlstm_gate_bias': mlstm_gate_bias,
            'w_branch_a': w_branch_a, 'w_branch_b': w_branch_b, 'w_out': w_out,
            'norm2_w': norm2_w, 'w_gate_up': w_gate_up, 'w_down': w_down, 'norm_f_w': norm_f_w}

def first_block(x, norm1_w, w_in, conv_w, conv_b, filt_w1, filt_b1, filt_freq1, filt_w2, filt_b2,
              filt_freq2, filt_w3, hyena_bias, mlstm_gate_bias, w_branch_a, w_branch_b, w_out,
              norm2_w, w_gate_up, w_down, norm_f_w):
    B, L, _ = x.shape
    f32 = jnp.float32
    HW, MW, H, dh = HYENA_WIDTH, MLSTM_WIDTH, MLSTM_HEADS, MLSTM_HEAD_DIM
    for l in range(DEPTH):
        hn = rmsnorm(x, norm1_w[l])
        proj = hn @ w_in[l]
        conv_out = centred_depthwise_conv(proj[..., :SHORT_CONV_CH], conv_w[l], conv_b[l])
        rest = proj[..., SHORT_CONV_CH:]

        hy = conv_out[..., :3 * HW].astype(f32)
        hv, hx1, hx2 = hy[..., :HW], hy[..., HW:2 * HW], hy[..., 2 * HW:]
        filt = hyena_filters(L, filt_w1[l], filt_b1[l], filt_freq1[l], filt_w2[l], filt_b2[l],
                             filt_freq2[l], filt_w3[l])
        kf = two_sided_spectrum(filt)
        hb = hyena_bias[l].astype(f32)
        z = hx1 * long_conv(hv, kf[:, 0], hb[0])
        y_a = (hx2 * long_conv(z, kf[:, 1], hb[1])).astype(x.dtype)

        qk = jax.nn.silu(conv_out[..., 3 * HW:].astype(f32))
        q = qk[..., :MW].reshape(B, L, H, dh)
        k = qk[..., MW:].reshape(B, L, H, dh)
        v = rest[..., :MW].astype(f32).reshape(B, L, H, dh)
        o = jax.nn.sigmoid(rest[..., MW:2 * MW].astype(f32))
        g = (rest[..., 2 * MW:2 * MW + N_MLSTM_GATES].astype(f32).reshape(B, L, 4, H)
             + mlstm_gate_bias[l].astype(f32))
        h_fwd = mlstm_direction(q, k, v, g[:, :, 0], g[:, :, 1])
        flip = lambda t: jnp.flip(t, axis=1)
        h_bwd = flip(mlstm_direction(flip(q), flip(k), flip(v), flip(g[:, :, 2]), flip(g[:, :, 3])))
        y_b = (o * (h_fwd + h_bwd).reshape(B, L, MW)).astype(x.dtype)

        merge = rest[..., 2 * MW + N_MLSTM_GATES:]
        gate_a = jax.nn.sigmoid(merge[..., :D_MODEL])
        gate_b = jax.nn.sigmoid(merge[..., D_MODEL:])
        mixed = gate_a * (y_a @ w_branch_a[l]) + gate_b * (y_b @ w_branch_b[l])
        x = x + mixed @ w_out[l]

        hn2 = rmsnorm(x, norm2_w[l])
        gu = hn2 @ w_gate_up[l]
        x = x + (jax.nn.silu(gu[..., :FFN_HIDDEN]) * gu[..., FFN_HIDDEN:]) @ w_down[l]
    return rmsnorm(x, norm_f_w)


GLA_HEADS = 4
GLA_DK = D_MODEL // 16
GLA_DV = D_MODEL // 8
GLA_GATE_RANK = 16
GLA_GATE_TAU = 16.0
GLA_CHUNK = 64
CONV_WIDTH = 4

NSA_HEADS = 8
NSA_KV_HEADS = 2
NSA_GROUP = NSA_HEADS // NSA_KV_HEADS
NSA_HEAD_DIM = 128
CMP_BLOCK = 32
CMP_STRIDE = 16
CMP_HIDDEN = 128
SEL_BLOCK = 64
SEL_TOPK = 16
WINDOW = 512
Q_BLOCK = 128

D_FF = -(-8 * D_MODEL // (3 * 256)) * 256
EPS = 1e-6
NEG = -1e30

GLA_QK = GLA_HEADS * GLA_DK
GLA_VW = GLA_HEADS * GLA_DV
GLA_QKV = 2 * GLA_QK + GLA_VW
NSA_QW = NSA_HEADS * NSA_HEAD_DIM
NSA_KVW = NSA_KV_HEADS * NSA_HEAD_DIM
MIX_WIDTH = GLA_VW + NSA_QW
PROJ_SIZES = (GLA_QKV, GLA_GATE_RANK, GLA_VW, NSA_QW, NSA_KVW, NSA_KVW, NSA_KVW, NSA_KVW, NSA_KVW, NSA_KVW, 3 * NSA_HEADS)
PROJ_WIDTH = sum(PROJ_SIZES)


def rms_norm(u, g):
    uf = u.astype(jnp.float32)
    y = uf * lax.rsqrt(jnp.mean(uf * uf, axis=-1, keepdims=True) + EPS)
    return (y * g.astype(jnp.float32)).astype(u.dtype)

def causal_short_conv(u, w):
    s = u.shape[1]
    up = jnp.pad(u, ((0, 0), (CONV_WIDTH - 1, 0), (0, 0)))
    return sum(up[:, i:i + s] * w[i] for i in range(CONV_WIDTH))

def gla_mixer(q, k, v, gate_lr, out_gate, gate_w2, gate_b, norm_g):
    b_, s, _ = q.shape
    h, c = GLA_HEADS, GLA_CHUNK
    n_chunks = s // c
    log_a = jax.nn.log_sigmoid((gate_lr @ gate_w2 + gate_b).astype(jnp.float32)) / GLA_GATE_TAU

    def chunks(u, d):
        return u.reshape(b_, n_chunks, c, h, d).transpose(1, 0, 3, 2, 4)

    qc = chunks(q.astype(jnp.float32) * GLA_DK ** -0.5, GLA_DK)
    kc = chunks(k.astype(jnp.float32), GLA_DK)
    vc = chunks(v.astype(jnp.float32), GLA_DV)
    gc = chunks(log_a, GLA_DK)
    causal = jnp.tril(jnp.ones((c, c), dtype=bool))[:, :, None]

    def step(state, inp):
        qi, ki, vi, gi = inp
        b = jnp.cumsum(gi, axis=2)
        o_inter = jnp.einsum('bhtd,bhde->bhte', qi * jnp.exp(b), state)
        decay = jnp.exp(jnp.where(causal, b[:, :, :, None, :] - b[:, :, None, :, :], -jnp.inf))
        scores = jnp.einsum('bhtd,bhsd,bhtsd->bhts', qi, ki, decay)
        o_intra = jnp.einsum('bhts,bhse->bhte', scores, vi)
        b_last = b[:, :, -1:, :]
        state = (jnp.exp(b_last[:, :, 0, :])[..., None] * state
                 + jnp.einsum('bhsd,bhse->bhde', ki * jnp.exp(b_last - b), vi))
        return state, o_inter + o_intra

    state0 = jnp.zeros((b_, h, GLA_DK, GLA_DV), jnp.float32)
    _, o = lax.scan(step, state0, (qc, kc, vc, gc))
    o = o.transpose(1, 0, 3, 2, 4).reshape(b_, s, h, GLA_DV)
    o = rms_norm(o, norm_g) * jax.nn.silu(out_gate.astype(jnp.float32)).reshape(b_, s, h, GLA_DV)
    return o.reshape(b_, s, GLA_VW).astype(q.dtype)

def nsa_mixer(q, kc_raw, vc_raw, ks_raw, vs_raw, kw_raw, vw_raw, gate_logits,
              q_g, kc_g, ks_g, kw_g, k_pos, k_w1, k_w2, v_pos, v_w1, v_w2):
    b_, s, _ = q.shape
    hk, g, dh = NSA_KV_HEADS, NSA_GROUP, NSA_HEAD_DIM
    n_cmp = (s - CMP_BLOCK) // CMP_STRIDE + 1
    n_sel_blocks = s // SEL_BLOCK
    n_sel = min(SEL_TOPK, n_sel_blocks)
    scale = dh ** -0.5

    def heads(u, n):
        return u.reshape(b_, s, n, dh).transpose(0, 2, 1, 3)

    qh = rms_norm(heads(q, NSA_HEADS), q_g).reshape(b_, hk, g, s, dh)

    cmp_idx = jnp.arange(n_cmp)[:, None] * CMP_STRIDE + jnp.arange(CMP_BLOCK)[None, :]

    def compress(u, pos, w1, w2):
        blocks = u[:, :, cmp_idx] + pos
        flat = blocks.reshape(b_, hk, n_cmp, CMP_BLOCK * dh)
        return jax.nn.silu(flat @ w1) @ w2

    k_cmp = rms_norm(compress(heads(kc_raw, hk), k_pos, k_w1, k_w2), kc_g)
    v_cmp = compress(heads(vc_raw, hk), v_pos, v_w1, v_w2)
    cmp_end = jnp.arange(n_cmp) * CMP_STRIDE + CMP_BLOCK - 1

    c_start = jnp.arange(n_cmp)[:, None] * CMP_STRIDE
    s_start = jnp.arange(n_sel_blocks)[None, :] * SEL_BLOCK
    overlap = jnp.clip(jnp.minimum(c_start + CMP_BLOCK, s_start + SEL_BLOCK)
                       - jnp.maximum(c_start, s_start), 0, None).astype(jnp.float32) / CMP_STRIDE

    k_sel = rms_norm(heads(ks_raw, hk), ks_g).reshape(b_, hk, n_sel_blocks, SEL_BLOCK, dh)
    v_sel = heads(vs_raw, hk).reshape(b_, hk, n_sel_blocks, SEL_BLOCK, dh)
    win_pad = ((0, 0), (0, 0), (WINDOW, 0), (0, 0))
    k_win = jnp.pad(rms_norm(heads(kw_raw, hk), kw_g), win_pad)
    v_win = jnp.pad(heads(vw_raw, hk), win_pad)
    gates = jax.nn.sigmoid(gate_logits.astype(jnp.float32)).reshape(b_, s, hk, g, 3).transpose(0, 2, 3, 1, 4)

    gather_blocks = jax.vmap(jax.vmap(lambda blk, ix: blk[ix]))
    sel_offsets = jnp.arange(SEL_BLOCK)
    win_offsets = jnp.arange(WINDOW + Q_BLOCK)
    sel_ids = jnp.arange(n_sel_blocks)

    def query_block(s0):
        t = s0 + jnp.arange(Q_BLOCK)
        qb = lax.dynamic_slice_in_dim(qh, s0, Q_BLOCK, axis=3)

        sc = jnp.einsum('bhgqd,bhnd->bhgqn', qb, k_cmp).astype(jnp.float32) * scale
        mc = cmp_end[None, :] <= t[:, None]
        pc = jax.nn.softmax(jnp.where(mc, sc, NEG), axis=-1) * mc
        o_cmp = jnp.einsum('bhgqn,bhnd->bhgqd', pc.astype(v_cmp.dtype), v_cmp)

        imp = jnp.einsum('bhgqn,nj->bhqj', pc, overlap)
        jt = (t // SEL_BLOCK)[:, None]
        forced = (sel_ids == 0) | (sel_ids == jt) | (sel_ids == jt - 1)
        imp = jnp.where(sel_ids > jt, -jnp.inf, jnp.where(forced, jnp.inf, imp))
        _, idx = lax.top_k(imp, n_sel)
        ks = gather_blocks(k_sel, idx).reshape(b_, hk, Q_BLOCK, n_sel * SEL_BLOCK, dh)
        vs = gather_blocks(v_sel, idx).reshape(b_, hk, Q_BLOCK, n_sel * SEL_BLOCK, dh)
        kpos = (idx[..., None] * SEL_BLOCK + sel_offsets).reshape(b_, hk, Q_BLOCK, n_sel * SEL_BLOCK)
        ms = (kpos <= t[:, None])[:, :, None]
        ss = jnp.einsum('bhgqd,bhqkd->bhgqk', qb, ks).astype(jnp.float32) * scale
        ps = jax.nn.softmax(jnp.where(ms, ss, NEG), axis=-1)
        o_sel = jnp.einsum('bhgqk,bhqkd->bhgqd', ps.astype(vs.dtype), vs)

        kwb = lax.dynamic_slice_in_dim(k_win, s0, WINDOW + Q_BLOCK, axis=2)
        vwb = lax.dynamic_slice_in_dim(v_win, s0, WINDOW + Q_BLOCK, axis=2)
        wpos = s0 - WINDOW + win_offsets
        dist = t[:, None] - wpos[None, :]
        mw = (wpos[None, :] >= 0) & (dist >= 0) & (dist < WINDOW)
        sw = jnp.einsum('bhgqd,bhkd->bhgqk', qb, kwb).astype(jnp.float32) * scale
        pw = jax.nn.softmax(jnp.where(mw, sw, NEG), axis=-1)
        o_win = jnp.einsum('bhgqk,bhkd->bhgqd', pw.astype(vwb.dtype), vwb)

        gb = lax.dynamic_slice_in_dim(gates, s0, Q_BLOCK, axis=3)
        return gb[..., 0:1] * o_cmp + gb[..., 1:2] * o_sel + gb[..., 2:3] * o_win

    n_blocks = s // Q_BLOCK
    out = lax.map(query_block, jnp.arange(n_blocks) * Q_BLOCK)
    out = out.transpose(1, 0, 4, 2, 3, 5).reshape(b_, s, NSA_QW)
    return out.astype(q.dtype)

def hybrid_layer(x, attn_norm_g, w_in, gla_conv_w, gla_gate_w2, gla_gate_b, gla_norm_g,
                 nsa_q_norm_g, nsa_kc_norm_g, nsa_ks_norm_g, nsa_kw_norm_g,
                 cmp_k_pos, cmp_k_w1, cmp_k_w2, cmp_v_pos, cmp_v_w1, cmp_v_w2,
                 w_out, ffn_norm_g, w_gate, w_up, w_down):
    n = rms_norm(x, attn_norm_g)
    proj = n @ w_in
    offsets = np.cumsum(PROJ_SIZES)[:-1].tolist()
    (g_qkv, g_lr, g_out, nq, kc, vc, ks, vs, kw, vw, ng) = jnp.split(proj, offsets, axis=-1)
    g_qkv = jax.nn.silu(causal_short_conv(g_qkv, gla_conv_w))
    gq, gk, gv = jnp.split(g_qkv, [GLA_QK, 2 * GLA_QK], axis=-1)
    gla_out = gla_mixer(gq, gk, gv, g_lr, g_out, gla_gate_w2, gla_gate_b, gla_norm_g)
    nsa_out = nsa_mixer(nq, kc, vc, ks, vs, kw, vw, ng,
                        nsa_q_norm_g, nsa_kc_norm_g, nsa_ks_norm_g, nsa_kw_norm_g,
                        cmp_k_pos, cmp_k_w1, cmp_k_w2, cmp_v_pos, cmp_v_w1, cmp_v_w2)
    h = x + jnp.concatenate([gla_out, nsa_out], axis=-1) @ w_out
    m = rms_norm(h, ffn_norm_g)
    return h + (jax.nn.silu(m @ w_gate) * (m @ w_up)) @ w_down

def second_inputs(seed: int = 0) -> dict:
    key = jax.random.key(seed)
    ks = jax.random.split(key, 22)

    def dense(k, shape, fan_in):
        return jax.random.normal(k, shape, jnp.float32) * fan_in ** -0.5

    def gain(k, d):
        return 1.0 + 0.02 * jax.random.normal(k, (DEPTH, d), jnp.float32)

    dh = NSA_HEAD_DIM
    return {
        'x': jax.random.normal(ks[0], (BATCH, SEQ, D_MODEL), jnp.float32),
        'attn_norm_g': gain(ks[1], D_MODEL),
        'w_in': dense(ks[2], (DEPTH, D_MODEL, PROJ_WIDTH), D_MODEL),
        'gla_conv_w': dense(ks[3], (DEPTH, CONV_WIDTH, GLA_QKV), CONV_WIDTH),
        'gla_gate_w2': dense(ks[4], (DEPTH, GLA_GATE_RANK, GLA_QK), GLA_GATE_RANK),
        'gla_gate_b': 0.02 * jax.random.normal(ks[5], (DEPTH, GLA_QK), jnp.float32),
        'gla_norm_g': gain(ks[6], GLA_DV),
        'nsa_q_norm_g': gain(ks[7], dh),
        'nsa_kc_norm_g': gain(ks[8], dh),
        'nsa_ks_norm_g': gain(ks[9], dh),
        'nsa_kw_norm_g': gain(ks[10], dh),
        'cmp_k_pos': 0.1 * jax.random.normal(ks[11], (DEPTH, CMP_BLOCK, dh), jnp.float32),
        'cmp_k_w1': dense(ks[12], (DEPTH, CMP_BLOCK * dh, CMP_HIDDEN), CMP_BLOCK * dh),
        'cmp_k_w2': dense(ks[13], (DEPTH, CMP_HIDDEN, dh), CMP_HIDDEN),
        'cmp_v_pos': 0.1 * jax.random.normal(ks[14], (DEPTH, CMP_BLOCK, dh), jnp.float32),
        'cmp_v_w1': dense(ks[15], (DEPTH, CMP_BLOCK * dh, CMP_HIDDEN), CMP_BLOCK * dh),
        'cmp_v_w2': dense(ks[16], (DEPTH, CMP_HIDDEN, dh), CMP_HIDDEN),
        'w_out': dense(ks[17], (DEPTH, MIX_WIDTH, D_MODEL), MIX_WIDTH),
        'ffn_norm_g': gain(ks[18], D_MODEL),
        'w_gate': dense(ks[19], (DEPTH, D_MODEL, D_FF), D_MODEL),
        'w_up': dense(ks[20], (DEPTH, D_MODEL, D_FF), D_MODEL),
        'w_down': dense(ks[21], (DEPTH, D_FF, D_MODEL), D_FF),
    }

def second_block(x, attn_norm_g, w_in, gla_conv_w, gla_gate_w2, gla_gate_b, gla_norm_g,
              nsa_q_norm_g, nsa_kc_norm_g, nsa_ks_norm_g, nsa_kw_norm_g,
              cmp_k_pos, cmp_k_w1, cmp_k_w2, cmp_v_pos, cmp_v_w1, cmp_v_w2,
              w_out, ffn_norm_g, w_gate, w_up, w_down):
    for l in range(DEPTH):
        x = hybrid_layer(x, attn_norm_g[l], w_in[l], gla_conv_w[l], gla_gate_w2[l], gla_gate_b[l],
                         gla_norm_g[l], nsa_q_norm_g[l], nsa_kc_norm_g[l], nsa_ks_norm_g[l],
                         nsa_kw_norm_g[l], cmp_k_pos[l], cmp_k_w1[l], cmp_k_w2[l], cmp_v_pos[l],
                         cmp_v_w1[l], cmp_v_w2[l], w_out[l], ffn_norm_g[l], w_gate[l], w_up[l],
                         w_down[l])
    return x


def setup_inputs(seed=0):
    out = dict(first_inputs(seed))
    for name, value in second_inputs(seed + 1).items():
        if name != "x":
            out[name + "_2"] = value
    return out


def reference(
    x, norm1_w, w_in, conv_w, conv_b, filt_w1, filt_b1, filt_freq1, filt_w2, filt_b2,
    filt_freq2, filt_w3, hyena_bias, mlstm_gate_bias, w_branch_a, w_branch_b, w_out, norm2_w,
    w_gate_up, w_down, norm_f_w, attn_norm_g_2, w_in_2, gla_conv_w_2, gla_gate_w2_2,
    gla_gate_b_2, gla_norm_g_2, nsa_q_norm_g_2, nsa_kc_norm_g_2, nsa_ks_norm_g_2,
    nsa_kw_norm_g_2, cmp_k_pos_2, cmp_k_w1_2, cmp_k_w2_2, cmp_v_pos_2, cmp_v_w1_2, cmp_v_w2_2,
    w_out_2, ffn_norm_g_2, w_gate_2, w_up_2, w_down_2,
):
    x = first_block(
        x, norm1_w, w_in, conv_w, conv_b, filt_w1, filt_b1, filt_freq1, filt_w2, filt_b2,
        filt_freq2, filt_w3, hyena_bias, mlstm_gate_bias, w_branch_a, w_branch_b, w_out,
        norm2_w, w_gate_up, w_down, norm_f_w,
    )
    return second_block(
        x, attn_norm_g_2, w_in_2, gla_conv_w_2, gla_gate_w2_2, gla_gate_b_2, gla_norm_g_2,
        nsa_q_norm_g_2, nsa_kc_norm_g_2, nsa_ks_norm_g_2, nsa_kw_norm_g_2, cmp_k_pos_2,
        cmp_k_w1_2, cmp_k_w2_2, cmp_v_pos_2, cmp_v_w1_2, cmp_v_w2_2, w_out_2, ffn_norm_g_2,
        w_gate_2, w_up_2, w_down_2,
    )


_drawn_inputs = setup_inputs


def setup_inputs(seed=0):
    import zlib

    import numpy as np

    out = dict(_drawn_inputs(seed))
    spreads = {}
    factors = {'filt_freq1': 2.897,
     'attn_norm_g_2': 4.616,
     'gla_gate_w2_2': 3.555,
     'gla_gate_b_2': 171.818,
     'gla_norm_g_2': 6.566,
     'nsa_q_norm_g_2': 8.0,
     'nsa_kc_norm_g_2': 200.0,
     'nsa_ks_norm_g_2': 25.232,
     'nsa_kw_norm_g_2': 23.407,
     'cmp_k_pos_2': 8.0,
     'cmp_v_pos_2': 21.688,
     'ffn_norm_g_2': 13.413}
    for name, (base, spread) in spreads.items():
        noise = np.random.default_rng([zlib.crc32(name.encode()), seed]).standard_normal(out[name].shape)
        drawn = base * np.exp(spread * noise) if base else spread * noise
        out[name] = jnp.asarray(drawn.astype(out[name].dtype))
    for name, factor in factors.items():
        out[name] = (out[name] * factor).astype(out[name].dtype)
    return out
```

```python
from contextlib import ExitStack
import math

import numpy as np
import concourse.bass as bass
from concourse import mybir

F32 = mybir.dt.float32
F32R = mybir.dt.float32r
I32 = mybir.dt.int32
ALU = mybir.AluOpType
ACT = mybir.ActivationFunctionType
AX = mybir.AxisListType

T = 256
KB = 1024
NEG = -1.0e30
EPS = 1e-6
RU = 16
SU = 8
NRAW = 3
NSPL = 4
AHEAD = 3

VECS = {}


def vec_layout():
    n = 0
    for name, k in (("norm1", 16), ("norm2", 16), ("normf", 16), ("attn", 16), ("ffn", 16),
                    ("cw0", 40), ("cw1", 40), ("cw2", 40), ("cb", 40), ("hb", 16),
                    ("gw0", 16), ("gw1", 16), ("gw2", 16), ("gw3", 16), ("gb", 4), ("gng", 2),
                    ("qg", 1), ("kcg", 1), ("ksg", 1), ("kwg", 1),
                    ("f1", 1), ("b1", 1), ("f2", 1), ("b2", 1), ("gbias", 1), ("rowmask", 1)):
        VECS[name] = (n, k)
        n += k
    return n


NVEC = vec_layout()


class Engine:

    def __init__(self, sem):
        self.sem = sem
        self.n = 0
        self.todo = []
        self.seen = {}

    def wait(self, after):
        for t in after:
            if t is None:
                continue
            sem, value = t
            if self.seen.get(id(sem), 0) < value:
                self.seen[id(sem)] = value
                self.todo.append(lambda e, s=sem, v=value: e.wait_ge(s, v))

    def __call__(self, fn, after=(), chain=True, inc=True):
        if chain and self.n:
            self.wait([(self.sem, self.n)])
        self.wait(after)
        if inc:
            self.n += 1
            self.todo.append(lambda e, f=fn, s=self.sem: f(e).then_inc(s, 1))
            return (self.sem, self.n)
        self.todo.append(fn)
        return None

    def last(self):
        return (self.sem, self.n)

    def play(self, e):
        for f in self.todo:
            f(e)


class Bank:

    def __init__(self, t):
        self.t = t
        self.rel = []


class Act:

    def __init__(self, hi, lo, kt):
        self.hi, self.lo = hi, lo
        self.t = [[] for _ in range(kt)]


def build(nc, A, out):
    ctx = ExitStack()
    with ctx:
        def sem(name):
            return ctx.enter_context(nc.semaphore(name))

        PE, AC, DV, GP, SP = (Engine(sem(f"s_{n}")) for n in ("pe", "act", "dve", "pool", "sp"))
        raw_sem = [sem(f"s_raw{i}") for i in range(NRAW)]

        base = (nc.sbuf_base + 31) // 32 * 32
        cur = [base]

        def at(name, shape, dt, off):
            return nc.alloc_sbuf_tensor_at(name, shape, dt, offset=off)

        def bump(name, shape, dt=F32):
            size = int(np.prod(shape[1:])) * 4
            t = at(name, shape, dt, cur[0])
            cur[0] += (size + 31) // 32 * 32
            return t

        RAW = bump("RAW", [128, NRAW, RU * 128])
        WH = bump("WH", [128, NSPL, SU * 128], F32R)
        WL = bump("WL", [128, NSPL, SU * 128], F32R)
        HNH = bump("HNH", [128, 16, T], F32R)
        HNL = bump("HNL", [128, 16, T], F32R)
        VEC = bump("VEC", [128, NVEC])
        ONES = bump("ONES", [128, 128])
        IDENT = bump("IDENT", [128, 128])
        TMP = bump("TMP", [128, 4, T])
        RSTD = bump("RSTD", [128, T])
        RF = bump("RF", [128, T])
        RTOK = bump("RTOK", [128, 2])
        xt_off = cur[0]
        XT = bump("XT", [128, 16, T])
        arena = cur[0]
        limit = nc.sbuf_usable_end

        def ar(name, shape, kb, dt=F32):
            size = int(np.prod(shape[1:])) * 4
            off = arena + int(kb * KB)
            assert off + size <= limit, (name, off + size - limit)
            return at(name, shape, dt, off)

        banks = [Bank(nc.alloc_psum_tensor(f"PB{i}", [128, 512], F32)) for i in range(8)]
        mains = banks[0:3]
        nbank = banks[3]
        sides = banks[4:8]
        turn = {"m": 0, "s": 0}

        def mbank():
            turn["m"] += 1
            return mains[turn["m"] % 3]

        def sbank():
            turn["s"] += 1
            return sides[turn["s"] % 4]

        def vec(name, j=0, p=128):
            n, k = VECS[name]
            assert j < k
            return VEC[0:p, n + j:n + j + 1]

        def tt(E, o, a, b, op, after=(), **k):
            return E(lambda e: e.tensor_tensor(o, a, b, op), after, **k)

        def ts(E, o, a, s1, s2, op0, op1=None, after=(), **k):
            if op1 is None:
                return E(lambda e: e.tensor_scalar(o, a, s1, None, op0), after, **k)
            return E(lambda e: e.tensor_scalar(o, a, s1, s2, op0, op1), after, **k)

        def stt(o, a, s, b, op0, op1, after=(), **k):
            return DV(lambda e: e.scalar_tensor_tensor(out=o, in0=a, scalar=s, in1=b, op0=op0, op1=op1),
                      after, **k)

        def cp(E, o, a, after=(), **k):
            if E is AC:
                return E(lambda e: e.activation(o, a, ACT.Copy), after, **k)
            return E(lambda e: e.tensor_copy(o, a), after, **k)

        def act(o, a, f, after=(), bias=None, scale=None, accum=None, **k):
            kw = {}
            if bias is not None:
                kw["bias"] = bias
            if scale is not None:
                kw["scale"] = scale
            if accum is not None:
                kw["accum_out"] = accum
            return AC(lambda e: e.activation(o, a, f, **kw), after, **k)

        def mm(o, l, r, start, stop, after=(), inc=False, skip=False):
            return PE(lambda e: e.matmul(o, l, r, start=start, stop=stop, skip_group_check=skip),
                      after, chain=False, inc=inc)

        def tr(o, a, ident, after=(), inc=False):
            return PE(lambda e: e.transpose(o, a, ident), after, chain=False, inc=inc)

        def recip(o, a, after=()):
            return DV(lambda e: e.reciprocal(o, a), after)

        def load(dst, src, after=()):
            s = sem(f"s_ld{len(loads)}")
            loads.append(s)
            SP.wait(after)
            SP.todo.append(lambda e: e.dma_start(dst, src).then_inc(s, 16))
            return (s, 16)

        loads = []

        def f32(ap):
            return ap.bitcast(F32)

        tmp_rel = [[] for _ in range(4)]
        tmp_n = [0]

        def tmp():
            i = tmp_n[0] % 4
            tmp_n[0] += 1
            return i, TMP[:, i, :], tmp_rel[i]

        def split(hi, lo, x, after=(), hi_after=()):
            a = cp(AC, hi, x, list(after) + list(hi_after))
            b = tt(DV, lo, x, f32(hi), ALU.subtract, list(after) + [a])
            return [a, b]

        order = []
        order += [("w_in_a", i) for i in range(56)]
        order += [("w_ga", i) for i in range(24)] + [("w_gb", i) for i in range(24)]
        order += [("w_out", i) for i in range(16)]
        for h in range(2):
            order += [("w_gu", 44 * h + i) for i in range(44)] + [("w_dn", 22 * h + i) for i in range(22)]
        order += [("w_in2", i) for i in range(44)] + [("w_cmp", i) for i in range(4)]
        order += [("w_out2", i) for i in range(16)]
        for h in range(2):
            order += [("w_gu2", 44 * h + i) for i in range(44)] + [("w_dn2", 22 * h + i) for i in range(22)]

        raw_used = [[] for _ in range(NRAW)]
        unit_pe = {}
        unit_ready = {}
        issued = [0]
        splits = [0]
        tile_at = [0]

        def issue_raw():
            n = issued[0]
            if n >= len(order):
                return
            name, i = order[n]
            slot = n % NRAW
            SP.wait(raw_used[slot])
            SP.todo.append(lambda e, s=slot, src=A[name][i]: e.dma_start(RAW[:, s, :], src)
                           .then_inc(raw_sem[s], 16))
            issued[0] += 1

        def do_split():
            u = splits[0]
            if u * SU >= len(order) * RU:
                return
            splits[0] += 1
            n, half = divmod(u, RU // SU)
            slot, sp = n % NRAW, u % NSPL
            landed = (raw_sem[slot], 16 * (n // NRAW + 1))
            src = RAW[:, slot, half * SU * 128:(half + 1) * SU * 128]
            free = [unit_pe.get(u - NSPL)]
            h = cp(AC, WH[:, sp, :], src, [landed] + free, chain=False)
            E = GP if u % 2 else DV
            lo = tt(E, WL[:, sp, :], src, f32(WH[:, sp, :]), ALU.subtract, [landed, h] + free, chain=False)
            unit_ready[u] = (h, lo)
            if half == RU // SU - 1:
                raw_used[slot] = [h, lo, unit_ready[u - 1][0], unit_ready[u - 1][1]]
                issue_raw()

        def tile():
            i = tile_at[0]
            tile_at[0] += 1
            u, r = divmod(i, SU)
            if r == 0:
                while splits[0] <= u + AHEAD - 1 + 0 and splits[0] * SU < len(order) * RU:
                    do_split()
            sl = u % NSPL
            return (WH[:, sl, r * 128:(r + 1) * 128], WL[:, sl, r * 128:(r + 1) * 128],
                    unit_ready[u][0], unit_ready[u][1], u if r == SU - 1 else None)

        def mm3(o, x, k, first, last, after=(), n=slice(0, T), skip=False):
            h, l, th, tl, end = tile()
            mm(o, h, x.hi[:, k, n], first, False, list(after) + x.t[k] + [th], skip=skip)
            mm(o, h, x.lo[:, k, n], False, False, skip=skip)
            t = mm(o, l, x.hi[:, k, n], False, last, [tl], inc=last or end is not None, skip=skip)
            if end is not None:
                unit_pe[end] = t
            return t

        def ntile(o, x, ks, after):
            t = None
            for i, k in enumerate(ks):
                t = mm3(o, x, k, i == 0, i == len(ks) - 1, after if i == 0 else ())
            return t

        def ntile_tok(bank, x, after):
            t = None
            for k in range(16):
                h, l, th, tl, end = tile()
                for c in range(2):
                    o = bank.t[:, c * 128:(c + 1) * 128]
                    s = slice(c * 128, (c + 1) * 128)
                    mm(o, x.hi[:, k, s], h, k == 0 and c == 0, False,
                       (list(after) if k == 0 else []) + x.t[k] + [th], skip=True)
                    mm(o, x.lo[:, k, s], h, False, False, skip=True)
                    t = mm(o, x.hi[:, k, s], l, False, k == 15 and c == 1, [tl],
                           inc=(c == 1 and (k == 15 or end is not None)), skip=True)
                if end is not None:
                    unit_pe[end] = t
            return t

        for _ in range(2):
            issue_raw()
        L = {}
        L["vec"] = load(VEC[:, :], A["vecs"])
        L["xT"] = [load(XT[:, 4 * i:4 * i + 4, :], A["xT"][:, 4 * i:4 * i + 4, :]) for i in range(4)]
        L["ident"] = load(IDENT[:, :], A["ident"])
        issue_raw()
        t_ones = GP(lambda e: e.memset(ONES[:, :], 1.0))

        HN = Act(HNH, HNL, 16)

        def sum_sq(x, k, bank, after=()):
            i, s, rel = tmp()
            a = act(s, x, ACT.Square, list(after) + rel)
            t = mm(bank.t[:, 0:T], ONES[:, :], s, k == 0, k == 15,
                   [a, t_ones] + (bank.rel if k == 0 else []), inc=True)
            tmp_rel[i] = [t]
            return t

        def make_hn(x, k, g, after=(), free=()):
            a = act(HNH[:, k, :], x, ACT.Copy, list(after) + list(free), scale=g)
            b = stt(HNL[:, k, :], x, g, f32(HNH[:, k, :]), ALU.mult, ALU.subtract, list(after) + [a])
            HN.t[k] = [a, b]

        def rsqrt_mean(dst, src, width, after=()):
            a = act(dst, src, ACT.Sqrt, after, bias=EPSC[:, 0:1], scale=1.0 / width)
            return recip(dst, dst, [a]), a

        EPSC = at("EPSC", [128, 8], F32, arena)
        t_eps = GP(lambda e: e.memset(EPSC[:, 0:1], EPS))
        arena = arena + 32

        def rstd_tok(bank):
            mm(bank.t[:, 0:1], RSTD[0:1, 0:128], ONES[0:1, 0:1], True, True, [t_rstd[0], t_ones] + bank.rel)
            t = mm(bank.t[:, 1:2], RSTD[0:1, 128:256], ONES[0:1, 0:1], True, True, inc=True)
            e = cp(DV, RTOK[:, :], bank.t[:, 0:2], [t])
            bank.rel = [e]
            return e

        t_rstd = [None]
        t_rtok = [None]

        for k in range(16):
            sum_sq(XT[:, k, :], k, nbank, [L["xT"][k // 4]])
            make_hn(XT[:, k, :], k, vec("norm1", k), [L["xT"][k // 4], L["vec"]])
        t_x1 = [AC.last(), DV.last(), PE.last()]
        t_rstd[0], r = rsqrt_mean(RSTD[:, :], nbank.t[:, 0:T], 2048.0, [PE.last(), t_eps])
        nbank.rel = [r]
        t_rtok[0] = rstd_tok(sbank())

        DF = ar("DF", [128, 2, 2, T], 0)
        DG = ar("DG", [128, 2, 2, T], 4)
        V = ar("V", [128, 8, T], 8)
        X1 = ar("X1", [128, 8, T], 16)
        YAH = ar("YAH", [128, 8, T], 8, F32R)
        YAL = ar("YAL", [128, 8, T], 16, F32R)
        X2 = ar("X2", [128, 8, T], 24)
        WIN = ar("WIN", [128, 2, 2, T], 32)
        W3 = ar("W3", [64, 2, T], 36)
        FW = ar("FW", [128, 2, 2, T], 38)
        HSD = ar("HSD", [128, 2, 2, T], 42)
        KS = ar("KSP", [128, 2, 2, T], 46)
        M1 = ar("M1", [128, 2, T], 50)
        Y = ar("Y", [128, 2, 2, T], 52)
        UT = ar("UT", [128, 2, 2, 128], 56)
        H2 = ar("H2", [64, T], 58)
        ZT = ar("ZT", [33, T], 59)
        FW1 = ar("FW1", [64, 128], 60)
        HA = ar("HA", [64, 3, T], 61)
        VT = ar("VT", [128, 2, 1024], 64)
        O = ar("O", [128, 8, T], 72)
        QK = at("QK", [128, 16, T], F32, xt_off)

        L["df"] = load(DF[:, :, :, :], A["df"])
        L["dg"] = load(DG[:, :, :, :], A["dg"])
        L["zt"] = load(ZT[:, :], A["zt"])
        L["fw1"] = load(FW1[0:33, 0:64], A["filt_w1"])
        L["fw2"] = load(FW1[0:64, 64:128], A["filt_w2"])

        t_v = {}

        def scaled(bank, t, w=T):
            i, s, rel = tmp()
            a = tt(DV, s[:, 0:w], bank.t[:, 0:w], RSTD[:, 0:w], ALU.mult, [t, t_rstd[0]] + rel)
            bank.rel = [a]
            return i, s, a

        def conv3(dst, j):
            b = mbank()
            t = ntile(b.t[:, 0:T], HN, range(16), b.rel)
            i, s, a = scaled(b, t)
            c = act(dst, s, ACT.Identity, [a, L["vec"]], bias=vec("cb", j), scale=vec("cw1", j))
            d = stt(dst[:, 1:T], s[:, 0:T - 1], vec("cw0", j), dst[:, 1:T], ALU.mult, ALU.add, [c])
            d = stt(dst[:, 0:T - 1], s[:, 1:T], vec("cw2", j), dst[:, 0:T - 1], ALU.mult, ALU.add, [d])
            tmp_rel[i] = [d, c]
            return d

        def main_hyena():
            for j in range(24):
                dst = (V, X1, X2)[j // 8][:, j % 8, :]
                t_v[j] = conv3(dst, j)
                yield

        def sine(dst, src, P, after):
            k, r = HA[0:P, 1, :], HA[0:P, 2, :]
            magic = 12582912.0
            a = ts(DV, k, src, 1.0 / (2.0 * math.pi), magic, ALU.mult, ALU.add, after)
            a = ts(DV, k, k, magic, None, ALU.subtract)
            c1 = 6.28125
            c2 = float(np.float32(2.0 * math.pi - c1).view(np.uint32) & 0xFFFFF000)
            c2 = float(np.array(int(c2), np.uint32).view(np.float32))
            c3 = 2.0 * math.pi - c1 - c2
            stt(r, k, -c1, src, ALU.mult, ALU.add)
            stt(r, k, -c2, r, ALU.mult, ALU.add)
            stt(r, k, -c3, r, ALU.mult, ALU.add)
            a = ts(DV, r, r, 3.1415925, -3.1415925, ALU.min, ALU.max)
            return act(dst, r, ACT.Sin, [a])

        def side_filter():
            b = sbank()
            t = mm(b.t[0:64, 0:T], FW1[0:33, 0:64], ZT[:, :], True, True, [L["fw1"], L["zt"]] + b.rel, inc=True)
            a = ts(DV, HA[:, 0, :], b.t[0:64, 0:T], vec("b1", 0, 64), vec("f1", 0, 64), ALU.add, ALU.mult,
                   [t, L["vec"]])
            b.rel = [a]
            s = sine(H2[:, :], HA[:, 0, :], 64, [a])
            yield
            yield
            b = sbank()
            t = mm(b.t[0:64, 0:T], FW1[0:64, 64:128], H2[:, :], True, True, [L["fw2"], s] + b.rel, inc=True)
            a = ts(DV, HA[:, 0, :], b.t[0:64, 0:T], vec("b2", 0, 64), vec("f2", 0, 64), ALU.add, ALU.mult,
                   [t, L["vec"]])
            b.rel = [a]
            t_v["h2"] = sine(H2[:, :], HA[:, 0, :], 64, [a])
            yield

        def side_hyena():
            w3_rel, win_rel = [], []
            for qt in range(4):
                t_win = load(WIN[:, :, :, :], A["win"][qt], win_rel)
                for o in range(2):
                    c0 = qt * 256
                    t_w3 = load(W3[:, :, :], A["filt_w3"][:, o, :, c0:c0 + 256], w3_rel)
                    ends = []
                    for c in range(2):
                        b = sbank()
                        t = mm(b.t[:, :], H2[:, c * 128:(c + 1) * 128],
                               W3[:, :, :].rearrange("p a n -> p (a n)"), True, True,
                               [t_v["h2"], t_w3] + b.rel, inc=True)
                        w3_rel = [t]
                        a = tt(DV, FW[:, c, :, :].rearrange("p a n -> p (a n)"), b.t[:, :],
                               WIN[:, c, :, :].rearrange("p a n -> p (a n)"), ALU.mult, [t, t_win])
                        b.rel = [a]
                        win_rel = [a]
                        tt(DV, HSD[:, 0, c, :], FW[:, c, 0, :], FW[:, c, 1, :], ALU.add, [PE.last()])
                        ends.append(tt(DV, HSD[:, 1, c, :], FW[:, c, 1, :], FW[:, c, 0, :], ALU.subtract))
                    t_hsd = ends[-1]
                    yield
                    ua = []
                    b = sbank()
                    for ct in range(2):
                        for c in range(2):
                            ua = tr(b.t[:, (c * 2 + ct) * 128:(c * 2 + ct + 1) * 128],
                                    V[:, 2 * qt + ct, c * 128:(c + 1) * 128], IDENT[:, :],
                                    [t_v[2 * qt + ct], L["ident"]] + b.rel, inc=True)
                    t_ut = cp(AC, UT[:, :, :, :].rearrange("p a b c -> p (a b c)"), b.t[:, :], [ua])
                    b.rel = [t_ut]
                    for f in range(2):
                        b = sbank()
                        for ri in range(2):
                            for c in range(2):
                                t = mm(b.t[:, ri * 256:(ri + 1) * 256], DF[:, ri, c, f * 128:(f + 1) * 128],
                                       HSD[:, ri, c, :], c == 0, c == 1, [t_hsd, L["df"]] + b.rel,
                                       inc=(ri == 1 and c == 1))
                        a = cp(AC, KS[:, f, :, :].rearrange("p a n -> p (a n)"), b.t[:, :], [t])
                        b.rel = [a]
                        t_ks = a
                    yield
                    for f in range(2):
                        b = sbank()
                        for ri in range(2):
                            for c in range(2):
                                t = mm(b.t[:, ri * 256:(ri + 1) * 256], DF[:, ri, c, f * 128:(f + 1) * 128],
                                       UT[:, c, :, :].rearrange("p a n -> p (a n)"), c == 0, c == 1,
                                       [t_ut, L["df"]] + b.rel, inc=(ri == 1 and c == 1))
                        m = M1[:, :, :]
                        tt(DV, m.rearrange("p a n -> p (a n)"), b.t[:, :],
                           KS[:, f, :, :].rearrange("p a n -> p (a n)"), ALU.mult, [t, t_ks, PE.last()])
                        tt(DV, Y[:, f, 0, :], M1[:, 0, :], M1[:, 1, :], ALU.add)
                        tt(DV, M1[:, 0, :], b.t[:, 0:256], KS[:, f, 1, :], ALU.mult)
                        a = tt(DV, M1[:, 1, :], b.t[:, 256:512], KS[:, f, 0, :], ALU.mult)
                        b.rel = [a]
                        t_y = tt(DV, Y[:, f, 1, :], M1[:, 0, :], M1[:, 1, :], ALU.subtract)
                    yield
                    b = sbank()
                    for ct in range(2):
                        n = 0
                        for f in range(2):
                            for ri in range(2):
                                t = mm(b.t[:, ct * 256:(ct + 1) * 256], Y[:, f, ri, ct * 128:(ct + 1) * 128],
                                       DG[:, ri, f, :], n == 0, n == 3, [t_y, L["dg"]] + b.rel,
                                       inc=(ct == 1 and n == 3))
                                n += 1
                    for ct in range(2):
                        j = 2 * qt + ct
                        i, s, rel = tmp()
                        a = stt(s, V[:, j, :], vec("hb", o * 8 + j), b.t[:, ct * 256:(ct + 1) * 256],
                                ALU.mult, ALU.add, [t] + rel)
                        if ct == 1:
                            b.rel = [a]
                        if o == 0:
                            t_v[j] = tt(DV, V[:, j, :], s, X1[:, j, :], ALU.mult, [t_v[8 + j], a])
                            tmp_rel[i] = [t_v[j]]
                        else:
                            z = tt(DV, s, s, X2[:, j, :], ALU.mult, [t_v[16 + j], a])
                            YA.t[j] = split(YAH[:, j, :], YAL[:, j, :], s, [z])
                            tmp_rel[i] = YA.t[j]
                    yield

        YA = Act(YAH, YAL, 8)

        def silu_conv(dst, j):
            i, s, rel = tmp()
            t = conv3_to(s, j, rel)
            a = act(dst, s, ACT.Silu, [t] + t_x1)
            tmp_rel[i] = [a]
            return a

        def conv3_to(s, j, rel):
            DV.wait(rel)
            AC.wait(rel)
            return conv3(s, j)

        def small_cols(dst_bank, w, n, after):
            for c in range(2):
                o = dst_bank.t[:, c * 64:c * 64 + n]
                for k in range(16):
                    s = slice(c * 128, (c + 1) * 128)
                    mm(o, HNH[:, k, s], w[0][:, k, :], k == 0, False,
                       list(after) + HN.t[k] + dst_bank.rel, skip=True)
                    mm(o, HNL[:, k, s], w[0][:, k, :], False, False, skip=True)
                    t = mm(o, HNH[:, k, s], w[1][:, k, :], False, k == 15, inc=(k == 15 and c == 1), skip=True)
            return t

        SMR = at("SMR", [128, 16, 24], F32, arena + 81 * KB)
        SMH = at("SMH", [128, 16, 24], F32R, arena + int(82.5 * KB))
        SML = at("SML", [128, 16, 24], F32R, arena + 84 * KB)
        GTK = at("GTK", [128, 2, 24], F32, arena + int(85.5 * KB))
        assert arena + 86 * KB <= limit, (limit - arena) / KB

        def small_proj(src, n, after):
            t = load(SMR[:, :, 0:n], src, after)
            h = cp(AC, SMH[:, :, 0:n], SMR[:, :, 0:n], [t, PE.last()])
            l = tt(DV, SML[:, :, 0:n], SMR[:, :, 0:n], f32(SMH[:, :, 0:n]), ALU.subtract, [h, PE.last()])
            b = sbank()
            t = small_cols(b, (SMH[:, :, 0:n], SML[:, :, 0:n]), n, [h, l])
            for c in range(2):
                a = ts(DV, GTK[:, c, 0:n], b.t[:, c * 64:c * 64 + n], RTOK[:, c:c + 1], None, ALU.mult, None,
                       [t, t_rtok[0]])
            b.rel = [a]
            return a

        def main_qkvo():
            for j in range(16):
                t_v["qk", j] = silu_conv(QK[:, j, :], 24 + j)
                yield
            for j in range(8):
                b = mbank()
                t = ntile_tok(b, HN, b.rel)
                for c in range(2):
                    a = act(VT[:, c, j * 128:(j + 1) * 128], b.t[:, c * 128:(c + 1) * 128], ACT.Copy,
                            [t, t_rtok[0]], scale=RTOK[:, c:c + 1])
                b.rel = [a]
                t_v["vt", j] = a
                yield
            for j in range(8):
                b = mbank()
                t = ntile(b.t[:, 0:T], HN, range(16), b.rel)
                i, s, a = scaled(b, t)
                t_v["o", j] = act(O[:, j, :], s, ACT.Sigmoid, [a])
                tmp_rel[i] = [t_v["o", j]]
                yield
            t_v["g"] = small_proj(A["w_g"], 16, [])
            yield

        def run(main, side, every=1, steps=1):
            n = 0
            for _ in main:
                n += 1
                if n % every == 0:
                    for _ in range(steps):
                        next(side, None)
            for _ in side:
                pass

        run(main_hyena(), side_filter(), 2)
        run(main_qkvo(), side_hyena(), 1)
        t_hy = [DV.last(), AC.last(), PE.last()]

        MIX = ar("MIX", [128, 16, T], 24)
        MSK = ar("MSK", [128, 2, 2, T], 40)
        WW = ar("WW", [128, 2, 2, T], 44)
        PP = ar("PP", [128, 2, 2, T], 48)
        EMB = ar("EMB", [128, 2, T], 52)
        RR = ar("RR", [128, 2, T], 54)
        ROWS = ar("ROWS", [4, 4, 2, T], 56)
        G16 = ar("G16", [16, T], 52)
        SEL = ar("SEL", [4, 4, 128], 81)
        NN = ar("NN", [128, 2, T], 83)
        GTT = ar("GTT", [128, 4, 4], 85)
        YBH = ar("YBH", [128, 8, T], 0, F32R)
        YBL = ar("YBL", [128, 8, T], 72, F32R)
        YB = Act(YBH, YBL, 8)

        def side_mlstm():
            t_msk = load(MSK[:, :, :, :], A["mmask"], t_hy)
            t_sel = load(SEL[:, :, :], A["sel4"], [t_v["g"]])
            b = sbank()
            for c in range(2):
                t = tr(b.t[0:16, c * 128:(c + 1) * 128], GTK[:, c, 0:16], IDENT[:, :], [t_v["g"]] + b.rel, inc=True)
            a = ts(DV, G16[:, :], b.t[0:16, 0:T], vec("gbias", 0, 16), None, ALU.add, None, [t] + t_hy)
            b.rel = [a]
            yield
            bi, bf = sbank(), sbank()
            for d in range(2):
                mm(bi.t[0:4, d * T:(d + 1) * T], IDENT[0:16, 8 * d:8 * d + 4], G16[:, :], True, True, [a] + bi.rel)
            for d in range(2):
                t = mm(bf.t[0:4, d * T:(d + 1) * T], IDENT[0:16, 8 * d + 4:8 * d + 8], G16[:, :], True, True,
                       bf.rel, inc=True)
            r = [ROWS[:, i, :, :] for i in range(4)]
            fl = [ROWS[:, i, :, :].rearrange("p a n -> p (a n)") for i in range(4)]
            a = cp(AC, fl[3], bf.t[0:4, :], [t])
            a = stt(fl[0], fl[3], -1.0, fl[3], ALU.mult, ALU.max, [a])
            a = act(fl[0], fl[0], ACT.Exp, [a], scale=-1.0)
            a = act(fl[0], fl[0], ACT.Ln, [a], bias=1.0)
            a = stt(fl[0], fl[3], 0.0, fl[0], ALU.min, ALU.subtract, [a])
            bf.rel = [a]
            on = ONES[0:4, 0:1].broadcast_to([4, T])
            for d in range(2):
                x = r[0][:, d, :] if d == 0 else r[0][:, d, ::-1]
                y = r[1][:, d, :] if d == 0 else r[1][:, d, ::-1]
                a = DV(lambda e, x=x, y=y: e.tensor_tensor_scan(y, on, x, 0.0, ALU.mult, ALU.add), [t_ones])
            a = tt(DV, fl[2], bi.t[0:4, :], fl[1], ALU.subtract)
            bi.rel = [a]
            for d in range(2):
                x = r[2][:, d, :] if d == 0 else r[2][:, d, ::-1]
                y = r[3][:, d, :] if d == 0 else r[3][:, d, ::-1]
                a = DV(lambda e, x=x, y=y: e.tensor_tensor_scan(y, x, x, 0.0, ALU.max, ALU.max))
            a = tt(DV, fl[0], fl[1], fl[3], ALU.add)
            t_em = act(fl[0], fl[0], ACT.Exp, [a], scale=-1.0)
            a = ts(DV, fl[3], fl[3], -1.0, None, ALU.mult, None, [t_em])
            t_nm = a
            yield
            b = sbank()
            for d in range(2):
                for c in range(2):
                    j = d * 2 + c
                    t = mm(b.t[:, 4 * j:4 * j + 4], r[2][:, d, c * 128:(c + 1) * 128], IDENT[0:4, 0:4], True, True,
                           [t_nm] + b.rel, inc=True)
            t_gtt = cp(DV, GTT[:, :, :].rearrange("p a b -> p (a b)"), b.t[:, 0:16], [t])
            b.rel = [t_gtt]
            yield
            pe_last = None
            for h in range(4):
                bs, bn, be = sbank(), sbank(), sbank()
                for c in range(2):
                    for k in range(2):
                        q, kk = QK[:, 2 * h + k, :], QK[:, 8 + 2 * h + k, c * 128:(c + 1) * 128]
                        t_s = mm(bs.t[:, c * T:(c + 1) * T], kk, q, k == 0, k == 1,
                                 [t_v["qk", 2 * h + k], t_v["qk", 8 + 2 * h + k]] + bs.rel, inc=(k == 1))
                t_n = mm(bn.t[:, :], SEL[:, h, :], fl[3], True, True, [t_nm, t_sel] + bn.rel, inc=True)
                t_e = mm(be.t[:, :], SEL[:, h, :], fl[0], True, True, [t_em] + be.rel, inc=True)
                t_emb = cp(AC, EMB[:, :, :].rearrange("p a n -> p (a n)"), be.t[:, :], [t_e, DV.last()])
                be.rel = [t_emb]
                for d in range(2):
                    for c in range(2):
                        a = stt(WW[:, d, c, :], bn.t[:, d * T:(d + 1) * T], GTT[:, d * 2 + c, h:h + 1],
                                MSK[:, d, c, :], ALU.add, ALU.min, [t_n, t_gtt, t_msk])
                bn.rel = [a]
                a = act(WW[:, :, :, :].rearrange("p a b n -> p (a b n)"),
                        WW[:, :, :, :].rearrange("p a b n -> p (a b n)"), ACT.Exp, [a])
                for d in range(2):
                    p = stt(PP[:, d, :, :].rearrange("p b n -> p (b n)"), bs.t[:, :], 1.0 / 16.0,
                            WW[:, d, :, :].rearrange("p b n -> p (b n)"), ALU.mult, ALU.mult, [t_s, a, pe_last])
                bs.rel = [p]
                yield
                bd = sbank()
                nb = [sbank(), sbank()]
                for d in range(2):
                    cs = (0, 1) if d == 0 else (1, 0)
                    for n, c in enumerate(cs):
                        sl = slice(0, T) if n == 0 else (slice(128, T) if d == 0 else slice(0, 128))
                        o0 = d * T
                        t_d = mm(bd.t[:, o0 + sl.start:o0 + sl.stop], ONES[:, :], PP[:, d, c, sl],
                                 n == 0, n == 1, [p] + bd.rel, inc=(n == 1), skip=True)
                    for v in range(2):
                        for n, c in enumerate(cs):
                            sl = slice(0, T) if n == 0 else (slice(128, T) if d == 0 else slice(0, 128))
                            t_u = mm(nb[d].t[:, v * T + sl.start:v * T + sl.stop],
                                     VT[:, c, h * 256 + v * 128:h * 256 + (v + 1) * 128], PP[:, d, c, sl],
                                     n == 0, n == 1, [t_v["vt", 2 * h + v]] + nb[d].rel,
                                     inc=(n == 1), skip=True)
                pe_last = t_u
                rr = RR[:, :, :].rearrange("p a n -> p (a n)")
                tt(DV, rr, bd.t[:, :], EMB[:, :, :].rearrange("p a n -> p (a n)"), ALU.max, [t_d])
                a = stt(rr, bd.t[:, :], -1.0, rr, ALU.mult, ALU.max)
                bd.rel = [a]
                a = recip(RR[:, :, :].rearrange("p a n -> p (a n)"), RR[:, :, :].rearrange("p a n -> p (a n)"))
                for v in range(2):
                    i, s, rel = tmp()
                    a = tt(DV, NN[:, v, :], nb[0].t[:, v * T:(v + 1) * T], RR[:, 0, :], ALU.mult, [t_u])
                    a = tt(DV, s, nb[1].t[:, v * T:(v + 1) * T], RR[:, 1, :], ALU.mult, rel)
                    tt(DV, s, s, NN[:, v, :], ALU.add)
                    j = 2 * h + v
                    z = tt(DV, s, s, O[:, j, :], ALU.mult, [t_v["o", j]])
                    YB.t[j] = split(YBH[:, j, :], YBL[:, j, :], s, [z])
                    tmp_rel[i] = YB.t[j]
                nb[0].rel = nb[1].rel = [z]
                yield

        def branch(x, first):
            for n in range(16):
                b = mbank()
                ntile(b.t[:, 0:T], HN, range(16), b.rel)
                t2 = ntile(b.t[:, T:2 * T], x, range(8), [])
                i, s, a = scaled(b, t2)
                g = act(s, s, ACT.Sigmoid, [a])
                if first:
                    z = tt(DV, MIX[:, n, :], s, b.t[:, T:2 * T], ALU.mult, [g, t2] + t_hy)
                    tmp_rel[i] = [z]
                    b.rel = [a, z]
                else:
                    z = tt(DV, s, s, b.t[:, T:2 * T], ALU.mult, [g, t2])
                    b.rel = [a, z]
                    z = tt(DV, s, s, MIX[:, n, :], ALU.add)
                    MX.t[n] = split(MXH[:, n, :], MXL[:, n, :], s, [z], t_ml)
                    tmp_rel[i] = MX.t[n]
                yield

        run(branch(YA, True), side_mlstm(), 1)
        t_ml = [DV.last(), AC.last(), PE.last()]
        t_xt = [load(XT[:, 4 * i:4 * i + 4, :], A["xT"][:, 4 * i:4 * i + 4, :], t_ml) for i in range(4)]
        MXH = ar("MXH", [128, 16, T], 8, F32R)
        MXL = ar("MXL", [128, 16, T], 44, F32R)
        MX = Act(MXH, MXL, 16)
        t_mlg = t_ml
        for _ in branch(YB, False):
            pass

        def residual(x, ks, bank_after, n, finish):
            b = mbank()
            t = ntile(b.t[:, 0:T], x, ks, b.rel)
            a = tt(DV, XT[:, n, :], b.t[:, 0:T], XT[:, n, :], ALU.add, [t] + bank_after)
            b.rel = [a]
            if finish:
                finish(n, a)

        def norm_after(gname):
            late = []

            def f(n, a):
                late.append((n, a))
                make_hn(XT[:, n, :], n, vec(gname, n), [a], [PE.last()])
                if n > 0:
                    m, am = late[n - 1]
                    sum_sq(XT[:, m, :], m, nbank, [am])
                if n == 15:
                    sum_sq(XT[:, n, :], n, nbank, [a])
            return f

        def finish_rstd():
            t_rstd[0], r = rsqrt_mean(RSTD[:, :], nbank.t[:, 0:T], 2048.0, [PE.last()])
            nbank.rel = [r]

        f = norm_after("norm2")
        for n in range(16):
            residual(MX, range(16), [t_xt[n // 4]], n, f)
        finish_rstd()

        HDH = ar("HDH", [128, 22, T], 0, F32R)
        HDL = ar("HDL", [128, 22, T], 22, F32R)
        HD = Act(HDH, HDL, 22)
        SG = ar("SG", [128, 2, T], 44)
        HS = ar("HS", [128, 2, T], 46)

        def ffn(finish):
            used = [PE.last(), DV.last(), AC.last()]
            for half in range(2):
                for j in range(22):
                    b = mbank()
                    ntile(b.t[:, 0:T], HN, range(16), b.rel)
                    t = ntile(b.t[:, T:2 * T], HN, range(16), [])
                    i, s, a = scaled(b, t)
                    sg = SG[:, j % 2, :]
                    g = act(sg, s, ACT.Silu, [a] + used)
                    z = tt(DV, s, b.t[:, T:2 * T], RSTD[:, :], ALU.mult, [g])
                    b.rel = [z]
                    z = tt(DV, s, s, sg, ALU.mult)
                    HD.t[j] = split(HDH[:, j, :], HDL[:, j, :], s, [z], used)
                    tmp_rel[i] = HD.t[j]
                for n in range(16):
                    residual(HD, range(22), [], n, finish if half else None)
                used = [PE.last()]

        late2 = []
        nb2 = banks[7]

        def two_norms(n, a):
            b = ts(DV, XT[:, n, :], XT[:, n, :], vec("normf", n), None, ALU.mult, None, [a, AC.last()])
            make_hn(XT[:, n, :], n, vec("attn", n), [b], [PE.last()])

        def x_sq_first(n, a):
            i, s, rel = tmp()
            q = act(s, XT[:, n, :], ACT.Square, [a] + rel)
            t = mm(nbank.t[:, 0:T], ONES[:, :], s, n == 0, n == 15, [q] + (nbank.rel if n == 0 else []), inc=True)
            tmp_rel[i] = [t]
            two_norms(n, a)
            i, s, rel = tmp()
            q = act(s, XT[:, n, :], ACT.Square, [DV.last()] + rel)
            t = mm(nb2.t[:, 0:T], ONES[:, :], s, n == 0, n == 15, [q] + (nb2.rel if n == 0 else []), inc=True)
            tmp_rel[i] = [t]

        ffn(x_sq_first)
        t_rf, r = rsqrt_mean(RF[:, :], nbank.t[:, 0:T], 2048.0, [PE.last()])
        nbank.rel = [r]
        i, s, rel = tmp()
        a = tt(DV, s, RF[:, :], RF[:, :], ALU.mult, rel)
        a = tt(DV, s, s, nb2.t[:, 0:T], ALU.mult)
        nb2.rel = [a]
        t_ra, r = rsqrt_mean(RSTD[:, :], s, 2048.0, [a])
        tmp_rel[i] = [r]
        t_rstd[0] = tt(DV, RSTD[:, :], RSTD[:, :], RF[:, :], ALU.mult)
        t_rtok[0] = rstd_tok(sbank())
        t_b1 = [DV.last(), AC.last(), PE.last()]

        GQ = ar("GQ", [128, 4, T], 0)
        GK = ar("GK", [128, 4, T], 4)
        VTG = ar("VTG", [128, 2, 1024], 8)
        OG = ar("OG", [128, 8, T], 16)
        GG = ar("GG", [128, 4, T], 24)
        GB = ar("GB", [128, 4, T], 28)
        GE = ar("GE", [128, 4, T], 32)
        QE = ar("QE", [128, 4, T], 36)
        PT = ar("PT", [128, 2, 4, 128], 40)
        PT2 = ar("PT2", [128, 4, 128], 44)
        LM = ar("LM", [128, 7, 128], 46, I32)
        RST = ar("RST", [128, T], 49.5)
        LR = ar("LR", [16, T], 38)
        GW2 = ar("GW2", [16, 512], 36)
        MGH = ar("MGH", [128, 8, T], 50.5, F32R)
        MGL = ar("MGL", [128, 8, T], 58.5, F32R)
        NKC = ar("NKC", [128, 2, 2, T], 66.5)
        NKS = ar("NKS", [128, 2, 2, T], 70.5)
        NVT = ar("NVT", [128, 2, 2, 256], 74.5)
        MG = Act(MGH, MGL, 8)

        t_lm = load(LM[:, :, :], A["lmask"], t_b1)
        t_rst = load(RST[:, :], A["reset"], t_b1)
        t_gw2 = load(GW2[:, :], A["gla_gate_w2"], t_b1)

        def conv4(dst, j):
            b = mbank()
            t = ntile(b.t[:, 0:T], HN, range(16), b.rel)
            i, s, a = scaled(b, t)
            i2, y, rel = tmp()
            c = act(y, s, ACT.Copy, [a] + rel, scale=vec("gw3", j))
            for m in range(1, 4):
                d = stt(y[:, m:T], s[:, 0:T - m], vec(f"gw{3 - m}", j), y[:, m:T], ALU.mult, ALU.add, [c])
            tmp_rel[i] = [d, c]
            if dst is None:
                f = act(y, y, ACT.Silu, [d])
                return i2, y, f
            f = act(dst, y, ACT.Silu, [d] + t_b1)
            tmp_rel[i2] = [f]
            return f

        def transpose_v(i2, y, f, j):
            b = sbank()
            for c in range(2):
                t = tr(b.t[:, c * 128:(c + 1) * 128], y[:, c * 128:(c + 1) * 128], IDENT[:, :], [f] + b.rel,
                       inc=True)
            tmp_rel[i2] = [t]
            for c in range(2):
                a = cp(DV, VTG[:, c, j * 128:(j + 1) * 128], b.t[:, c * 128:(c + 1) * 128], [t] + t_b1)
            b.rel = [a]
            t_v["vtg", j] = a

        held = None
        for j in range(16):
            if j < 8:
                t_v["g", j] = conv4((GQ if j < 4 else GK)[:, j % 4, :], j)
            else:
                new = conv4(None, j)
                if held:
                    transpose_v(*held)
                held = (*new, j - 8)
        a_lr = small_proj(A["w_lr"], 16, t_b1)
        transpose_v(*held)
        b = sbank()
        for c in range(2):
            t = tr(b.t[0:16, c * 128:(c + 1) * 128], GTK[:, c, 0:16], IDENT[:, :], [a_lr] + b.rel, inc=True)
        t_lr = cp(DV, LR[:, :], b.t[0:16, 0:T], [t] + t_b1)
        b.rel = [t_lr]
        t_gtk_free = [t]

        def flat(x):
            return x[:, :, :].rearrange("p a n -> p (a n)")

        def side_gla():
            bz = [sbank(), sbank()]
            for h in range(4):
                t = mm(bz[h // 2].t[:, (h % 2) * T:(h % 2 + 1) * T], GW2[:, h * 128:(h + 1) * 128], LR[:, :],
                       True, True, [t_lr, t_gw2] + bz[h // 2].rel, inc=True)
            for h in range(4):
                a = ts(DV, GG[:, h, :], bz[h // 2].t[:, (h % 2) * T:(h % 2 + 1) * T], vec("gb", h), None, ALU.add,
                       None, [t])
            bz[0].rel = bz[1].rel = [a]
            a = stt(flat(GE), flat(GG), -1.0, flat(GG), ALU.mult, ALU.max)
            a = act(flat(GE), flat(GE), ACT.Exp, [a], scale=-1.0)
            a = act(flat(GE), flat(GE), ACT.Ln, [a], bias=1.0)
            a = stt(flat(GG), flat(GG), 0.0, flat(GE), ALU.min, ALU.subtract, [a])
            a = ts(DV, flat(GG), flat(GG), 1.0 / 16.0, None, ALU.mult)
            for h in range(4):
                a = DV(lambda e, h=h: e.tensor_tensor_scan(GB[:, h, :], RST[:, :], GG[:, h, :], 0.0, ALU.mult,
                                                           ALU.add), [t_rst])
            a = ts(DV, flat(GQ), flat(GQ), 128.0 ** -0.5, None, ALU.mult, None, [t_v["g", j] for j in range(4)])
            yield
            bb = [sbank(), sbank()]
            for c in range(2):
                for h in range(4):
                    t = mm(bb[c].t[:, h * 128:(h + 1) * 128], GK[:, h, c * 128:(c + 1) * 128],
                           GQ[:, h, c * 128:(c + 1) * 128], True, True, [a, t_v["g", 4 + h]] + bb[c].rel, inc=True)
            for c in range(2):
                a = tt(DV, PT[:, c, :, :], bb[c].t[:, :].rearrange("p (a n) -> p a n", a=4),
                       IDENT[:, :].unsqueeze(1).broadcast_to([128, 4, 128]), ALU.mult, [t])
                bb[c].rel = [a]
            for lv in range(7):
                w = 1 << lv
                g = flat(GB).rearrange("p (n a w) -> p n a w", a=2, w=w)
                e4 = flat(GE).rearrange("p (n a w) -> p n a w", a=2, w=w)
                n = 1024 // (2 * w)
                end = g[:, :, 0, w - 1:w].broadcast_to([128, n, w])
                tt(DV, e4[:, :, 0, :], end, g[:, :, 0, :], ALU.subtract, [PE.last()])
                if w < 64:
                    a = tt(DV, e4[:, :, 1, :], g[:, :, 1, :], end, ALU.subtract)
                else:
                    a = cp(DV, e4[:, :, 1, :], g[:, :, 1, :])
                a = act(flat(GE), flat(GE), ACT.Exp, [a])
                tt(DV, flat(QE), flat(GQ), flat(GE), ALU.mult, [a])
                a = tt(DV, flat(GE), flat(GK), flat(GE), ALU.mult)
                yield
                bb = [sbank(), sbank()]
                for c in range(2):
                    for h in range(4):
                        t = mm(bb[c].t[:, h * 128:(h + 1) * 128], GE[:, h, c * 128:(c + 1) * 128],
                               QE[:, h, c * 128:(c + 1) * 128], True, True, [a] + bb[c].rel, inc=True)
                for c in range(2):
                    m = LM[:, lv, :].unsqueeze(1).broadcast_to([128, 4, 128])
                    a = DV(lambda e, c=c, m=m, src=bb[c].t: e.copy_predicated(
                        PT[:, c, :, :], m, src[:, :].rearrange("p (a n) -> p a n", a=4)), [t, t_lm])
                    bb[c].rel = [a]
            for h in range(4):
                last2 = GB[:, h, 191:192]
                last1 = GB[:, h, 127:128]
                last0 = GB[:, h, 63:64]
                cp(DV, GE[:, h, 128:192], GB[:, h, 128:192], [PE.last()])
                ts(DV, GE[:, h, 192:256], GB[:, h, 192:256], last2, None, ALU.add)
                ts(DV, GE[:, h, 64:128], GB[:, h, 64:128], last1, -1.0, ALU.subtract, ALU.mult)
                ts(DV, GE[:, h, 0:64], GB[:, h, 0:64], last0, -1.0, ALU.subtract, ALU.mult)
                a = ts(DV, GE[:, h, 0:64], GE[:, h, 0:64], last1, None, ALU.add)
            a = act(flat(GE), flat(GE), ACT.Exp, [a])
            tt(DV, QE[:, :, 128:256], GQ[:, :, 128:256], GE[:, :, 128:256], ALU.mult, [a])
            a = tt(DV, GE[:, :, 0:128], GK[:, :, 0:128], GE[:, :, 0:128], ALU.mult)
            yield
            b = sbank()
            for h in range(4):
                t = mm(b.t[:, h * 128:(h + 1) * 128], GE[:, h, 0:128], QE[:, h, 128:256], True, True,
                       [a] + b.rel, inc=True)
            p = cp(AC, flat(PT2), b.t[:, :], [t])
            b.rel = [p]
            yield
            for h in range(4):
                b = sbank()
                for v in range(2):
                    cs = slice(h * 256 + v * 128, h * 256 + (v + 1) * 128)
                    o = v * T
                    mm(b.t[:, o:o + 128], VTG[:, 0, cs], PT[:, 0, h, :], True, True,
                       [p, DV.last(), t_v["vtg", 2 * h + v]] + b.rel)
                    mm(b.t[:, o + 128:o + 256], VTG[:, 0, cs], PT2[:, h, :], True, False)
                    t = mm(b.t[:, o + 128:o + 256], VTG[:, 1, cs], PT[:, 1, h, :], False, True, inc=True)
                sq = QE[:, 0:2, :].rearrange("p a n -> p (a n)")
                a = act(sq, b.t[:, :], ACT.Square, [t, PE.last()])
                b2 = sbank()
                yield
                for v in range(2):
                    t = mm(b2.t[:, 0:T], ONES[:, :], QE[:, v, :], v == 0, v == 1, [a] + b2.rel, inc=True)
                r = GG[:, 0, :]
                ra, rr = rsqrt_mean(r, b2.t[:, 0:T], 256.0, [t, DV.last()])
                b2.rel = [rr]
                for v in range(2):
                    i, s, rel = tmp()
                    j = 2 * h + v
                    a = tt(DV, s, b.t[:, v * T:(v + 1) * T], r, ALU.mult, [ra] + rel)
                    z = stt(s, s, vec("gng", v), OG[:, j, :], ALU.mult, ALU.mult, [t_v["og", j]])
                    MG.t[j] = split(MGH[:, j, :], MGL[:, j, :], s, [z])
                    tmp_rel[i] = MG.t[j]
                b.rel = [a]
                yield

        def plain(dst, after=()):
            b = mbank()
            t = ntile(b.t[:, 0:T], HN, range(16), b.rel)
            a = tt(DV, dst, b.t[:, 0:T], RSTD[:, :], ALU.mult, [t, t_rstd[0]] + list(after))
            b.rel = [a]
            return a

        def main_second():
            for j in range(8):
                b = mbank()
                t = ntile(b.t[:, 0:T], HN, range(16), b.rel)
                i, s, a = scaled(b, t)
                t_v["og", j] = act(OG[:, j, :], s, ACT.Silu, [a])
                tmp_rel[i] = [t_v["og", j]]
                yield
            for m in range(2):
                for g in range(2):
                    t_v["kc", m, g] = plain(NKC[:, m, g, :], t_b1)
                    yield
            for m in range(2):
                for g in range(2):
                    t_v["ks", m, g] = plain(NKS[:, m, g, :], t_b1)
                    yield
            for m in range(2):
                for g in range(2):
                    b = mbank()
                    t = ntile_tok(b, HN, b.rel)
                    for c in range(2):
                        a = ts(DV, NVT[:, m, c, g * 128:(g + 1) * 128], b.t[:, c * 128:(c + 1) * 128],
                               RTOK[:, c:c + 1], None, ALU.mult, None, [t, t_rtok[0]] + t_b1)
                    b.rel = [a]
                    t_v["vs", m, g] = a
                    yield

        run(main_second(), side_gla(), 1)
        t_gl = [DV.last(), AC.last(), PE.last()]

        NQA = ar("NQA", [128, 8, T], 0)
        MNH = ar("MNH", [128, 8, T], 8, F32R)
        MNL = ar("MNL", [128, 8, T], 16, F32R)
        CBH = ar("CBH", [128, 32, 2, 15], 24, F32R)
        CBL = ar("CBL", [128, 32, 2, 15], 28, F32R)
        CB = ar("CB", [128, 32, 2, 15], 32)
        SQ2 = ar("SQ2", [128, 2, T], 36)
        RN = ar("RN", [128, 2, T], 38)
        CW2 = ar("CW2", [128, 2, 128], 40)
        HID = ar("HID", [128, 2, 32], 41)
        KCN = ar("KCN", [128, 32], 41.5)
        VCN = ar("VCN", [16, 2, 128], 42)
        PC = ar("PC", [128, 16, 16], 43)
        PC2 = ar("PC2", [128, 16, 16], 44)
        CM = ar("CM", [128, 2, 2, 16], 45)
        SMALL = ar("SMALL", [128, 16, 8], 45.5)
        PCT = ar("PCT", [16, 8, 2, 128], 24)
        AM = ar("AM", [128, 384], 46)
        SS = ar("SS", [128, 2, 384], 47.5)
        PTS = ar("PTS", [128, 2, 384], 32)
        GATE = ar("GATE", [128, 2, 24], 45.25)
        POS = ar("POS", [128, 2, 32], 41.25)
        MN = Act(MNH, MNL, 8)

        t_pos = load(POS[:, :, :], A["posT"], t_gl)
        t_cw2 = load(CW2[:, :, :], A["cmp_w2"], t_gl)
        t_cm = load(CM[:, :, :, :], A["cmask"], t_gl)
        t_am = load(AM[:, :], A["amask"], t_gl)

        a_ng = small_proj(A["w_ng"], 24, t_gl)
        t_gate = act(GATE[:, :, :].rearrange("p a n -> p (a n)"), GTK[:, :, :].rearrange("p a n -> p (a n)"),
                     ACT.Sigmoid, [a_ng] + t_gl)

        for j in range(8):
            t_v["nq", j] = plain(NQA[:, j, :], t_gl)

        def head_norm(x2, gname, scale, after, bank=None, n=512):
            sq = SQ2[:, :, :].rearrange("p a n -> p (a n)")[:, 0:n]
            rn = RN[:, :, :].rearrange("p a n -> p (a n)")[:, 0:n]
            a = act(sq, x2, ACT.Square, list(after) + [PE.last()])
            b = sbank()
            t = mm(b.t[:, 0:n], ONES[:, :], sq, True, True, [a] + b.rel, inc=True)
            yield
            ra, rr = rsqrt_mean(rn, b.t[:, 0:n], 128.0, [t, DV.last()])
            b.rel = [rr]
            z = tt(DV, x2, x2, rn, ALU.mult, [ra])
            z = ts(DV, x2, x2, vec(gname), scale, ALU.mult, ALU.mult)
            yield z

        def hn_run(*a, **k):
            z = None
            for z in head_norm(*a, **k):
                pass
            return z

        for m in range(2):
            st = None
            for g in range(2):
                win = NKC[:, m, g, :].rearrange("p (n l) -> p l n", l=16)
                for half in range(2):
                    o = CB[:, half * 16:(half + 1) * 16, g, :]
                    i1 = POS[:, m, half * 16:(half + 1) * 16].unsqueeze(2).broadcast_to([128, 16, 15])
                    st = tt(DV, o, win[:, :, half:half + 15], i1, ALU.add,
                            [t_v["kc", m, g], t_pos] + t_gl)
            hi = cp(AC, CBH[:, :, :, :].rearrange("p a b n -> p (a b n)"),
                    CB[:, :, :, :].rearrange("p a b n -> p (a b n)"), [st, PE.last()])
            lo = tt(DV, CBL[:, :, :, :].rearrange("p a b n -> p (a b n)"),
                    CB[:, :, :, :].rearrange("p a b n -> p (a b n)"),
                    f32(CBH[:, :, :, :].rearrange("p a b n -> p (a b n)")), ALU.subtract, [hi, PE.last()])
            x = Act(CBH[:, :, :, :].rearrange("p a b n -> p a (b n)"),
                    CBL[:, :, :, :].rearrange("p a b n -> p a (b n)"), 32)
            x.t = [[hi, lo]] * 32
            b = mbank()
            t = None
            for l in range(32):
                t = mm3(b.t[:, 0:30], x, l, l == 0, l == 31, b.rel, n=slice(0, 30))
            a = act(HID[:, m, 0:30], b.t[:, 0:30], ACT.Silu, [t])
            b.rel = [a]
            t_v["hid", m] = a

        def side_nsa():
            b = sbank()
            t = mm(b.t[:, 0:30], CW2[:, 0, :], HID[:, 0, 0:30], True, True, [t_v["hid", 0], t_cw2] + b.rel, inc=True)
            a = cp(DV, KCN[:, 0:30], b.t[:, 0:30], [t])
            b.rel = [a]
            b = sbank()
            for g in range(2):
                t = mm(b.t[0:15, g * 128:(g + 1) * 128], HID[:, 1, 15 * g:15 * g + 15], CW2[:, 1, :], True, True,
                       [t_v["hid", 1]] + b.rel, inc=True)
            v = cp(DV, VCN[0:15, :, :].rearrange("p a n -> p (a n)"), b.t[0:15, 0:256], [t])
            b.rel = [v]
            t_vcn = v
            yield
            z = None
            for z in head_norm(KCN[:, 0:30], "kcg", 1.0, [a], n=30):
                yield
            t_kcn = z
            for m, gn in ((0, "ksg"), (1, "kwg")):
                for z in head_norm(NKS[:, m, :, :].rearrange("p a n -> p (a n)"), gn, 1.0,
                                   [t_v["ks", m, 0], t_v["ks", m, 1]]):
                    yield
            t_kk = z
            for j in range(0, 8, 2):
                for z in head_norm(NQA[:, j:j + 2, :].rearrange("p a n -> p (a n)"), "qg", 128.0 ** -0.5,
                                   [t_v["nq", j], t_v["nq", j + 1]]):
                    yield
            t_q = z
            b = sbank()
            for h in range(8):
                for c in range(2):
                    o = (h * 2 + c) * 16
                    t = mm(b.t[:, o:o + 15], NQA[:, h, c * 128:(c + 1) * 128],
                           KCN[:, 15 * (h // 4):15 * (h // 4) + 15], True, True, [t_q, t_kcn, DV.last()] + b.rel,
                           inc=True)
            pc4 = PC[:, :, :].rearrange("p (h c) n -> p h c n", c=2)
            for c in range(2):
                a = tt(DV, pc4[:, :, c, 0:15],
                       b.t[:, 0:256].rearrange("p (h c n) -> p h c n", c=2, n=16)[:, :, c, 0:15],
                       CM[:, 0, c, 0:15].unsqueeze(1).broadcast_to([128, 8, 15]), ALU.add, [t, t_cm])
            b.rel = [a]
            mx = SMALL[:, :, 0:1]
            DV(lambda e: e.tensor_reduce(SMALL[:, :, 0], PC[:, :, 0:15], AX.X, ALU.max))
            a = tt(DV, PC[:, :, 0:15], PC[:, :, 0:15], mx.broadcast_to([128, 16, 15]), ALU.subtract)
            a = act(PC2[:, :, 0:15], PC[:, :, 0:15], ACT.Exp, [a])
            DV(lambda e: e.tensor_reduce(SMALL[:, :, 1], PC2[:, :, 0:15], AX.X, ALU.add), [a])
            recip(SMALL[:, :, 2], SMALL[:, :, 1])
            sm = SMALL[:, :, :].rearrange("p (h c) n -> p h c n", c=2)
            for c in range(2):
                gt = GATE[:, c, :].rearrange("p (h r) -> p h r", r=3)
                tt(DV, sm[:, :, c, 3], sm[:, :, c, 2], gt[:, :, 0], ALU.mult, [t_gate])
            a = tt(DV, PC2[:, :, 0:15], PC2[:, :, 0:15], SMALL[:, :, 3:4].broadcast_to([128, 16, 15]), ALU.mult)
            p4 = PC2[:, :, :].rearrange("p (h c) n -> p h c n", c=2)
            for c in range(2):
                a = tt(DV, p4[:, :, c, 0:15], p4[:, :, c, 0:15],
                       CM[:, 1, c, 0:15].unsqueeze(1).broadcast_to([128, 8, 15]), ALU.mult)
            yield
            t_pct = {}
            for q in range(4):
                b = sbank()
                for m in range(4):
                    hc = 4 * q + m
                    t = tr(b.t[0:15, m * 128:(m + 1) * 128], PC2[:, hc, 0:15], IDENT[:, :], [a] + b.rel, inc=True)
                c0 = cp(AC, PCT[0:15, 2 * q:2 * q + 2, :, :].rearrange("p a b n -> p (a b n)"),
                        b.t[0:15, :], [t, PE.last()])
                b.rel = [c0]
                t_pct[2 * q] = t_pct[2 * q + 1] = c0
                if q % 2:
                    yield

            def scores(h, m):
                b = sbank()
                g = h // 4
                for c in range(2):
                    n = 128 * (c + 1)
                    o = 128 * c
                    t = mm(b.t[:, o:o + n], NQA[:, h, c * 128:(c + 1) * 128], NKS[:, m, g, 0:n], True, True,
                           [t_kk, t_q] + b.rel, inc=(c == 1))
                return b, t

            def soft(b, t, h, m):
                s = SS[:, m, :]
                a = tt(DV, s, b.t[:, 0:384], AM[:, :], ALU.add, [t, t_am, PE.last()])
                b.rel = [a]
                for c in range(2):
                    x = s[:, 128 * c:128 * c + 128 * (c + 1)]
                    mxc = SMALL[:, m * 2 + c, 4:5]
                    DV(lambda e, x=x, o=mxc: e.tensor_reduce(o, x, AX.X, ALU.max, negate=True))
                a = DV.last()
                for c in range(2):
                    x = s[:, 128 * c:128 * c + 128 * (c + 1)]
                    e1 = act(x, x, ACT.Exp, [a], bias=SMALL[:, m * 2 + c, 4:5], accum=SMALL[:, m * 2 + c, 5:6])
                for c in range(2):
                    x = s[:, 128 * c:128 * c + 128 * (c + 1)]
                    sc = SMALL[:, m * 2 + c, 5:6]
                    recip(SMALL[:, m * 2 + c, 6:7], sc, [e1])
                    tt(DV, SMALL[:, m * 2 + c, 7:8], SMALL[:, m * 2 + c, 6:7],
                       GATE[:, c, 3 * h + 1 + m:3 * h + 2 + m], ALU.mult)
                    a = ts(DV, x, x, SMALL[:, m * 2 + c, 7:8], None, ALU.mult)
                return a

            def turnp(h, m, a):
                b = sbank()
                for k in range(3):
                    t = tr(b.t[:, k * 128:(k + 1) * 128], SS[:, m, k * 128:(k + 1) * 128], IDENT[:, :], [a] + b.rel,
                           inc=(k == 2))
                a = cp(AC if m else DV, PTS[:, m, :], b.t[:, 0:384], [t, PE.last()])
                b.rel = [a]
                return a

            for h in range(8):
                ab = [scores(h, m) for m in range(2)]
                aa = [soft(*ab[m], h, m) for m in range(2)]
                yield
                pp = [turnp(h, m, aa[m]) for m in range(2)]
                yield
                b = sbank()
                g = h // 4
                mm(b.t[:, 0:T], VCN[0:15, g, :], PCT[0:15, h, :, :].rearrange("p a n -> p (a n)"), True, False,
                   [t_vcn, t_pct[h]] + b.rel, skip=True)
                for m in range(2):
                    mm(b.t[:, 0:T], NVT[:, m, 0, g * 128:(g + 1) * 128], PTS[:, m, 0:256], False, False,
                       [pp[m], t_v["vs", m, g]], skip=True)
                    t = mm(b.t[:, 128:T], NVT[:, m, 1, g * 128:(g + 1) * 128], PTS[:, m, 256:384], False, m == 1,
                           inc=(m == 1), skip=True)
                hi = cp(AC, MNH[:, h, :], b.t[:, 0:T], [t])
                lo = tt(DV, MNL[:, h, :], b.t[:, 0:T], f32(MNH[:, h, :]), ALU.subtract, [hi])
                b.rel = [lo]
                MN.t[h] = [hi, lo]

        def main_out_a():
            for n in range(16):
                b = mbank()
                t = ntile(b.t[:, 0:T], MG, range(8), b.rel)
                z = tt(DV, XT[:, n, :], XT[:, n, :], RF[:, :], ALU.mult, [t_rf])
                z = tt(DV, XT[:, n, :], XT[:, n, :], b.t[:, 0:T], ALU.add, [t])
                b.rel = [z]
                t_v["h", n] = z
                yield

        run(main_out_a(), side_nsa(), 1, 2)
        f = norm_after("ffn")
        for n in range(16):
            residual(MN, range(8), [t_v["h", n]], n, f)
        finish_rstd()

        out_tickets = []

        def store(n, a):
            s = out_sem[n % 4]
            SP.wait([a])
            SP.todo.append(lambda e, n=n, s=s: e.dma_start(out[:, n, :], XT[:, n, :]).then_inc(s, 16))
            out_tickets.append((s, 16 * (n // 4 + 1)))

        out_sem = [sem(f"s_out{i}") for i in range(4)]
        ffn(store)
        SP.wait(out_tickets[-4:])
        assert tile_at[0] == len(order) * RU, (tile_at[0], len(order) * RU)

        block = ctx.enter_context(nc.Block())

        @block.sync
        def _(e):
            SP.play(e)

        @block.gpsimd
        def _(e):
            GP.play(e)

        @block.scalar
        def _(e):
            AC.play(e)

        @block.vector
        def _(e):
            DV.play(e)

        @block.tensor
        def _(e):
            PE.play(e)


def tiles(w, kt=None):
    K, N = w.shape
    t = w.reshape(K // 128, 128, N // 128, 128).transpose(2, 0, 1, 3)
    return t.reshape(-1, 128, 128)


def units(t):
    return np.ascontiguousarray(t.reshape(-1, RU, 128, 128).transpose(0, 2, 1, 3)).reshape(-1, 128, RU * 128)


def gated(w, b):
    ta = tiles(w).reshape(-1, w.shape[0] // 128, 128, 128)
    tb = tiles(b).reshape(-1, b.shape[0] // 128, 128, 128)
    return units(np.concatenate([ta, tb], axis=1).reshape(-1, 128, 128))


def down(w):
    t = tiles(w).reshape(16, 2, 22, 128, 128).transpose(1, 0, 2, 3, 4)
    return units(t.reshape(-1, 128, 128))


def cols(v):
    return np.ascontiguousarray(v.reshape(-1, 128).T)


def consts():
    L = 256
    f = np.float64
    t = np.arange(L, dtype=f)[:, None]
    m = np.arange(L, dtype=f)[None, :]
    ang = 2.0 * np.pi * (m + 0.5) * t / 512.0
    C, S = np.cos(ang), np.sin(ang)
    c = {}
    c["df"] = np.stack([C, S]).reshape(2, 2, 128, L).transpose(2, 0, 1, 3).astype(np.float32)
    c["dg"] = np.stack([C.T / 256.0, -S.T / 256.0]).reshape(2, 2, 128, L).transpose(2, 0, 1, 3).astype(np.float32)
    tl = np.linspace(0.0, 1.0, L, dtype=np.float32)[:, None]
    om = (np.float32(2.0 * math.pi) * np.arange(L, dtype=np.float32) / np.float32(L)).astype(np.float32)
    fr = np.linspace(1e-4, 15, 16, dtype=np.float32)
    an = (om[:, None] * fr[None, :]).astype(np.float32).astype(f)
    z = np.concatenate([tl, np.cos(an), -np.sin(an)], axis=1).astype(np.float32)
    c["zt"] = np.ascontiguousarray(z.T)
    d = np.linspace(math.log(1e-2) / 1.5, math.log(1e-2) / 0.3, 1024, dtype=np.float32)
    win = np.exp((-tl * np.abs(d)[None, :]).astype(f)).astype(np.float32)
    wb = win.copy()
    wb[0] = 0.0
    w2 = np.stack([win, wb], axis=1).reshape(2, 128, 2, 4, 256)
    c["win"] = w2.transpose(3, 1, 0, 2, 4)
    p = np.arange(128)
    j = np.arange(L)
    mk = np.zeros((128, 2, 2, L), np.float32)
    for h in range(2):
        s = (h * 128 + p)[:, None]
        mk[:, 0, h] = np.where(s <= j[None, :], 0.0, NEG)
        mk[:, 1, h] = np.where(s >= j[None, :], 0.0, NEG)
    c["mmask"] = mk
    sel = np.zeros((4, 4, 128), np.float32)
    for h in range(4):
        sel[h, h] = 1.0
    c["sel4"] = sel
    lm = np.zeros((128, 7, 128), np.int32)
    s, q = p[:, None], p[None, :]
    for lv in range(7):
        w = 1 << lv
        lm[:, lv] = (s // (2 * w) == q // (2 * w)) & (s // w % 2 == 0) & (q // w % 2 == 1)
    c["lmask"] = lm
    r = np.ones((128, L), np.float32)
    r[:, ::64] = 0.0
    c["reset"] = r
    cm = np.zeros((128, 2, 2, 16), np.float32)
    for h in range(2):
        ok = (16 * np.arange(16)[None, :] + 31) <= (h * 128 + p)[:, None]
        cm[:, 0, h] = np.where(ok, 0.0, NEG)
        cm[:, 1, h] = ok
    c["cmask"] = cm
    am = np.zeros((128, 384), np.float32)
    dm = np.where(q <= s, 0.0, NEG)
    am[:, 0:128] = dm
    am[:, 256:384] = dm
    c["amask"] = am
    c["ident"] = np.eye(128, dtype=np.float32)
    return {k: np.ascontiguousarray(v) for k, v in c.items()}


def kernel(**inputs):
    import concourse.bacc as bacc
    from concourse.bass_utils import run_bass_kernel_spmd as launch

    x = {k: np.asarray(v) for k, v in inputs.items()}
    one = {k: (v[0] if k != "norm_f_w" else v) for k, v in x.items()}
    a = consts()
    w = one["w_in"]
    a["w_in_a"] = units(tiles(w[:, 0:7168]))
    a["w_g"] = np.ascontiguousarray(w[:, 7168:7184].reshape(16, 128, 16).transpose(1, 0, 2))
    a["w_ga"] = gated(w[:, 7184:9232], one["w_branch_a"])
    a["w_gb"] = gated(w[:, 9232:11280], one["w_branch_b"])
    a["w_out"] = units(tiles(one["w_out"]))
    gu = one["w_gate_up"]
    a["w_gu"] = gated(gu[:, 0:5632], gu[:, 5632:])
    a["w_dn"] = down(one["w_down"])
    w = one["w_in_2"]
    a["w_in2"] = units(tiles(np.concatenate(
        [w[:, 0:2048], w[:, 2064:3088], w[:, 4112:4624], w[:, 4624:4880], w[:, 5136:5392],
         w[:, 4880:5136], w[:, 5392:5648], w[:, 3088:4112]], axis=1)))
    a["w_lr"] = np.ascontiguousarray(w[:, 2048:2064].reshape(16, 128, 16).transpose(1, 0, 2))
    a["w_ng"] = np.ascontiguousarray(w[:, 5648:5672].reshape(16, 128, 24).transpose(1, 0, 2))
    a["w_cmp"] = units(np.concatenate([one["cmp_k_w1_2"].reshape(32, 128, 128),
                                       one["cmp_v_w1_2"].reshape(32, 128, 128)]))
    a["cmp_w2"] = np.ascontiguousarray(np.stack([one["cmp_k_w2_2"], one["cmp_v_w2_2"]], axis=1))
    a["posT"] = np.ascontiguousarray(np.stack([one["cmp_k_pos_2"].T, one["cmp_v_pos_2"].T], axis=1))
    w = one["w_out_2"]
    a["w_out2"] = units(np.concatenate([tiles(w[0:1024]), tiles(w[1024:2048])]))
    a["w_gu2"] = gated(one["w_gate_2"], one["w_up_2"])
    a["w_dn2"] = down(one["w_down_2"])
    a["filt_w1"] = np.ascontiguousarray(one["filt_w1"])
    a["filt_w2"] = np.ascontiguousarray(one["filt_w2"])
    a["filt_w3"] = np.ascontiguousarray(one["filt_w3"].reshape(64, 2, 2, 1024))
    a["gla_gate_w2"] = np.ascontiguousarray(one["gla_gate_w2_2"])
    a["xT"] = np.ascontiguousarray(x["x"][0].T.reshape(16, 128, 256).transpose(1, 0, 2))

    v = np.zeros((128, NVEC), np.float32)

    def put(name, m):
        n, k = VECS[name]
        v[0:m.shape[0], n:n + k] = m

    put("norm1", cols(one["norm1_w"]))
    put("norm2", cols(one["norm2_w"]))
    put("normf", cols(one["norm_f_w"]))
    put("attn", cols(one["attn_norm_g_2"]))
    put("ffn", cols(one["ffn_norm_g_2"]))
    for i in range(3):
        put(f"cw{i}", cols(one["conv_w"][i]))
    put("cb", cols(one["conv_b"]))
    put("hb", cols(one["hyena_bias"].reshape(-1)))
    for i in range(4):
        put(f"gw{i}", cols(one["gla_conv_w_2"][i]))
    put("gb", cols(one["gla_gate_b_2"]))
    put("gng", cols(one["gla_norm_g_2"]))
    put("qg", cols(one["nsa_q_norm_g_2"]))
    put("kcg", cols(one["nsa_kc_norm_g_2"]))
    put("ksg", cols(one["nsa_ks_norm_g_2"]))
    put("kwg", cols(one["nsa_kw_norm_g_2"]))
    put("f1", one["filt_freq1"].reshape(64, 1))
    put("b1", one["filt_b1"].reshape(64, 1))
    put("f2", one["filt_freq2"].reshape(64, 1))
    put("b2", one["filt_b2"].reshape(64, 1))
    put("gbias", one["mlstm_gate_bias"].reshape(16, 1))
    a["vecs"] = v

    nc = bacc.Bacc("TRN2", target_bir_lowering=False, num_devices=1)
    arrays, aps = {}, {}
    for k, m in a.items():
        arrays[f"in_{k}"] = m
        aps[k] = nc.dram_tensor(f"in_{k}", m.shape, mybir.dt.from_np(m.dtype), kind="ExternalInput").ap()
    out = nc.dram_tensor("out_x", (128, 16, 256), F32, kind="ExternalOutput").ap()
    build(nc, aps, out)
    r = launch(nc, [arrays], core_ids=[0])
    got = r.results[0]["out_x"]
    return np.ascontiguousarray(got.transpose(1, 0, 2).reshape(2048, 256).T).reshape(1, 256, 2048)
```

```python
from contextlib import ExitStack
import math

import numpy as np
import concourse.bass as bass
from concourse import mybir

F32 = mybir.dt.float32
F32R = mybir.dt.float32r
I32 = mybir.dt.int32
ALU = mybir.AluOpType
ACT = mybir.ActivationFunctionType
AX = mybir.AxisListType

T = 256
KB = 1024
NEG = -1.0e30
EPS = 1e-6
RU = 16
SU = 8
NRAW = 3
NSPL = 4
AHEAD = 4

VECS = {}


def vec_layout():
    n = 0
    for name, k in (("norm1", 16), ("norm2", 16), ("normf", 16), ("attn", 16), ("ffn", 16),
                    ("cw0", 40), ("cw1", 40), ("cw2", 40), ("cb", 40), ("hb", 16),
                    ("gw0", 16), ("gw1", 16), ("gw2", 16), ("gw3", 16), ("gb", 4), ("gng", 2),
                    ("qg", 1), ("kcg", 1), ("ksg", 1), ("kwg", 1),
                    ("f1", 1), ("b1", 1), ("f2", 1), ("b2", 1), ("gbias", 1), ("rowmask", 1)):
        VECS[name] = (n, k)
        n += k
    return n


NVEC = vec_layout()


class Engine:

    def __init__(self, sem):
        self.sem = sem
        self.n = 0
        self.todo = []
        self.seen = {}

    def wait(self, after):
        for t in after:
            if t is None:
                continue
            sem, value = t
            if self.seen.get(id(sem), 0) < value:
                self.seen[id(sem)] = value
                self.todo.append(lambda e, s=sem, v=value: e.wait_ge(s, v))

    def __call__(self, fn, after=(), chain=True, inc=True):
        if chain and self.n:
            self.wait([(self.sem, self.n)])
        self.wait(after)
        if inc:
            self.n += 1
            self.todo.append(lambda e, f=fn, s=self.sem: f(e).then_inc(s, 1))
            return (self.sem, self.n)
        self.todo.append(fn)
        return None

    def last(self):
        return (self.sem, self.n)

    def play(self, e):
        for f in self.todo:
            f(e)


class Bank:

    def __init__(self, t):
        self.t = t
        self.rel = []


class Act:

    def __init__(self, hi, lo, kt):
        self.hi, self.lo = hi, lo
        self.t = [[] for _ in range(kt)]


def build(nc, A, out):
    ctx = ExitStack()
    with ctx:
        def sem(name):
            return ctx.enter_context(nc.semaphore(name))

        PE, AC, DV, GP, SP = (Engine(sem(f"s_{n}")) for n in ("pe", "act", "dve", "pool", "sp"))
        raw_sem = [sem(f"s_raw{i}") for i in range(NRAW)]

        base = (nc.sbuf_base + 31) // 32 * 32
        cur = [base]

        def at(name, shape, dt, off):
            return nc.alloc_sbuf_tensor_at(name, shape, dt, offset=off)

        def bump(name, shape, dt=F32):
            size = int(np.prod(shape[1:])) * 4
            t = at(name, shape, dt, cur[0])
            cur[0] += (size + 31) // 32 * 32
            return t

        RAW = bump("RAW", [128, NRAW, RU * 128])
        WH = bump("WH", [128, NSPL, SU * 128], F32R)
        WL = bump("WL", [128, NSPL, SU * 128], F32R)
        HNH = bump("HNH", [128, 16, T], F32R)
        HNL = bump("HNL", [128, 16, T], F32R)
        VEC = bump("VEC", [128, NVEC])
        ONES = bump("ONES", [128, 128])
        IDENT = bump("IDENT", [128, 128])
        TMP = bump("TMP", [128, 4, T])
        RSTD = bump("RSTD", [128, T])
        RF = bump("RF", [128, T])
        RTOK = bump("RTOK", [128, 2])
        SQA = bump("SQA", [128, 2, T])
        xt_off = cur[0]
        XT = bump("XT", [128, 16, T])
        arena = cur[0]
        limit = nc.sbuf_usable_end

        def ar(name, shape, kb, dt=F32):
            size = int(np.prod(shape[1:])) * 4
            off = arena + int(kb * KB)
            assert off + size <= limit, (name, off + size - limit)
            return at(name, shape, dt, off)

        banks = [Bank(nc.alloc_psum_tensor(f"PB{i}", [128, 512], F32)) for i in range(8)]
        mains = banks[0:3]
        sides = banks[3:8]
        turn = {"m": 0, "s": 0}

        def mbank():
            turn["m"] += 1
            return mains[turn["m"] % 3]

        def sbank():
            turn["s"] += 1
            return sides[turn["s"] % 5]

        def vec(name, j=0, p=128):
            n, k = VECS[name]
            assert j < k
            return VEC[0:p, n + j:n + j + 1]

        def tt(E, o, a, b, op, after=(), **k):
            return E(lambda e: e.tensor_tensor(o, a, b, op), after, **k)

        def ts(E, o, a, s1, s2, op0, op1=None, after=(), **k):
            if op1 is None:
                return E(lambda e: e.tensor_scalar(o, a, s1, None, op0), after, **k)
            return E(lambda e: e.tensor_scalar(o, a, s1, s2, op0, op1), after, **k)

        def stt(o, a, s, b, op0, op1, after=(), **k):
            return DV(lambda e: e.scalar_tensor_tensor(out=o, in0=a, scalar=s, in1=b, op0=op0, op1=op1),
                      after, **k)

        def cp(E, o, a, after=(), **k):
            if E is AC:
                return E(lambda e: e.activation(o, a, ACT.Copy), after, **k)
            return E(lambda e: e.tensor_copy(o, a), after, **k)

        def act(o, a, f, after=(), bias=None, scale=None, accum=None, **k):
            kw = {}
            if bias is not None:
                kw["bias"] = bias
            if scale is not None:
                kw["scale"] = scale
            if accum is not None:
                kw["accum_out"] = accum
            return AC(lambda e: e.activation(o, a, f, **kw), after, **k)

        def mm(o, l, r, start, stop, after=(), inc=False, skip=False):
            return PE(lambda e: e.matmul(o, l, r, start=start, stop=stop, skip_group_check=skip),
                      after, chain=False, inc=inc)

        def tr(o, a, ident, after=(), inc=False):
            return PE(lambda e: e.transpose(o, a, ident), after, chain=False, inc=inc)

        def recip(o, a, after=()):
            return DV(lambda e: e.reciprocal(o, a), after)

        def load(dst, src, after=()):
            s = sem(f"s_ld{len(loads)}")
            loads.append(s)
            SP.wait(after)
            SP.todo.append(lambda e: e.dma_start(dst, src).then_inc(s, 16))
            return (s, 16)

        loads = []

        def f32(ap):
            return ap.bitcast(F32)

        tmp_rel = [[] for _ in range(4)]
        tmp_n = [0]

        def tmp():
            i = tmp_n[0] % 4
            tmp_n[0] += 1
            return i, TMP[:, i, :], tmp_rel[i]

        def split(hi, lo, x, after=(), hi_after=()):
            a = cp(AC, hi, x, list(after) + list(hi_after))
            b = tt(DV, lo, x, f32(hi), ALU.subtract, list(after) + [a])
            return [a, b]

        order = []
        order += [("w_in_a", i) for i in range(57)]
        order += [("w_ga", i) for i in range(24)] + [("w_gb", i) for i in range(24)]
        order += [("w_out", i) for i in range(16)]
        for h in range(2):
            order += [("w_gu", 44 * h + i) for i in range(44)] + [("w_dn", 22 * h + i) for i in range(22)]
        order += [("w_in2", i) for i in range(46)] + [("w_cmp", i) for i in range(4)]
        order += [("w_out2", i) for i in range(16)]
        for h in range(2):
            order += [("w_gu2", 44 * h + i) for i in range(44)] + [("w_dn2", 22 * h + i) for i in range(22)]

        raw_used = {}
        unit_pe = {}
        unit_ready = {}
        issued = [0]
        splits = [0]
        tile_at = [0]

        def issue_raw():
            while issued[0] < len(order) and (issued[0] < NRAW or issued[0] - NRAW in raw_used):
                n = issued[0]
                name, i = order[n]
                slot = n % NRAW
                SP.wait(raw_used.get(n - NRAW, ()))
                SP.todo.append(lambda e, s=slot, src=A[name][i]: e.dma_start(RAW[:, s, :], src)
                               .then_inc(raw_sem[s], 16))
                issued[0] += 1

        def do_split():
            u = splits[0]
            if u * SU >= len(order) * RU:
                return
            splits[0] += 1
            n, half = divmod(u, RU // SU)
            if order[n][0] == "w_cmp":
                unit_ready[u] = (None, None)
                return
            slot, sp = n % NRAW, u % NSPL
            landed = (raw_sem[slot], 16 * (n // NRAW + 1))
            src = RAW[:, slot, half * SU * 128:(half + 1) * SU * 128]
            free = [unit_pe.get(u - NSPL)]
            h = cp(AC, WH[:, sp, :], src, [landed] + free, chain=False)
            E = GP if u % 2 else DV
            lo = tt(E, WL[:, sp, :], src, f32(WH[:, sp, :]), ALU.subtract, [landed, h] + free, chain=False)
            unit_ready[u] = (h, lo)
            if half == RU // SU - 1:
                raw_used[n] = [h, lo, unit_ready[u - 1][0], unit_ready[u - 1][1]]
                issue_raw()

        def tile():
            i = tile_at[0]
            tile_at[0] += 1
            u, r = divmod(i, SU)
            if r == 0:
                while splits[0] <= u + AHEAD - 1 + 0 and splits[0] * SU < len(order) * RU:
                    do_split()
            sl = u % NSPL
            return (WH, sl, r), (WL, sl, r), unit_ready[u][0], unit_ready[u][1], u if r == SU - 1 else None

        def one(which):
            X, sl, r = which
            return X[:, sl, r * 128:(r + 1) * 128]

        def raw_product(o, x, l, t_x, first, last, after):
            i = tile_at[0]
            tile()
            n, r = divmod(i, RU)
            slot = n % NRAW
            landed = (raw_sem[slot], 16 * (n // NRAW + 1))
            end = r == RU - 1
            t = mm(o, x[:, l, :], RAW[:, slot, r * 128:(r + 1) * 128], first, last, list(after) + t_x + [landed],
                   inc=last or end)
            if end:
                raw_used[n] = [t]
                issue_raw()
            return t

        def mm3(o, x, k, first, last, after=(), n=slice(0, T), skip=False):
            h, l, th, tl, end = tile()
            h, l = one(h), one(l)
            mm(o, h, x.hi[:, k, n], first, False, list(after) + x.t[k] + [th], skip=skip)
            mm(o, h, x.lo[:, k, n], False, False, skip=skip)
            t = mm(o, l, x.hi[:, k, n], False, last, [tl], inc=last or end is not None, skip=skip)
            if end is not None:
                unit_pe[end] = t
            return t

        def ntile(o, x, ks, after):
            t = None
            for i, k in enumerate(ks):
                t = mm3(o, x, k, i == 0, i == len(ks) - 1, after if i == 0 else ())
            return t

        def npair_tok(x):
            bank = mbank()
            t = None
            for k in range(16):
                h, l, th, tl, _ = tile()
                _, _, _, _, end = tile()
                h, l = wide(h), wide(l)
                for c in range(2):
                    o = bank.t[:, c * T:(c + 1) * T]
                    s = slice(c * 128, (c + 1) * 128)
                    mm(o, x.hi[:, k, s], h, k == 0 and c == 0, False,
                       (bank.rel if k == 0 else []) + x.t[k] + [th], skip=True)
                    mm(o, x.lo[:, k, s], h, False, False, skip=True)
                    t = mm(o, x.hi[:, k, s], l, False, k == 15 and c == 1, [tl],
                           inc=(c == 1 and (k == 15 or end is not None)), skip=True)
                if end is not None:
                    unit_pe[end] = t
            return bank, t

        def wide(which):
            X, sl, r = which
            return X[:, sl, r * 128:(r + 2) * 128]

        L = {}
        L["vec"] = load(VEC[:, :], A["vecs"])
        L["xT"] = [load(XT[:, 4 * i:4 * i + 4, :], A["xT"][:, 4 * i:4 * i + 4, :]) for i in range(4)]
        issue_raw()
        L["ident"] = load(IDENT[:, :], A["ident"])
        t_ones = GP(lambda e: e.memset(ONES[:, :], 1.0))

        HN = Act(HNH, HNL, 16)

        sq_rel = [[], []]

        def add_sq(x, k, which=0, after=()):
            acc = SQA[:, which, :]
            if k == 0:
                a = act(acc, x, ACT.Square, list(after) + sq_rel[which])
                sq_rel[which] = [a]
                return
            i, s, rel = tmp()
            a = act(s, x, ACT.Square, list(after) + rel)
            t = tt(GP, acc, acc, s, ALU.add, [a] + sq_rel[which])
            tmp_rel[i] = [t]
            sq_rel[which] = [t]

        def sum_sq(which=0):
            b = sbank()
            t = mm(b.t[:, 0:T], ONES[:, :], SQA[:, which, :], True, True, sq_rel[which] + [t_ones] + b.rel, inc=True)
            sq_rel[which] = [t]
            return b, t

        def make_hn(x, k, g, after=(), free=()):
            a = act(HNH[:, k, :], x, ACT.Copy, list(after) + list(free), scale=g)
            b = stt(HNL[:, k, :], x, g, f32(HNH[:, k, :]), ALU.mult, ALU.subtract, list(after) + [a])
            HN.t[k] = [a, b]

        def rsqrt_mean(dst, src, width, after=()):
            a = act(dst, src, ACT.Sqrt, after, bias=EPSC[:, 0:1], scale=1.0 / width)
            return recip(dst, dst, [a]), a

        EPSC = at("EPSC", [128, 8], F32, arena)
        t_eps = GP(lambda e: e.memset(EPSC[:, 0:1], EPS))
        arena = arena + 32

        def rstd_tok(bank):
            mm(bank.t[:, 0:1], RSTD[0:1, 0:128], ONES[0:1, 0:1], True, True, [t_rstd[0], t_ones] + bank.rel)
            t = mm(bank.t[:, 1:2], RSTD[0:1, 128:256], ONES[0:1, 0:1], True, True, inc=True)
            e = cp(DV, RTOK[:, :], bank.t[:, 0:2], [t])
            bank.rel = [e]
            return e

        t_rstd = [None]
        t_rtok = [None]

        for k in range(16):
            make_hn(XT[:, k, :], k, vec("norm1", k), [L["xT"][k // 4], L["vec"]])
        t_x1 = []

        def first_norm():
            for k in range(16):
                add_sq(XT[:, k, :], k)
            t_x1.extend([AC.last(), DV.last()])
            finish_rstd()
            t_rtok[0] = rstd_tok(sbank())

        def finish_rstd():
            b, t = sum_sq()
            t_rstd[0], r = rsqrt_mean(RSTD[:, :], b.t[:, 0:T], 2048.0, [t, t_eps, DV.last()])
            b.rel = [r]

        DF = ar("DF", [128, 2, 2, T], 0)
        DG = ar("DG", [128, 2, 2, T], 4)
        V = ar("V", [128, 8, T], 8)
        X1 = ar("X1", [128, 8, T], 16)
        YAH = ar("YAH", [128, 8, T], 8, F32R)
        YAL = ar("YAL", [128, 8, T], 16, F32R)
        X2 = ar("X2", [128, 8, T], 24)
        WIN = ar("WIN", [128, 2, 2, T], 32)
        W3 = ar("W3", [64, 2, T], 36)
        FW = ar("FW", [128, 2, 2, T], 38)
        HSD = ar("HSD", [128, 2, 2, T], 42)
        KS = ar("KSP", [128, 2, 2, T], 46)
        M1 = ar("M1", [128, 2, T], 50)
        Y = ar("Y", [128, 2, 2, T], 52)
        UT = ar("UT", [128, 2, 2, 128], 56)
        H2 = ar("H2", [64, T], 58)
        ZT = ar("ZT", [33, T], 59)
        FW1 = ar("FW1", [64, 128], 60)
        HA = ar("HA", [64, 3, T], 61)
        VT = ar("VT", [128, 2, 1024], 64)
        O = ar("O", [128, 8, T], 72)
        G16 = ar("G16", [16, T], 80)
        QK = at("QK", [128, 16, T], F32, xt_off)

        L["df"] = load(DF[:, :, :, :], A["df"])
        L["dg"] = load(DG[:, :, :, :], A["dg"])
        L["zt"] = load(ZT[:, :], A["zt"])
        L["fw1"] = load(FW1[0:33, 0:64], A["filt_w1"])
        L["fw2"] = load(FW1[0:64, 64:128], A["filt_w2"])

        t_v = {}

        def scaled(bank, t, w=T):
            i, s, rel = tmp()
            a = tt(DV, s[:, 0:w], bank.t[:, 0:w], RSTD[:, 0:w], ALU.mult, [t, t_rstd[0]] + rel)
            bank.rel = [a]
            return i, s, a

        def conv3(dst, j):
            b = mbank()
            t = ntile(b.t[:, 0:T], HN, range(16), b.rel)
            return conv3_end(dst, j, b, t)

        def conv3_end(dst, j, b, t):
            i, s, a = scaled(b, t)
            c = act(dst, s, ACT.Identity, [a, L["vec"]], bias=vec("cb", j), scale=vec("cw1", j))
            d = stt(dst[:, 1:T], s[:, 0:T - 1], vec("cw0", j), dst[:, 1:T], ALU.mult, ALU.add, [c])
            d = stt(dst[:, 0:T - 1], s[:, 1:T], vec("cw2", j), dst[:, 0:T - 1], ALU.mult, ALU.add, [d])
            tmp_rel[i] = [d, c]
            return d

        def main_hyena():
            for j in range(24):
                dst = (V, X1, X2)[j // 8][:, j % 8, :]
                if j == 0:
                    b = mbank()
                    t = ntile(b.t[:, 0:T], HN, range(16), b.rel)
                    first_norm()
                    t_v[0] = conv3_end(dst, 0, b, t)
                    yield
                    continue
                t_v[j] = conv3(dst, j)
                yield

        def sine(dst, src, P, after):
            k, r = HA[0:P, 1, :], HA[0:P, 2, :]
            magic = 12582912.0
            a = ts(DV, k, src, 1.0 / (2.0 * math.pi), magic, ALU.mult, ALU.add, after)
            a = ts(DV, k, k, magic, None, ALU.subtract)
            c1 = 6.28125
            c2 = float(np.float32(2.0 * math.pi - c1).view(np.uint32) & 0xFFFFF000)
            c2 = float(np.array(int(c2), np.uint32).view(np.float32))
            c3 = 2.0 * math.pi - c1 - c2
            stt(r, k, -c1, src, ALU.mult, ALU.add)
            stt(r, k, -c2, r, ALU.mult, ALU.add)
            stt(r, k, -c3, r, ALU.mult, ALU.add)
            a = ts(DV, r, r, 3.1415925, -3.1415925, ALU.min, ALU.max)
            return act(dst, r, ACT.Sin, [a])

        def side_hyena_all():
            yield from side_filter()
            yield from side_hyena()

        def side_filter():
            b = sbank()
            t = mm(b.t[0:64, 0:T], FW1[0:33, 0:64], ZT[:, :], True, True, [L["fw1"], L["zt"]] + b.rel, inc=True)
            a = ts(DV, HA[:, 0, :], b.t[0:64, 0:T], vec("b1", 0, 64), vec("f1", 0, 64), ALU.add, ALU.mult,
                   [t, L["vec"]])
            b.rel = [a]
            s = sine(H2[:, :], HA[:, 0, :], 64, [a])
            yield
            b = sbank()
            t = mm(b.t[0:64, 0:T], FW1[0:64, 64:128], H2[:, :], True, True, [L["fw2"], s] + b.rel, inc=True)
            a = ts(DV, HA[:, 0, :], b.t[0:64, 0:T], vec("b2", 0, 64), vec("f2", 0, 64), ALU.add, ALU.mult,
                   [t, L["vec"]])
            b.rel = [a]
            t_v["h2"] = sine(H2[:, :], HA[:, 0, :], 64, [a])
            yield

        hy = {}

        def hyena_loads(o, qt, win_free, w3_free):
            hy["next"] = (load(WIN[:, :, :, :], A["win"][qt], win_free),
                          load(W3[:, :, :], A["filt_w3"][:, o, :, qt * 256:(qt + 1) * 256], w3_free))

        hyena_loads(0, 0, [], [])

        def side_hyena():
            for o in range(2):
                for qt in range(4):
                    t_win, t_w3 = hy["next"]
                    ends = []
                    for c in range(2):
                        b = sbank()
                        t = mm(b.t[:, :], H2[:, c * 128:(c + 1) * 128],
                               W3[:, :, :].rearrange("p a n -> p (a n)"), True, True,
                               [t_v["h2"], t_w3] + b.rel, inc=True)
                        w3_free = [t]
                        a = tt(DV, FW[:, c, :, :].rearrange("p a n -> p (a n)"), b.t[:, :],
                               WIN[:, c, :, :].rearrange("p a n -> p (a n)"), ALU.mult, [t, t_win])
                        b.rel = [a]
                        win_free = [a]
                        tt(DV, HSD[:, 0, c, :], FW[:, c, 0, :], FW[:, c, 1, :], ALU.add, [PE.last()])
                        ends.append(tt(DV, HSD[:, 1, c, :], FW[:, c, 1, :], FW[:, c, 0, :], ALU.subtract))
                    t_hsd = ends[-1]
                    if (o, qt) != (1, 3):
                        hyena_loads(*divmod(o * 4 + qt + 1, 4), win_free, w3_free)
                    yield
                    ua = []
                    b = sbank()
                    for ct in range(2):
                        for c in range(2):
                            ua = tr(b.t[:, (c * 2 + ct) * 128:(c * 2 + ct + 1) * 128],
                                    V[:, 2 * qt + ct, c * 128:(c + 1) * 128], IDENT[:, :],
                                    [t_v[2 * qt + ct], L["ident"]] + b.rel, inc=True)
                    t_ut = cp(AC, UT[:, :, :, :].rearrange("p a b c -> p (a b c)"), b.t[:, :], [ua])
                    b.rel = [t_ut]
                    for f in range(2):
                        b = sbank()
                        for ri in range(2):
                            for c in range(2):
                                t = mm(b.t[:, ri * 256:(ri + 1) * 256], DF[:, ri, c, f * 128:(f + 1) * 128],
                                       HSD[:, ri, c, :], c == 0, c == 1, [t_hsd, L["df"]] + b.rel,
                                       inc=(ri == 1 and c == 1))
                        a = cp(AC, KS[:, f, :, :].rearrange("p a n -> p (a n)"), b.t[:, :], [t])
                        b.rel = [a]
                        t_ks = a
                    yield
                    for f in range(2):
                        b = sbank()
                        for ri in range(2):
                            for c in range(2):
                                t = mm(b.t[:, ri * 256:(ri + 1) * 256], DF[:, ri, c, f * 128:(f + 1) * 128],
                                       UT[:, c, :, :].rearrange("p a n -> p (a n)"), c == 0, c == 1,
                                       [t_ut, L["df"]] + b.rel, inc=(ri == 1 and c == 1))
                        m = M1[:, :, :]
                        tt(DV, m.rearrange("p a n -> p (a n)"), b.t[:, :],
                           KS[:, f, :, :].rearrange("p a n -> p (a n)"), ALU.mult, [t, t_ks, PE.last()])
                        tt(DV, Y[:, f, 0, :], M1[:, 0, :], M1[:, 1, :], ALU.add)
                        tt(DV, M1[:, 0, :], b.t[:, 0:256], KS[:, f, 1, :], ALU.mult)
                        a = tt(DV, M1[:, 1, :], b.t[:, 256:512], KS[:, f, 0, :], ALU.mult)
                        b.rel = [a]
                        t_y = tt(DV, Y[:, f, 1, :], M1[:, 0, :], M1[:, 1, :], ALU.subtract)
                    yield
                    b = sbank()
                    for ct in range(2):
                        n = 0
                        for f in range(2):
                            for ri in range(2):
                                t = mm(b.t[:, ct * 256:(ct + 1) * 256], Y[:, f, ri, ct * 128:(ct + 1) * 128],
                                       DG[:, ri, f, :], n == 0, n == 3, [t_y, L["dg"]] + b.rel,
                                       inc=(ct == 1 and n == 3))
                                n += 1
                    for ct in range(2):
                        j = 2 * qt + ct
                        i, s, rel = tmp()
                        a = stt(s, V[:, j, :], vec("hb", o * 8 + j), b.t[:, ct * 256:(ct + 1) * 256],
                                ALU.mult, ALU.add, [t] + rel)
                        if ct == 1:
                            b.rel = [a]
                        if o == 0:
                            t_v[j] = tt(DV, V[:, j, :], s, X1[:, j, :], ALU.mult, [t_v[8 + j], a])
                            tmp_rel[i] = [t_v[j]]
                        else:
                            z = tt(DV, s, s, X2[:, j, :], ALU.mult, [t_v[16 + j], a])
                            YA.t[j] = split(YAH[:, j, :], YAL[:, j, :], s, [z])
                            tmp_rel[i] = YA.t[j]
                    yield

        YA = Act(YAH, YAL, 8)

        def silu_conv(dst, j):
            i, s, rel = tmp()
            t = conv3_to(s, j, rel)
            a = act(dst, s, ACT.Silu, [t] + t_x1)
            tmp_rel[i] = [a]
            return a

        def conv3_to(s, j, rel):
            DV.wait(rel)
            AC.wait(rel)
            return conv3(s, j)

        def main_qkvo():
            for j in range(16):
                t_v["qk", j] = silu_conv(QK[:, j, :], 24 + j)
                yield
            b = mbank()
            t = ntile(b.t[:, 0:T], HN, range(16), b.rel)
            i, s, a = scaled(b, t)
            t_v["g"] = ts(DV, G16[:, :], s[0:16, :], vec("gbias", 0, 16), None, ALU.add)
            tmp_rel[i] = [t_v["g"]]
            yield
            for j in range(4):
                b, t = npair_tok(HN)
                for c in range(2):
                    a = act(VT[:, c, j * 256:(j + 1) * 256], b.t[:, c * T:(c + 1) * T], ACT.Copy,
                            [t, t_rtok[0]], scale=RTOK[:, c:c + 1])
                b.rel = [a]
                t_v["vt", 2 * j] = t_v["vt", 2 * j + 1] = a
                yield
                yield
            for j in range(8):
                b = mbank()
                t = ntile(b.t[:, 0:T], HN, range(16), b.rel)
                i, s, a = scaled(b, t)
                t_v["o", j] = act(O[:, j, :], s, ACT.Sigmoid, [a])
                tmp_rel[i] = [t_v["o", j]]
                yield
        def run(main, side, rate=1.0, skip=0):
            due = 0.0
            for n, _ in enumerate(main):
                if n >= skip:
                    due += rate
                while due >= 1.0:
                    next(side, None)
                    due -= 1.0

        side = side_hyena_all()
        run(main_hyena(), side, 1.25, 7)
        run(main_qkvo(), side, 0.75)
        for _ in side:
            pass
        t_hy = [DV.last(), AC.last(), PE.last()]

        MIX = ar("MIX", [128, 16, T], 24)
        MSK = ar("MSK", [128, 2, 2, T], 40)
        WW = ar("WW", [128, 2, 2, T], 44)
        PP = ar("PP", [128, 2, 2, T], 48)
        EMB = ar("EMB", [128, 2, T], 52)
        RR = ar("RR", [128, 2, T], 54)
        ROWS = ar("ROWS", [4, 4, 2, T], 56)
        SEL = ar("SEL", [4, 4, 128], 81)
        NN = ar("NN", [128, 2, T], 83)
        GTT = ar("GTT", [128, 4, 4], 85)
        YBH = ar("YBH", [128, 8, T], 0, F32R)
        YBL = ar("YBL", [128, 8, T], 72, F32R)
        YB = Act(YBH, YBL, 8)

        def side_mlstm():
            t_msk = load(MSK[:, :, :, :], A["mmask"], t_hy)
            t_sel = load(SEL[:, :, :], A["sel4"], [t_v["g"]])
            a = t_v["g"]
            bi, bf = sbank(), sbank()
            for d in range(2):
                mm(bi.t[0:4, d * T:(d + 1) * T], IDENT[0:16, 8 * d:8 * d + 4], G16[:, :], True, True, [a] + bi.rel)
            for d in range(2):
                t = mm(bf.t[0:4, d * T:(d + 1) * T], IDENT[0:16, 8 * d + 4:8 * d + 8], G16[:, :], True, True,
                       bf.rel, inc=True)
            r = [ROWS[:, i, :, :] for i in range(4)]
            fl = [ROWS[:, i, :, :].rearrange("p a n -> p (a n)") for i in range(4)]
            a = cp(AC, fl[3], bf.t[0:4, :], [t])
            a = stt(fl[0], fl[3], -1.0, fl[3], ALU.mult, ALU.max, [a])
            a = act(fl[0], fl[0], ACT.Exp, [a], scale=-1.0)
            a = act(fl[0], fl[0], ACT.Ln, [a], bias=1.0)
            a = stt(fl[0], fl[3], 0.0, fl[0], ALU.min, ALU.subtract, [a])
            bf.rel = [a]
            on = ONES[0:4, 0:1].broadcast_to([4, T])
            for d in range(2):
                x = r[0][:, d, :] if d == 0 else r[0][:, d, ::-1]
                y = r[1][:, d, :] if d == 0 else r[1][:, d, ::-1]
                a = DV(lambda e, x=x, y=y: e.tensor_tensor_scan(y, on, x, 0.0, ALU.mult, ALU.add), [t_ones])
            a = tt(DV, fl[2], bi.t[0:4, :], fl[1], ALU.subtract)
            bi.rel = [a]
            for d in range(2):
                x = r[2][:, d, :] if d == 0 else r[2][:, d, ::-1]
                y = r[3][:, d, :] if d == 0 else r[3][:, d, ::-1]
                a = DV(lambda e, x=x, y=y: e.tensor_tensor_scan(y, x, x, 0.0, ALU.max, ALU.max))
            a = tt(DV, fl[0], fl[1], fl[3], ALU.add)
            t_em = act(fl[0], fl[0], ACT.Exp, [a], scale=-1.0)
            a = ts(DV, fl[3], fl[3], -1.0, None, ALU.mult, None, [t_em])
            t_nm = a
            yield
            b = sbank()
            for d in range(2):
                for c in range(2):
                    j = d * 2 + c
                    t = mm(b.t[:, 4 * j:4 * j + 4], r[2][:, d, c * 128:(c + 1) * 128], IDENT[0:4, 0:4], True, True,
                           [t_nm] + b.rel, inc=True)
            t_gtt = cp(DV, GTT[:, :, :].rearrange("p a b -> p (a b)"), b.t[:, 0:16], [t])
            b.rel = [t_gtt]
            yield
            pe_last = None
            for h in range(4):
                bs, bn, be = sbank(), sbank(), sbank()
                for c in range(2):
                    for k in range(2):
                        q, kk = QK[:, 2 * h + k, :], QK[:, 8 + 2 * h + k, c * 128:(c + 1) * 128]
                        t_s = mm(bs.t[:, c * T:(c + 1) * T], kk, q, k == 0, k == 1,
                                 [t_v["qk", 2 * h + k], t_v["qk", 8 + 2 * h + k]] + bs.rel, inc=(k == 1))
                t_n = mm(bn.t[:, :], SEL[:, h, :], fl[3], True, True, [t_nm, t_sel] + bn.rel, inc=True)
                t_e = mm(be.t[:, :], SEL[:, h, :], fl[0], True, True, [t_em] + be.rel, inc=True)
                t_emb = cp(AC, EMB[:, :, :].rearrange("p a n -> p (a n)"), be.t[:, :], [t_e, DV.last()])
                be.rel = [t_emb]
                for d in range(2):
                    for c in range(2):
                        a = stt(WW[:, d, c, :], bn.t[:, d * T:(d + 1) * T], GTT[:, d * 2 + c, h:h + 1],
                                MSK[:, d, c, :], ALU.add, ALU.min, [t_n, t_gtt, t_msk])
                bn.rel = [a]
                a = act(WW[:, :, :, :].rearrange("p a b n -> p (a b n)"),
                        WW[:, :, :, :].rearrange("p a b n -> p (a b n)"), ACT.Exp, [a])
                for d in range(2):
                    p = stt(PP[:, d, :, :].rearrange("p b n -> p (b n)"), bs.t[:, :], 1.0 / 16.0,
                            WW[:, d, :, :].rearrange("p b n -> p (b n)"), ALU.mult, ALU.mult, [t_s, a, pe_last])
                bs.rel = [p]
                yield
                bd = sbank()
                nb = [sbank(), sbank()]
                for d in range(2):
                    cs = (0, 1) if d == 0 else (1, 0)
                    for n, c in enumerate(cs):
                        sl = slice(0, T) if n == 0 else (slice(128, T) if d == 0 else slice(0, 128))
                        o0 = d * T
                        t_d = mm(bd.t[:, o0 + sl.start:o0 + sl.stop], ONES[:, :], PP[:, d, c, sl],
                                 n == 0, n == 1, [p] + bd.rel, inc=(n == 1), skip=True)
                    for v in range(2):
                        for n, c in enumerate(cs):
                            sl = slice(0, T) if n == 0 else (slice(128, T) if d == 0 else slice(0, 128))
                            t_u = mm(nb[d].t[:, v * T + sl.start:v * T + sl.stop],
                                     VT[:, c, h * 256 + v * 128:h * 256 + (v + 1) * 128], PP[:, d, c, sl],
                                     n == 0, n == 1, [t_v["vt", 2 * h + v]] + nb[d].rel,
                                     inc=(n == 1), skip=True)
                pe_last = t_u
                rr = RR[:, :, :].rearrange("p a n -> p (a n)")
                tt(DV, rr, bd.t[:, :], EMB[:, :, :].rearrange("p a n -> p (a n)"), ALU.max, [t_d])
                a = stt(rr, bd.t[:, :], -1.0, rr, ALU.mult, ALU.max)
                bd.rel = [a]
                a = recip(RR[:, :, :].rearrange("p a n -> p (a n)"), RR[:, :, :].rearrange("p a n -> p (a n)"))
                for v in range(2):
                    i, s, rel = tmp()
                    a = tt(DV, NN[:, v, :], nb[0].t[:, v * T:(v + 1) * T], RR[:, 0, :], ALU.mult, [t_u])
                    a = tt(DV, s, nb[1].t[:, v * T:(v + 1) * T], RR[:, 1, :], ALU.mult, rel)
                    tt(DV, s, s, NN[:, v, :], ALU.add)
                    j = 2 * h + v
                    z = tt(DV, s, s, O[:, j, :], ALU.mult, [t_v["o", j]])
                    YB.t[j] = split(YBH[:, j, :], YBL[:, j, :], s, [z])
                    tmp_rel[i] = YB.t[j]
                nb[0].rel = nb[1].rel = [z]
                yield

        def branch(x, first):
            for n in range(16):
                b = mbank()
                ntile(b.t[:, 0:T], HN, range(16), b.rel)
                t2 = ntile(b.t[:, T:2 * T], x, range(8), [])
                i, s, a = scaled(b, t2)
                g = act(s, s, ACT.Sigmoid, [a])
                if first:
                    z = tt(DV, MIX[:, n, :], s, b.t[:, T:2 * T], ALU.mult, [g, t2] + t_hy)
                    tmp_rel[i] = [z]
                    b.rel = [a, z]
                else:
                    z = tt(DV, s, s, b.t[:, T:2 * T], ALU.mult, [g, t2])
                    b.rel = [a, z]
                    z = tt(DV, s, s, MIX[:, n, :], ALU.add)
                    MX.t[n] = split(MXH[:, n, :], MXL[:, n, :], s, [z], t_ml)
                    tmp_rel[i] = MX.t[n]
                yield

        side = side_mlstm()
        run(branch(YA, True), side, 0.8)
        for _ in side:
            pass
        t_ml = [DV.last(), AC.last(), PE.last()]
        t_xt = [load(XT[:, 4 * i:4 * i + 4, :], A["xT"][:, 4 * i:4 * i + 4, :], t_ml) for i in range(4)]
        MXH = ar("MXH", [128, 16, T], 8, F32R)
        MXL = ar("MXL", [128, 16, T], 44, F32R)
        MX = Act(MXH, MXL, 16)
        t_mlg = t_ml
        for _ in branch(YB, False):
            pass

        def residual(x, ks, bank_after, n, finish):
            b = mbank()
            t = ntile(b.t[:, 0:T], x, ks, b.rel)
            a = tt(DV, XT[:, n, :], b.t[:, 0:T], XT[:, n, :], ALU.add, [t] + bank_after)
            b.rel = [a]
            if finish:
                finish(n, a)

        def norm_after(gname):
            def f(n, a):
                make_hn(XT[:, n, :], n, vec(gname, n), [a], [hn_free[0]])
                add_sq(XT[:, n, :], n, 0, [a])
            return f

        hn_free = [None]

        hn_free[0] = PE.last()
        f = norm_after("norm2")
        for n in range(16):
            residual(MX, range(16), [t_xt[n // 4]], n, f)

        HDH = ar("HDH", [128, 22, T], 0, F32R)
        HDL = ar("HDL", [128, 22, T], 22, F32R)
        HD = Act(HDH, HDL, 22)
        SG = ar("SG", [128, 2, T], 44)
        HS = ar("HS", [128, 2, T], 46)

        def ffn(finish):
            used = [PE.last(), DV.last(), AC.last()]
            for half in range(2):
                for j in range(22):
                    b = mbank()
                    ntile(b.t[:, 0:T], HN, range(16), b.rel)
                    if half == 0 and j == 0:
                        finish_rstd()
                    t = ntile(b.t[:, T:2 * T], HN, range(16), [])
                    i, s, a = scaled(b, t)
                    sg = SG[:, j % 2, :]
                    g = act(sg, s, ACT.Silu, [a] + used)
                    z = tt(DV, s, b.t[:, T:2 * T], RSTD[:, :], ALU.mult, [g])
                    b.rel = [z]
                    z = tt(DV, s, s, sg, ALU.mult)
                    HD.t[j] = split(HDH[:, j, :], HDL[:, j, :], s, [z], used)
                    tmp_rel[i] = HD.t[j]
                hn_free[0] = PE.last()
                for n in range(16):
                    residual(HD, range(22), [], n, finish if half else None)
                used = [PE.last()]

        def x_two_norms(n, a):
            add_sq(XT[:, n, :], n, 0, [a])
            b = ts(DV, XT[:, n, :], XT[:, n, :], vec("normf", n), None, ALU.mult, None, [a, AC.last()])
            make_hn(XT[:, n, :], n, vec("attn", n), [b], [hn_free[0]])
            add_sq(XT[:, n, :], n, 1, [b])

        ffn(x_two_norms)
        t_rf = [None]

        def second_norm():
            b0, t0 = sum_sq(0)
            t_rf[0], r = rsqrt_mean(RF[:, :], b0.t[:, 0:T], 2048.0, [t0])
            b0.rel = [r]
            b1, t1 = sum_sq(1)
            i, s, rel = tmp()
            a = tt(DV, s, RF[:, :], RF[:, :], ALU.mult, rel)
            a = tt(DV, s, s, b1.t[:, 0:T], ALU.mult, [t1])
            b1.rel = [a]
            t_ra, r = rsqrt_mean(RSTD[:, :], s, 2048.0, [a])
            tmp_rel[i] = [r]
            t_rstd[0] = tt(DV, RSTD[:, :], RSTD[:, :], RF[:, :], ALU.mult)
            t_rtok[0] = rstd_tok(sbank())

        t_b1 = [DV.last(), AC.last(), PE.last()]

        GQ = ar("GQ", [128, 4, T], 0)
        GK = ar("GK", [128, 4, T], 4)
        VTG = ar("VTG", [128, 2, 1024], 8)
        OG = ar("OG", [128, 8, T], 16)
        GG = ar("GG", [128, 4, T], 24)
        GB = ar("GB", [128, 4, T], 28)
        GE = ar("GE", [128, 4, T], 32)
        QE = ar("QE", [128, 4, T], 36)
        KE = GG
        PT = ar("PT", [128, 2, 4, 128], 40)
        PT2 = ar("PT2", [128, 4, 128], 44)
        LM = at("LM", [128, 7, 128], mybir.dt.uint8, arena + 46 * KB)
        RST = ar("RST", [128, T], 47)
        LR = ar("LR", [16, T], 38)
        GW2 = ar("GW2", [16, 512], 36)
        MGH = ar("MGH", [128, 8, T], 48, F32R)
        MGL = ar("MGL", [128, 8, T], 56, F32R)
        NKC = ar("NKC", [128, 2, 2, T], 64)
        NKS = ar("NKS", [128, 2, 2, T], 68)
        NVT = ar("NVT", [128, 2, 2, 256], 72)
        NQA = ar("NQA", [128, 8, T], 76)
        AM = ar("AM", [128, 384], 84)
        MG = Act(MGH, MGL, 8)

        LM4 = ar("LM4", [128, 7, 128], 32, I32)
        t_lm = cp(DV, LM[:, :, :], LM4[:, :, :], [load(LM4[:, :, :], A["lmask"], t_b1)] + t_b1)
        t_rst = load(RST[:, :], A["reset"], t_b1)
        t_gw2 = load(GW2[:, :], A["gla_gate_w2"], t_b1)

        def conv4(dst, j):
            b = mbank()
            t = ntile(b.t[:, 0:T], HN, range(16), b.rel)
            if j == 0:
                second_norm()
            i, s, a = scaled(b, t)
            i2, y, rel = tmp()
            c = act(y, s, ACT.Copy, [a] + rel, scale=vec("gw3", j))
            for m in range(1, 4):
                d = stt(y[:, m:T], s[:, 0:T - m], vec(f"gw{3 - m}", j), y[:, m:T], ALU.mult, ALU.add, [c])
            tmp_rel[i] = [d, c]
            if dst is None:
                f = act(y, y, ACT.Silu, [d])
                return i2, y, f
            f = act(dst, y, ACT.Silu, [d] + t_b1)
            tmp_rel[i2] = [f]
            return f

        def transpose_v(i2, y, f, j):
            b = sbank()
            for c in range(2):
                t = tr(b.t[:, c * 128:(c + 1) * 128], y[:, c * 128:(c + 1) * 128], IDENT[:, :], [f] + b.rel,
                       inc=True)
            tmp_rel[i2] = [t]
            for c in range(2):
                a = cp(DV, VTG[:, c, j * 128:(j + 1) * 128], b.t[:, c * 128:(c + 1) * 128], [t] + t_b1)
            b.rel = [a]
            t_v["vtg", j] = a

        held = None
        for j in range(16):
            if j < 8:
                t_v["g", j] = conv4((GQ if j < 4 else GK)[:, j % 4, :], j)
            else:
                new = conv4(None, j)
                if held:
                    transpose_v(*held)
                held = (*new, j - 8)
        b = mbank()
        t = ntile(b.t[:, 0:T], HN, range(16), b.rel)
        t_lr = tt(DV, LR[:, :], b.t[0:16, 0:T], RSTD[0:16, :], ALU.mult, [t] + t_b1)
        b.rel = [t_lr]
        transpose_v(*held)

        def flat(x):
            return x[:, :, :].rearrange("p a n -> p (a n)")

        def side_gla():
            bz = [sbank(), sbank()]
            for h in range(4):
                t = mm(bz[h // 2].t[:, (h % 2) * T:(h % 2 + 1) * T], GW2[:, h * 128:(h + 1) * 128], LR[:, :],
                       True, True, [t_lr, t_gw2] + bz[h // 2].rel, inc=True)
            for h in range(4):
                a = ts(DV, GG[:, h, :], bz[h // 2].t[:, (h % 2) * T:(h % 2 + 1) * T], vec("gb", h), None, ALU.add,
                       None, [t])
            bz[0].rel = bz[1].rel = [a]
            a = stt(flat(GE), flat(GG), -1.0, flat(GG), ALU.mult, ALU.max)
            a = act(flat(GE), flat(GE), ACT.Exp, [a], scale=-1.0)
            a = act(flat(GE), flat(GE), ACT.Ln, [a], bias=1.0)
            a = stt(flat(GG), flat(GG), 0.0, flat(GE), ALU.min, ALU.subtract, [a])
            a = ts(DV, flat(GG), flat(GG), 1.0 / 16.0, None, ALU.mult)
            for h in range(4):
                a = DV(lambda e, h=h: e.tensor_tensor_scan(GB[:, h, :], RST[:, :], GG[:, h, :], 0.0, ALU.mult,
                                                           ALU.add), [t_rst])
            a = ts(DV, flat(GQ), flat(GQ), 128.0 ** -0.5, None, ALU.mult, None, [t_v["g", j] for j in range(4)])
            t_gq = a
            t_gb = a
            pe_ge = None
            yield
            bb = [sbank(), sbank()]
            for c in range(2):
                for h in range(4):
                    t = mm(bb[c].t[:, h * 128:(h + 1) * 128], GK[:, h, c * 128:(c + 1) * 128],
                           GQ[:, h, c * 128:(c + 1) * 128], True, True, [a, t_v["g", 4 + h]] + bb[c].rel, inc=True)
            for c in range(2):
                a = tt(DV, PT[:, c, :, :], bb[c].t[:, :].rearrange("p (a n) -> p a n", a=4),
                       IDENT[:, :].unsqueeze(1).broadcast_to([128, 4, 128]), ALU.mult, [t])
                bb[c].rel = [a]
            for lv in range(7):
                w = 1 << lv
                g = flat(GB).rearrange("p (n a w) -> p n a w", a=2, w=w)
                e4 = flat(GE).rearrange("p (n a w) -> p n a w", a=2, w=w)
                n = 1024 // (2 * w)
                end = g[:, :, 0, w - 1:w].broadcast_to([128, n, w])
                a0 = tt(DV, e4[:, :, 0, :], end, g[:, :, 0, :], ALU.subtract, [pe_ge])
                if w < 64:
                    a = tt(GP, e4[:, :, 1, :], g[:, :, 1, :], end, ALU.subtract, [t_gb, pe_ge])
                else:
                    a = cp(GP, e4[:, :, 1, :], g[:, :, 1, :], [t_gb, pe_ge])
                a = act(flat(GE), flat(GE), ACT.Exp, [a0, a])
                q = tt(GP, flat(QE), flat(GQ), flat(GE), ALU.mult, [a, t_gq])
                a = tt(DV, KE[:, :, :].rearrange("p a n -> p (a n)"), flat(GK), flat(GE), ALU.mult,
                       [a, pe_ge])
                yield
                bb = [sbank(), sbank()]
                for c in range(2):
                    for h in range(4):
                        t = mm(bb[c].t[:, h * 128:(h + 1) * 128], KE[:, h, c * 128:(c + 1) * 128],
                               QE[:, h, c * 128:(c + 1) * 128], True, True, [a, q] + bb[c].rel, inc=True)
                pe_ge = t
                for c in range(2):
                    m = LM[:, lv, :].unsqueeze(1).broadcast_to([128, 4, 128])
                    a = DV(lambda e, c=c, m=m, src=bb[c].t: e.copy_predicated(
                        PT[:, c, :, :], m, src[:, :].rearrange("p (a n) -> p a n", a=4)), [t, t_lm])
                    bb[c].rel = [a]
            for h in range(4):
                last2 = GB[:, h, 191:192]
                last1 = GB[:, h, 127:128]
                last0 = GB[:, h, 63:64]
                cp(DV, GE[:, h, 128:192], GB[:, h, 128:192], [PE.last(), q])
                ts(DV, GE[:, h, 192:256], GB[:, h, 192:256], last2, None, ALU.add)
                ts(DV, GE[:, h, 64:128], GB[:, h, 64:128], last1, -1.0, ALU.subtract, ALU.mult)
                ts(DV, GE[:, h, 0:64], GB[:, h, 0:64], last0, -1.0, ALU.subtract, ALU.mult)
                a = ts(DV, GE[:, h, 0:64], GE[:, h, 0:64], last1, None, ALU.add)
            a = act(flat(GE), flat(GE), ACT.Exp, [a])
            tt(DV, QE[:, :, 128:256], GQ[:, :, 128:256], GE[:, :, 128:256], ALU.mult, [a])
            a = tt(DV, GE[:, :, 0:128], GK[:, :, 0:128], GE[:, :, 0:128], ALU.mult)
            yield
            b = sbank()
            for h in range(4):
                t = mm(b.t[:, h * 128:(h + 1) * 128], GE[:, h, 0:128], QE[:, h, 128:256], True, True,
                       [a] + b.rel, inc=True)
            p = cp(AC, flat(PT2), b.t[:, :], [t])
            b.rel = [p]
            yield
            for h in range(4):
                b = sbank()
                for v in range(2):
                    cs = slice(h * 256 + v * 128, h * 256 + (v + 1) * 128)
                    o = v * T
                    mm(b.t[:, o:o + 128], VTG[:, 0, cs], PT[:, 0, h, :], True, True,
                       [p, DV.last(), t_v["vtg", 2 * h + v]] + b.rel)
                    mm(b.t[:, o + 128:o + 256], VTG[:, 0, cs], PT2[:, h, :], True, False)
                    t = mm(b.t[:, o + 128:o + 256], VTG[:, 1, cs], PT[:, 1, h, :], False, True, inc=True)
                sq = QE[:, 0:2, :].rearrange("p a n -> p (a n)")
                a = act(sq, b.t[:, :], ACT.Square, [t, PE.last()])
                b2 = sbank()
                yield
                for v in range(2):
                    t = mm(b2.t[:, 0:T], ONES[:, :], QE[:, v, :], v == 0, v == 1, [a] + b2.rel, inc=True)
                r = GG[:, 0, :]
                ra, rr = rsqrt_mean(r, b2.t[:, 0:T], 256.0, [t, DV.last()])
                b2.rel = [rr]
                for v in range(2):
                    i, s, rel = tmp()
                    j = 2 * h + v
                    a = tt(DV, s, b.t[:, v * T:(v + 1) * T], r, ALU.mult, [ra] + rel)
                    z = stt(s, s, vec("gng", v), OG[:, j, :], ALU.mult, ALU.mult, [t_v["og", j]])
                    MG.t[j] = split(MGH[:, j, :], MGL[:, j, :], s, [z])
                    tmp_rel[i] = MG.t[j]
                b.rel = [a]
                yield

        def plain(dst, after=()):
            b = mbank()
            t = ntile(b.t[:, 0:T], HN, range(16), b.rel)
            a = tt(DV, dst, b.t[:, 0:T], RSTD[:, :], ALU.mult, [t, t_rstd[0]] + list(after))
            b.rel = [a]
            return a

        def main_second(side):
            for j in range(8):
                b = mbank()
                t = ntile(b.t[:, 0:T], HN, range(16), b.rel)
                i, s, a = scaled(b, t)
                t_v["og", j] = act(OG[:, j, :], s, ACT.Silu, [a])
                tmp_rel[i] = [t_v["og", j]]
                yield
            for j in range(8):
                t_v["nq", j] = plain(NQA[:, j, :], t_b1)
                yield
            for name, dst in (("ks", NKS), ("kc", NKC)):
                for m in range(2):
                    for g in range(2):
                        t_v[name, m, g] = plain(dst[:, m, g, :], t_b1)
                        yield
            for m in range(2):
                b, t = npair_tok(HN)
                for c in range(2):
                    a = ts(DV, NVT[:, m, c, :], b.t[:, c * T:(c + 1) * T],
                           RTOK[:, c:c + 1], None, ALU.mult, None, [t, t_rtok[0]] + t_b1)
                b.rel = [a]
                t_v["vs", m, 0] = t_v["vs", m, 1] = a
                yield
                yield
            while "gla" not in t_v:
                next(side)
            b = mbank()
            t = ntile(b.t[:, 0:T], HN, range(16), b.rel)
            i, s, a = scaled(b, t)
            g = act(s[0:24, :], s[0:24, :], ACT.Sigmoid, [a])
            yield
            b = sbank()
            for c in range(2):
                t = tr(b.t[:, c * 24:(c + 1) * 24], s[0:24, c * 128:(c + 1) * 128], IDENT[0:24, 0:24],
                       [g] + b.rel, inc=True)
            tmp_rel[i] = [t]
            t_v["gate"] = cp(DV, GATE[:, :, :].rearrange("p a n -> p (a n)"), b.t[:, 0:48], [t])
            b.rel = [t_v["gate"]]
            for m in range(2):
                while ("cb", m) not in t_v:
                    next(side)
                b = mbank()
                x = CB[:, m, :, :, :].rearrange("p a b n -> p a (b n)")
                for l in range(32):
                    t = raw_product(b.t[0:30, 0:128], x, l, t_v["cb", m], l == 0, l == 31, b.rel if l == 0 else ())
                a = act(HIDT[0:30, m, :], b.t[0:30, 0:128], ACT.Silu, [t])
                b.rel = [a]
                t_v["hidt", m] = a
                yield
            for n in range(16):
                b = mbank()
                t = ntile(b.t[:, 0:T], MG, range(8), b.rel)
                z = tt(DV, XT[:, n, :], XT[:, n, :], RF[:, :], ALU.mult, [t_rf[0]])
                z = tt(DV, XT[:, n, :], XT[:, n, :], b.t[:, 0:T], ALU.add, [t])
                b.rel = [z]
                t_v["h", n] = z
                yield

        MNH = ar("MNH", [128, 8, T], 0, F32R)
        MNL = ar("MNL", [128, 8, T], 8, F32R)
        CB = ar("CB", [128, 2, 32, 2, 15], 16)
        HIDT = ar("HIDT", [32, 2, 128], 84 + 1.5)
        PCT = ar("PCT", [16, 8, 2, 128], 24)
        PTS = ar("PTS", [128, 2, 2, 384], 16)
        SS = ar("SS", [128, 2, 2, 384], 32)
        SQ2 = ar("SQ2", [128, 2, T], 38)
        RN = ar("RN", [128, 2, T], 40)
        CW2 = ar("CW2", [128, 2, 128], 42)
        HID = ar("HID", [128, 2, 32], 43)
        POS = ar("POS", [128, 2, 32], 43.25)
        KCN = ar("KCN", [128, 32], 43.5)
        GATE = ar("GATE", [128, 2, 24], 43.75)
        VCN = ar("VCN", [16, 2, 128], 44)
        PC = ar("PC", [128, 16, 16], 45)
        PC2 = ar("PC2", [128, 16, 16], 46)
        CM = ar("CM", [128, 2, 2, 16], 47)
        SMALL = ar("SMALL", [128, 16, 4], 47.25)
        STAT = ar("STAT", [128, 2, 4, 4], 47.5)
        MN = Act(MNH, MNL, 8)

        def head_norm(x2, gname, scale, after, bank=None, n=512):
            sq = SQ2[:, :, :].rearrange("p a n -> p (a n)")[:, 0:n]
            rn = RN[:, :, :].rearrange("p a n -> p (a n)")[:, 0:n]
            a = act(sq, x2, ACT.Square, list(after) + [PE.last()])
            b = sbank()
            t = mm(b.t[:, 0:n], ONES[:, :], sq, True, True, [a] + b.rel, inc=True)
            yield
            ra, rr = rsqrt_mean(rn, b.t[:, 0:n], 128.0, [t, DV.last()])
            b.rel = [rr]
            z = tt(DV, x2, x2, rn, ALU.mult, [ra])
            z = ts(DV, x2, x2, vec(gname), scale, ALU.mult, ALU.mult)
            yield z

        def blocks(m, t_pos):
            for g in range(2):
                win = NKC[:, m, g, :].rearrange("p (n l) -> p l n", l=16)
                for half in range(2):
                    o = CB[:, m, half * 16:(half + 1) * 16, g, :]
                    i1 = POS[:, m, half * 16:(half + 1) * 16].unsqueeze(2).broadcast_to([128, 16, 15])
                    st = tt(DV, o, win[:, :, half:half + 15], i1, ALU.add, [t_v["kc", m, g], t_pos])
            t_v["cb", m] = [st]

        def side_nsa():
            t_gl = [DV.last(), AC.last(), PE.last(), GP.last()]
            t_v["gla"] = t_gl
            for E in (DV, AC, PE, GP):
                E.wait(t_gl)
            t_pos = load(POS[:, :, :], A["posT"], t_gl)
            t_cw2 = load(CW2[:, :, :], A["cmp_w2"])
            t_cm = load(CM[:, :, :, :], A["cmask"])
            while ("kc", 1, 1) not in t_v:
                yield
            blocks(0, t_pos)
            blocks(1, t_pos)
            yield
            for m, gn in ((0, "ksg"), (1, "kwg")):
                for z in head_norm(NKS[:, m, :, :].rearrange("p a n -> p (a n)"), gn, 1.0,
                                   [t_v["ks", m, 0], t_v["ks", m, 1]]):
                    yield
            t_kk = z
            for j in range(0, 8, 2):
                for z in head_norm(NQA[:, j:j + 2, :].rearrange("p a n -> p (a n)"), "qg", 128.0 ** -0.5,
                                   [t_v["nq", j], t_v["nq", j + 1]]):
                    yield
            t_q = z
            while ("hidt", 1) not in t_v:
                yield
            b = sbank()
            for m in range(2):
                t = tr(b.t[:, m * 32:m * 32 + 30], HIDT[0:30, m, :], IDENT[0:30, 0:30],
                       [t_v["hidt", m]] + b.rel, inc=True)
            a = cp(DV, HID[:, :, 0:30], b.t[:, 0:64].rearrange("p (m n) -> p m n", m=2)[:, :, 0:30], [t])
            b.rel = [a]
            t_v["hid", 0] = t_v["hid", 1] = a
            yield
            b = sbank()
            t = mm(b.t[:, 0:30], CW2[:, 0, :], HID[:, 0, 0:30], True, True, [t_v["hid", 0], t_cw2] + b.rel, inc=True)
            a = cp(DV, KCN[:, 0:30], b.t[:, 0:30], [t])
            b.rel = [a]
            b = sbank()
            for g in range(2):
                t = mm(b.t[0:15, g * 128:(g + 1) * 128], HID[:, 1, 15 * g:15 * g + 15], CW2[:, 1, :], True, True,
                       [t_v["hid", 1]] + b.rel, inc=True)
            v = cp(DV, VCN[0:15, :, :].rearrange("p a n -> p (a n)"), b.t[0:15, 0:256], [t])
            b.rel = [v]
            t_vcn = v
            yield
            z = None
            for z in head_norm(KCN[:, 0:30], "kcg", 1.0, [a], n=30):
                yield
            t_kcn = z
            b = sbank()
            for h in range(8):
                for c in range(2):
                    o = (h * 2 + c) * 16
                    t = mm(b.t[:, o:o + 15], NQA[:, h, c * 128:(c + 1) * 128],
                           KCN[:, 15 * (h // 4):15 * (h // 4) + 15], True, True, [t_q, t_kcn, DV.last()] + b.rel,
                           inc=True)
            pc4 = PC[:, :, :].rearrange("p (h c) n -> p h c n", c=2)
            for c in range(2):
                a = tt(DV, pc4[:, :, c, 0:15],
                       b.t[:, 0:256].rearrange("p (h c n) -> p h c n", c=2, n=16)[:, :, c, 0:15],
                       CM[:, 0, c, 0:15].unsqueeze(1).broadcast_to([128, 8, 15]), ALU.add, [t, t_cm])
            b.rel = [a]
            mx = SMALL[:, :, 0:1]
            DV(lambda e: e.tensor_reduce(SMALL[:, :, 0], PC[:, :, 0:15], AX.X, ALU.max))
            a = tt(DV, PC[:, :, 0:15], PC[:, :, 0:15], mx.broadcast_to([128, 16, 15]), ALU.subtract)
            a = act(PC2[:, :, 0:15], PC[:, :, 0:15], ACT.Exp, [a])
            DV(lambda e: e.tensor_reduce(SMALL[:, :, 1], PC2[:, :, 0:15], AX.X, ALU.add), [a])
            recip(SMALL[:, :, 2], SMALL[:, :, 1])
            sm = SMALL[:, :, :].rearrange("p (h c) n -> p h c n", c=2)
            for c in range(2):
                gt = GATE[:, c, :].rearrange("p (h r) -> p h r", r=3)
                tt(DV, sm[:, :, c, 3], sm[:, :, c, 2], gt[:, :, 0], ALU.mult, [t_v["gate"]])
            a = tt(DV, PC2[:, :, 0:15], PC2[:, :, 0:15], SMALL[:, :, 3:4].broadcast_to([128, 16, 15]), ALU.mult)
            p4 = PC2[:, :, :].rearrange("p (h c) n -> p h c n", c=2)
            for c in range(2):
                a = tt(DV, p4[:, :, c, 0:15], p4[:, :, c, 0:15],
                       CM[:, 1, c, 0:15].unsqueeze(1).broadcast_to([128, 8, 15]), ALU.mult)
            yield
            t_pct = {}
            for q in range(4):
                b = sbank()
                for m in range(4):
                    hc = 4 * q + m
                    t = tr(b.t[0:15, m * 128:(m + 1) * 128], PC2[:, hc, 0:15], IDENT[:, :], [a] + b.rel, inc=True)
                c0 = cp(AC, PCT[0:15, 2 * q:2 * q + 2, :, :].rearrange("p a b n -> p (a b n)"),
                        b.t[0:15, :], [t, PE.last()])
                b.rel = [c0]
                t_pct[2 * q] = t_pct[2 * q + 1] = c0
                if q % 2:
                    yield

            t_am = t_amask

            def scores(h):
                out = []
                for m in range(2):
                    b = sbank()
                    g = h // 4
                    for c in range(2):
                        n = 128 * (c + 1)
                        o = 128 * c
                        t = mm(b.t[:, o:o + n], NQA[:, h, c * 128:(c + 1) * 128], NKS[:, m, g, 0:n], True, True,
                               [t_kk, t_q] + b.rel, inc=(c == 1))
                    out.append((b, t))
                return out

            ss_free = [None, None]
            pts_free = [None, None]

            def soft(h, bt):
                w = h % 2
                s = SS[:, w, :, :]
                st = STAT[:, w, :, :]
                for m, (b, t) in enumerate(bt):
                    a = tt(DV, s[:, m, :], b.t[:, 0:384], AM[:, :], ALU.add, [t, t_am, ss_free[w]])
                    b.rel = [a]
                xs = [s[:, :, 0:128], s[:, :, 128:384]]
                for c in range(2):
                    a = DV(lambda e, x=xs[c], o=st[:, 2 * c:2 * c + 2, 0]: e.tensor_reduce(
                        o, x, AX.X, ALU.max, negate=True))
                for c in range(2):
                    for m in range(2):
                        x = xs[c][:, m, :]
                        q = 2 * c + m
                        e1 = act(x, x, ACT.Exp, [a], bias=st[:, q, 0:1], accum=st[:, q, 1:2])
                recip(st[:, :, 2], st[:, :, 1], [e1])
                for c in range(2):
                    a = tt(DV, st[:, 2 * c:2 * c + 2, 3], st[:, 2 * c:2 * c + 2, 2],
                           GATE[:, c, 3 * h + 1:3 * h + 3], ALU.mult)
                for c in range(2):
                    n = 128 * (c + 1)
                    p = tt(GP, xs[c], xs[c], st[:, 2 * c:2 * c + 2, 3:4].broadcast_to([128, 2, n]), ALU.mult, [a])
                return p

            def turnp(h, a):
                w = h % 2
                out = []
                for m in range(2):
                    b = sbank()
                    for k in range(3):
                        t = tr(b.t[:, k * 128:(k + 1) * 128], SS[:, w, m, k * 128:(k + 1) * 128], IDENT[:, :],
                               [a] + b.rel, inc=(k == 2))
                    a2 = cp(AC if m else DV, PTS[:, w, m, :], b.t[:, 0:384], [t, pts_free[w]])
                    b.rel = [a2]
                    out.append(a2)
                ss_free[w] = t
                return out

            def values(h, pp):
                w = h % 2
                b = sbank()
                g = h // 4
                mm(b.t[:, 0:T], VCN[0:15, g, :], PCT[0:15, h, :, :].rearrange("p a n -> p (a n)"), True, False,
                   [t_vcn, t_pct[h]] + b.rel, skip=True)
                for m in range(2):
                    mm(b.t[:, 0:T], NVT[:, m, 0, g * 128:(g + 1) * 128], PTS[:, w, m, 0:256], False, False,
                       [pp[m], t_v["vs", m, g]], skip=True)
                    t = mm(b.t[:, 128:T], NVT[:, m, 1, g * 128:(g + 1) * 128], PTS[:, w, m, 256:384], False, m == 1,
                           inc=(m == 1), skip=True)
                pts_free[w] = t
                hi = cp(AC, MNH[:, h, :], b.t[:, 0:T], [t])
                lo = tt(DV, MNL[:, h, :], b.t[:, 0:T], f32(MNH[:, h, :]), ALU.subtract, [hi])
                b.rel = [lo]
                MN.t[h] = [hi, lo]

            soft_t, turn_t = {}, {}
            for h in range(10):
                if h >= 2:
                    values(h - 2, turn_t[h - 2])
                bt = scores(h) if h < 8 else None
                if 1 <= h < 9:
                    turn_t[h - 1] = turnp(h - 1, soft_t[h - 1])
                if h < 8:
                    soft_t[h] = soft(h, bt)
                yield

        def side_second():
            yield from side_gla()
            yield from side_nsa()

        t_amask = load(AM[:, :], A["amask"], t_b1)
        side = side_second()
        run(main_second(side), side, 1.0)
        for _ in side:
            pass
        hn_free[0] = PE.last()
        f = norm_after("ffn")
        for n in range(16):
            residual(MN, range(8), [t_v["h", n]], n, f)

        out_tickets = []

        def store(n, a):
            s = out_sem[n % 4]
            SP.wait([a])
            SP.todo.append(lambda e, n=n, s=s: e.dma_start(out[:, n, :], XT[:, n, :]).then_inc(s, 16))
            out_tickets.append((s, 16 * (n // 4 + 1)))

        out_sem = [sem(f"s_out{i}") for i in range(4)]
        ffn(store)
        SP.wait(out_tickets[-4:])
        assert tile_at[0] == len(order) * RU, (tile_at[0], len(order) * RU)

        block = ctx.enter_context(nc.Block())

        @block.sync
        def _(e):
            SP.play(e)

        @block.gpsimd
        def _(e):
            GP.play(e)

        @block.scalar
        def _(e):
            AC.play(e)

        @block.vector
        def _(e):
            DV.play(e)

        @block.tensor
        def _(e):
            PE.play(e)


def tiles(w, kt=None):
    K, N = w.shape
    t = w.reshape(K // 128, 128, N // 128, 128).transpose(2, 0, 1, 3)
    return t.reshape(-1, 128, 128)


def pairs(w):
    K, N = w.shape
    return w.reshape(K // 128, 128, N // 256, 2, 128).transpose(2, 0, 3, 1, 4).reshape(-1, 128, 128)


def units(t):
    return np.ascontiguousarray(t.reshape(-1, RU, 128, 128).transpose(0, 2, 1, 3)).reshape(-1, 128, RU * 128)


def gated(w, b):
    ta = tiles(w).reshape(-1, w.shape[0] // 128, 128, 128)
    tb = tiles(b).reshape(-1, b.shape[0] // 128, 128, 128)
    return units(np.concatenate([ta, tb], axis=1).reshape(-1, 128, 128))


def down(w):
    t = tiles(w).reshape(16, 2, 22, 128, 128).transpose(1, 0, 2, 3, 4)
    return units(t.reshape(-1, 128, 128))


def padded(w):
    return np.pad(w, ((0, 0), (0, 128 - w.shape[1])))


def cols(v):
    return np.ascontiguousarray(v.reshape(-1, 128).T)


def consts():
    L = 256
    f = np.float64
    t = np.arange(L, dtype=f)[:, None]
    m = np.arange(L, dtype=f)[None, :]
    ang = 2.0 * np.pi * (m + 0.5) * t / 512.0
    C, S = np.cos(ang), np.sin(ang)
    c = {}
    c["df"] = np.stack([C, S]).reshape(2, 2, 128, L).transpose(2, 0, 1, 3).astype(np.float32)
    c["dg"] = np.stack([C.T / 256.0, -S.T / 256.0]).reshape(2, 2, 128, L).transpose(2, 0, 1, 3).astype(np.float32)
    tl = np.linspace(0.0, 1.0, L, dtype=np.float32)[:, None]
    om = (np.float32(2.0 * math.pi) * np.arange(L, dtype=np.float32) / np.float32(L)).astype(np.float32)
    fr = np.linspace(1e-4, 15, 16, dtype=np.float32)
    an = (om[:, None] * fr[None, :]).astype(np.float32).astype(f)
    z = np.concatenate([tl, np.cos(an), -np.sin(an)], axis=1).astype(np.float32)
    c["zt"] = np.ascontiguousarray(z.T)
    d = np.linspace(math.log(1e-2) / 1.5, math.log(1e-2) / 0.3, 1024, dtype=np.float32)
    win = np.exp((-tl * np.abs(d)[None, :]).astype(f)).astype(np.float32)
    wb = win.copy()
    wb[0] = 0.0
    w2 = np.stack([win, wb], axis=1).reshape(2, 128, 2, 4, 256)
    c["win"] = w2.transpose(3, 1, 0, 2, 4)
    p = np.arange(128)
    j = np.arange(L)
    mk = np.zeros((128, 2, 2, L), np.float32)
    for h in range(2):
        s = (h * 128 + p)[:, None]
        mk[:, 0, h] = np.where(s <= j[None, :], 0.0, NEG)
        mk[:, 1, h] = np.where(s >= j[None, :], 0.0, NEG)
    c["mmask"] = mk
    sel = np.zeros((4, 4, 128), np.float32)
    for h in range(4):
        sel[h, h] = 1.0
    c["sel4"] = sel
    lm = np.zeros((128, 7, 128), np.int32)
    s, q = p[:, None], p[None, :]
    for lv in range(7):
        w = 1 << lv
        lm[:, lv] = (s // (2 * w) == q // (2 * w)) & (s // w % 2 == 0) & (q // w % 2 == 1)
    c["lmask"] = lm
    r = np.ones((128, L), np.float32)
    r[:, ::64] = 0.0
    c["reset"] = r
    cm = np.zeros((128, 2, 2, 16), np.float32)
    for h in range(2):
        ok = (16 * np.arange(16)[None, :] + 31) <= (h * 128 + p)[:, None]
        cm[:, 0, h] = np.where(ok, 0.0, NEG)
        cm[:, 1, h] = ok
    c["cmask"] = cm
    am = np.zeros((128, 384), np.float32)
    dm = np.where(q <= s, 0.0, NEG)
    am[:, 0:128] = dm
    am[:, 256:384] = dm
    c["amask"] = am
    c["ident"] = np.eye(128, dtype=np.float32)
    return {k: np.ascontiguousarray(v) for k, v in c.items()}


def kernel(**inputs):
    import concourse.bacc as bacc
    from concourse.bass_utils import run_bass_kernel_spmd as launch

    x = {k: np.asarray(v) for k, v in inputs.items()}
    one = {k: (v[0] if k != "norm_f_w" else v) for k, v in x.items()}
    a = consts()
    w = one["w_in"]
    a["w_in_a"] = units(np.concatenate([tiles(w[:, 0:5120]), tiles(padded(w[:, 7168:7184])),
                                        pairs(w[:, 5120:6144]), tiles(w[:, 6144:7168])]))
    a["w_ga"] = gated(w[:, 7184:9232], one["w_branch_a"])
    a["w_gb"] = gated(w[:, 9232:11280], one["w_branch_b"])
    a["w_out"] = units(tiles(one["w_out"]))
    gu = one["w_gate_up"]
    a["w_gu"] = gated(gu[:, 0:5632], gu[:, 5632:])
    a["w_dn"] = down(one["w_down"])
    w = one["w_in_2"]
    a["w_in2"] = units(np.concatenate([tiles(m) for m in (
        w[:, 0:2048], padded(w[:, 2048:2064]), w[:, 2064:3088], w[:, 3088:4112], w[:, 4624:4880],
        w[:, 5136:5392], w[:, 4112:4624])] + [pairs(w[:, 4880:5136]), pairs(w[:, 5392:5648]),
                                              tiles(padded(w[:, 5648:5672]))]))
    a["w_cmp"] = units(np.concatenate([one["cmp_k_w1_2"].reshape(32, 128, 128),
                                       one["cmp_v_w1_2"].reshape(32, 128, 128)]))
    a["cmp_w2"] = np.ascontiguousarray(np.stack([one["cmp_k_w2_2"], one["cmp_v_w2_2"]], axis=1))
    a["posT"] = np.ascontiguousarray(np.stack([one["cmp_k_pos_2"].T, one["cmp_v_pos_2"].T], axis=1))
    w = one["w_out_2"]
    a["w_out2"] = units(np.concatenate([tiles(w[0:1024]), tiles(w[1024:2048])]))
    a["w_gu2"] = gated(one["w_gate_2"], one["w_up_2"])
    a["w_dn2"] = down(one["w_down_2"])
    a["filt_w1"] = np.ascontiguousarray(one["filt_w1"])
    a["filt_w2"] = np.ascontiguousarray(one["filt_w2"])
    a["filt_w3"] = np.ascontiguousarray(one["filt_w3"].reshape(64, 2, 2, 1024))
    a["gla_gate_w2"] = np.ascontiguousarray(one["gla_gate_w2_2"])
    a["xT"] = np.ascontiguousarray(x["x"][0].T.reshape(16, 128, 256).transpose(1, 0, 2))

    v = np.zeros((128, NVEC), np.float32)

    def put(name, m):
        n, k = VECS[name]
        v[0:m.shape[0], n:n + k] = m

    put("norm1", cols(one["norm1_w"]))
    put("norm2", cols(one["norm2_w"]))
    put("normf", cols(one["norm_f_w"]))
    put("attn", cols(one["attn_norm_g_2"]))
    put("ffn", cols(one["ffn_norm_g_2"]))
    for i in range(3):
        put(f"cw{i}", cols(one["conv_w"][i]))
    put("cb", cols(one["conv_b"]))
    put("hb", cols(one["hyena_bias"].reshape(-1)))
    for i in range(4):
        put(f"gw{i}", cols(one["gla_conv_w_2"][i]))
    put("gb", cols(one["gla_gate_b_2"]))
    put("gng", cols(one["gla_norm_g_2"]))
    put("qg", cols(one["nsa_q_norm_g_2"]))
    put("kcg", cols(one["nsa_kc_norm_g_2"]))
    put("ksg", cols(one["nsa_ks_norm_g_2"]))
    put("kwg", cols(one["nsa_kw_norm_g_2"]))
    put("f1", one["filt_freq1"].reshape(64, 1))
    put("b1", one["filt_b1"].reshape(64, 1))
    put("f2", one["filt_freq2"].reshape(64, 1))
    put("b2", one["filt_b2"].reshape(64, 1))
    put("gbias", one["mlstm_gate_bias"].reshape(16, 1))
    a["vecs"] = v

    nc = bacc.Bacc("TRN2", target_bir_lowering=False, num_devices=1)
    arrays, aps = {}, {}
    for k, m in a.items():
        arrays[f"in_{k}"] = m
        aps[k] = nc.dram_tensor(f"in_{k}", m.shape, mybir.dt.from_np(m.dtype), kind="ExternalInput").ap()
    out = nc.dram_tensor("out_x", (128, 16, 256), F32, kind="ExternalOutput").ap()
    build(nc, aps, out)
    r = launch(nc, [arrays], core_ids=[0])
    got = r.results[0]["out_x"]
    return np.ascontiguousarray(got.transpose(1, 0, 2).reshape(2048, 256).T).reshape(1, 256, 2048)
```

```python
from contextlib import ExitStack
import math

import numpy as np
import concourse.bass as bass
from concourse import mybir

F32 = mybir.dt.float32
F32R = mybir.dt.float32r
I32 = mybir.dt.int32
ALU = mybir.AluOpType
ACT = mybir.ActivationFunctionType
AX = mybir.AxisListType

T = 256
KB = 1024
NEG = -1.0e30
EPS = 1e-6
RU = 16
SU = 8
NRAW = 3
NSPL = 4
AHEAD = 4

VECS = {}


def vec_layout():
    n = 0
    for name, k in (("norm1", 16), ("norm2", 16), ("normf", 16), ("attn", 16), ("ffn", 16),
                    ("cw0", 40), ("cw1", 40), ("cw2", 40), ("cb", 40), ("hb", 16),
                    ("gw0", 16), ("gw1", 16), ("gw2", 16), ("gw3", 16), ("gb", 4), ("gng", 2),
                    ("qg", 1), ("kcg", 1), ("ksg", 1), ("kwg", 1),
                    ("f1", 1), ("b1", 1), ("f2", 1), ("b2", 1), ("gbias", 1), ("rowmask", 1)):
        VECS[name] = (n, k)
        n += k
    return n


NVEC = vec_layout()


class Engine:

    def __init__(self, sem):
        self.sem = sem
        self.n = 0
        self.todo = []
        self.seen = {}

    def wait(self, after):
        for t in after:
            if t is None:
                continue
            sem, value = t
            if self.seen.get(id(sem), 0) < value:
                self.seen[id(sem)] = value
                self.todo.append(lambda e, s=sem, v=value: e.wait_ge(s, v))

    def __call__(self, fn, after=(), chain=True, inc=True):
        if chain and self.n:
            self.wait([(self.sem, self.n)])
        self.wait(after)
        if inc:
            self.n += 1
            self.todo.append(lambda e, f=fn, s=self.sem: f(e).then_inc(s, 1))
            return (self.sem, self.n)
        self.todo.append(fn)
        return None

    def last(self):
        return (self.sem, self.n)

    def play(self, e):
        for f in self.todo:
            f(e)


class Bank:

    def __init__(self, t):
        self.t = t
        self.rel = []

    @property
    def rel(self):
        return self.free

    @rel.setter
    def rel(self, tickets):
        self.free = tickets
        self.taken = False

    def take(self):
        assert not self.taken
        self.taken = True
        return self


class Act:

    def __init__(self, hi, lo, kt):
        self.hi, self.lo = hi, lo
        self.t = [[] for _ in range(kt)]


NTMP = 4
RATES = (0.88, 0.97, 1.01, 2.2, 3.3, 1, 2.2)


def build(nc, A, out):
    ctx = ExitStack()
    with ctx:
        def sem(name):
            return ctx.enter_context(nc.semaphore(name))

        PE, AC, DV, GP, SP = (Engine(sem(f"s_{n}")) for n in ("pe", "act", "dve", "pool", "sp"))
        raw_sem = [sem(f"s_raw{i}") for i in range(NRAW)]

        base = (nc.sbuf_base + 31) // 32 * 32
        cur = [base]

        def at(name, shape, dt, off):
            return nc.alloc_sbuf_tensor_at(name, shape, dt, offset=off)

        def bump(name, shape, dt=F32):
            size = int(np.prod(shape[1:])) * 4
            t = at(name, shape, dt, cur[0])
            cur[0] += (size + 31) // 32 * 32
            return t

        RAW = bump("RAW", [128, NRAW, RU * 128])
        WH = bump("WH", [128, NSPL, SU * 128], F32R)
        WL = bump("WL", [128, NSPL, SU * 128], F32R)
        HNH = bump("HNH", [128, 16, T], F32R)
        HNL = bump("HNL", [128, 16, T], F32R)
        VEC = bump("VEC", [128, NVEC])
        ONES = bump("ONES", [128, 128])
        IDENT = bump("IDENT", [128, 128])
        TMP = bump("TMP", [128, NTMP, T])
        RSTD = bump("RSTD", [128, T])
        RF = bump("RF", [128, T])
        RTOK = bump("RTOK", [128, 2])
        SQA = bump("SQA", [128, 2, T])
        xt_off = cur[0]
        XT = bump("XT", [128, 16, T])
        arena = cur[0]
        limit = nc.sbuf_usable_end

        def ar(name, shape, kb, dt=F32):
            size = int(np.prod(shape[1:])) * 4
            off = arena + int(kb * KB)
            assert off + size <= limit, (name, off + size - limit)
            return at(name, shape, dt, off)

        banks = [Bank(nc.alloc_psum_tensor(f"PB{i}", [128, 512], F32)) for i in range(8)]
        mains = banks[0:3]
        sides = banks[3:8]
        turn = {"m": 0, "s": 0}

        def mbank():
            turn["m"] += 1
            return mains[turn["m"] % 3].take()

        def sbank():
            turn["s"] += 1
            return sides[turn["s"] % 5].take()

        def vec(name, j=0, p=128):
            n, k = VECS[name]
            assert j < k
            return VEC[0:p, n + j:n + j + 1]

        def tt(E, o, a, b, op, after=(), **k):
            return E(lambda e: e.tensor_tensor(o, a, b, op), after, **k)

        def ts(E, o, a, s1, s2, op0, op1=None, after=(), **k):
            if op1 is None:
                return E(lambda e: e.tensor_scalar(o, a, s1, None, op0), after, **k)
            return E(lambda e: e.tensor_scalar(o, a, s1, s2, op0, op1), after, **k)

        def stt(o, a, s, b, op0, op1, after=(), **k):
            return DV(lambda e: e.scalar_tensor_tensor(out=o, in0=a, scalar=s, in1=b, op0=op0, op1=op1),
                      after, **k)

        def cp(E, o, a, after=(), **k):
            if E is AC:
                return E(lambda e: e.activation(o, a, ACT.Copy), after, **k)
            return E(lambda e: e.tensor_copy(o, a), after, **k)

        def act(o, a, f, after=(), bias=None, scale=None, accum=None, **k):
            kw = {}
            if bias is not None:
                kw["bias"] = bias
            if scale is not None:
                kw["scale"] = scale
            if accum is not None:
                kw["accum_out"] = accum
            return AC(lambda e: e.activation(o, a, f, **kw), after, **k)

        def mm(o, l, r, start, stop, after=(), inc=False, skip=False):
            return PE(lambda e: e.matmul(o, l, r, start=start, stop=stop, skip_group_check=skip),
                      after, chain=False, inc=inc)

        def tr(o, a, ident, after=(), inc=False):
            return PE(lambda e: e.transpose(o, a, ident), after, chain=False, inc=inc)

        def recip(o, a, after=()):
            return DV(lambda e: e.reciprocal(o, a), after)

        def load(dst, src, after=()):
            s = sem(f"s_ld{len(loads)}")
            loads.append(s)
            SP.wait(after)
            SP.todo.append(lambda e: e.dma_start(dst, src).then_inc(s, 16))
            return (s, 16)

        loads = []

        def f32(ap):
            return ap.bitcast(F32)

        tmp_rel = [[] for _ in range(NTMP)]
        tmp_n = [0]

        def tmp():
            i = tmp_n[0] % NTMP
            tmp_n[0] += 1
            rel, tmp_rel[i] = tmp_rel[i], None
            assert rel is not None
            return i, TMP[:, i, :], rel

        def split(hi, lo, x, after=(), hi_after=()):
            a = cp(AC, hi, x, list(after) + list(hi_after))
            b = tt(DV, lo, x, f32(hi), ALU.subtract, list(after) + [a])
            return [a, b]

        def split_later(i, X, j, hi, lo, x, after=(), hi_after=()):
            a = cp(AC, hi, x, list(after) + list(hi_after))
            X.t[j] = None

            def low():
                X.t[j] = [a, tt(DV, lo, x, f32(hi), ALU.subtract, list(after) + [a])]
                if i is not None:
                    tmp_rel[i] = X.t[j]

            defer(low)

        order = []
        order += [("w_in_a", i) for i in range(57)]
        order += [("w_ga", i) for i in range(24)] + [("w_gb", i) for i in range(24)]
        order += [("w_out", i) for i in range(16)]
        for h in range(2):
            order += [("w_gu", 44 * h + i) for i in range(44)] + [("w_dn", 22 * h + i) for i in range(22)]
        order += [("w_in2", i) for i in range(37)] + [("w_cmp", i) for i in range(4)]
        order += [("w_in2", i) for i in range(37, 45)]
        order += [("w_out2", i) for i in range(16)]
        for h in range(2):
            order += [("w_gu2", 44 * h + i) for i in range(44)] + [("w_dn2", 22 * h + i) for i in range(22)]

        raw_used = {}
        unit_pe = {}
        unit_ready = {}
        issued = [0]
        splits = [0]
        tile_at = [0]

        def issue_raw(most=len(order)):
            while issued[0] < most and (issued[0] < NRAW or issued[0] - NRAW in raw_used):
                n = issued[0]
                name, i = order[n]
                slot = n % NRAW
                SP.wait(raw_used.get(n - NRAW, ()))
                SP.todo.append(lambda e, s=slot, src=A[name][i]: e.dma_start(RAW[:, s, :], src)
                               .then_inc(raw_sem[s], 16))
                issued[0] += 1

        def do_split():
            u = splits[0]
            if u * SU >= len(order) * RU:
                return
            splits[0] += 1
            n, half = divmod(u, RU // SU)
            if order[n][0] == "w_cmp":
                unit_ready[u] = (None, None)
                return
            slot, sp = n % NRAW, u % NSPL
            landed = (raw_sem[slot], 16 * (n // NRAW + 1))
            src = RAW[:, slot, half * SU * 128:(half + 1) * SU * 128]
            free = [unit_pe.get(u - NSPL)]
            h = cp(AC, WH[:, sp, :], src, [landed] + free, chain=False)
            E = GP if u % 2 and u > 7 else DV
            unit_ready[u] = None

            def low():
                lo = tt(E, WL[:, sp, :], src, f32(WH[:, sp, :]), ALU.subtract, [h], chain=False)
                unit_ready[u] = (lo, lo)
                if half == RU // SU - 1:
                    raw_used[n] = [lo, unit_ready[u - 1][1]]
                    issue_raw()

            defer(low, lows)

        def tile():
            i = tile_at[0]
            tile_at[0] += 1
            u, r = divmod(i, SU)
            if r == 0:
                while splits[0] <= u + AHEAD - 1 and splits[0] * SU < len(order) * RU:
                    do_split()
            while unit_ready[u] is None:
                step()
            sl = u % NSPL
            return (WH, sl, r), (WL, sl, r), unit_ready[u][0], unit_ready[u][1], u if r == SU - 1 else None

        def one(which):
            X, sl, r = which
            return X[:, sl, r * 128:(r + 1) * 128]

        def raw_product(o, x, l, t_x, first, last, after):
            i = tile_at[0]
            tile()
            n, r = divmod(i, RU)
            slot = n % NRAW
            landed = (raw_sem[slot], 16 * (n // NRAW + 1))
            end = r == RU - 1
            t = mm(o, x[:, l, :], RAW[:, slot, r * 128:(r + 1) * 128], first, last, list(after) + t_x + [landed],
                   inc=last or end)
            if end:
                raw_used[n] = [t]
                issue_raw()
            return t

        def mm3(o, x, k, first, last, after=(), n=slice(0, T), skip=False):
            assert x.t[k]
            h, l, th, tl, end = tile()
            h, l = one(h), one(l)
            mm(o, h, x.hi[:, k, n], first, False, list(after) + x.t[k] + [th], skip=skip)
            mm(o, h, x.lo[:, k, n], False, False, skip=skip)
            t = mm(o, l, x.hi[:, k, n], False, last, [tl], inc=last or end is not None, skip=skip)
            if end is not None:
                unit_pe[end] = t
            if pump[0] and not last:
                pump[0]()
            return t

        pump = [None]
        later = []
        lows = []

        def defer(f, to=later):
            if pump[0]:
                to.append(f)
            else:
                f()

        def step():
            (lows or later).pop(0)()

        def flush():
            while lows or later:
                step()

        def ntile(o, x, ks, after, halfway=None):
            t = None
            for i, k in enumerate(ks):
                if halfway and i == 8:
                    halfway()
                t = mm3(o, x, k, i == 0, i == len(ks) - 1, after if i == 0 else ())
            return t

        def npair_tok(x):
            bank = mbank()
            t = None
            for k in range(16):
                h, l, th, tl, _ = tile()
                _, _, _, _, end = tile()
                h, l = wide(h), wide(l)
                for c in range(2):
                    o = bank.t[:, c * T:(c + 1) * T]
                    s = slice(c * 128, (c + 1) * 128)
                    mm(o, x.hi[:, k, s], h, k == 0 and c == 0, False,
                       (bank.rel if k == 0 else []) + x.t[k] + [th], skip=True)
                    mm(o, x.lo[:, k, s], h, False, False, skip=True)
                    t = mm(o, x.hi[:, k, s], l, False, k == 15 and c == 1, [tl],
                           inc=(c == 1 and (k == 15 or end is not None)), skip=True)
                if end is not None:
                    unit_pe[end] = t
                if pump[0]:
                    pump[0]()
                    pump[0]()
            return bank, t

        def wide(which):
            X, sl, r = which
            return X[:, sl, r * 128:(r + 2) * 128]

        L = {}
        L["vec"] = load(VEC[:, :], A["vecs"])
        L["xT"] = [load(XT[:, 0:4, :], A["xT"][:, 0:4, :])]
        issue_raw(1)
        L["xT"] += [load(XT[:, 4 * i:4 * i + 4, :], A["xT"][:, 4 * i:4 * i + 4, :]) for i in range(1, 4)]
        issue_raw()
        L["ident"] = load(IDENT[:, :], A["ident"])
        t_ones = GP(lambda e: e.memset(ONES[:, :], 1.0))

        HN = Act(HNH, HNL, 16)

        sq_rel = [[], []]

        def add_sq(x, k, which=0, after=(), E=GP):
            acc = SQA[:, which, :]
            if k == 0:
                a = act(acc, x, ACT.Square, list(after) + sq_rel[which])
                sq_rel[which] = [a]
                return
            i, s, rel = tmp()
            a = act(s, x, ACT.Square, list(after) + rel)
            t = tt(E, acc, acc, s, ALU.add, [a] + sq_rel[which])
            tmp_rel[i] = [t]
            sq_rel[which] = [t]

        def sum_sq(*which):
            b = sbank()
            for w in which:
                t = mm(b.t[:, 0:T], ONES[:, :], SQA[:, w, :], w == which[0], w == which[-1],
                       sq_rel[w] + [t_ones] + b.rel, inc=True)
                sq_rel[w] = [t]
            return b, t

        def make_hn(x, k, g, after=(), free=(), chain=True):
            a = act(HNH[:, k, :], x, ACT.Copy, list(after) + list(free), scale=g, chain=chain)
            b = stt(HNL[:, k, :], x, g, f32(HNH[:, k, :]), ALU.mult, ALU.subtract, list(after) + [a], chain=chain)
            HN.t[k] = [a, b]

        def rsqrt_mean(dst, src, width, after=()):
            a = act(dst, src, ACT.Sqrt, after, bias=EPSC[:, 0:1], scale=1.0 / width)
            return recip(dst, dst, [a]), a

        EPSC = at("EPSC", [128, 8], F32, arena)
        GP(lambda e: e.memset(EPSC[:, 0:1], EPS))
        t_eps = GP(lambda e: e.memset(EPSC[:, 1:2], 128.0 * EPS))
        arena = arena + 32

        def rstd_tok(bank):
            mm(bank.t[:, 0:1], RSTD[0:1, 0:128], ONES[0:1, 0:1], True, True, [t_rstd[0], t_ones] + bank.rel)
            t = mm(bank.t[:, 1:2], RSTD[0:1, 128:256], ONES[0:1, 0:1], True, True, inc=True)
            e = cp(DV, RTOK[:, :], bank.t[:, 0:2], [t])
            bank.rel = [e]
            return e

        t_rstd = [None]
        t_rtok = [None]

        for k in range(16):
            if k in (4, 8):
                do_split()
            make_hn(XT[:, k, :], k, vec("norm1", k), [L["xT"][k // 4], L["vec"]], chain=False)
        t_x1 = []

        def first_norm():
            for k in range(16):
                defer(lambda k=k: add_sq(XT[:, k, :], k // 2, k % 2, (), (GP, DV)[k % 2]))

        def first_rstd():
            flush()
            t_x1.extend([AC.last(), DV.last()])
            finish_rstd(0, 1)

        def finish_rstd(*which):
            b, t = sum_sq(*which)
            t_rstd[0], r = rsqrt_mean(RSTD[:, :], b.t[:, 0:T], 2048.0, [t, t_eps, DV.last()])
            b.rel = [r]

        DF = ar("DF", [128, 2, 2, 128], 0)
        DG = ar("DG", [128, 2, 2, 128], 2)
        KT = ar("KT", [128, 2, 2, T], 4)
        UP = ar("UP", [128, 2, 2, T], 81)
        V = ar("V", [128, 8, T], 8)
        X1 = ar("X1", [128, 8, T], 16)
        YAH = ar("YAH", [128, 8, T], 8, F32R)
        YAL = ar("YAL", [128, 8, T], 16, F32R)
        X2 = ar("X2", [128, 8, T], 24)
        WIN = ar("WIN", [128, 2, 2, T], 32)
        W3 = ar("W3", [64, 2, T], 36)
        FW = ar("FW", [128, 2, 2, T], 38)
        HSD = ar("HSD", [128, 2, 2, T], 42)
        KS = ar("KSP", [128, 2, 2, T], 46)
        M1 = ar("M1", [128, 2, T], 50)
        Y = ar("Y", [128, 2, 2, T], 52)
        UT = ar("UT", [128, 2, 2, 128], 56)
        H2 = ar("H2", [64, T], 58)
        ZT = ar("ZT", [33, T], 59)
        FW1 = ar("FW1", [64, 128], 60)
        HA = ar("HA", [64, 3, T], 61)
        VT = ar("VT", [128, 2, 1024], 64)
        O = ar("O", [128, 8, T], 72)
        G16 = ar("G16", [16, T], 80)
        QK = at("QK", [128, 16, T], F32, xt_off)

        L["df"] = load(DF[:, :, :, :], A["df"])
        L["dg"] = load(DG[:, :, :, :], A["dg"])
        L["zt"] = load(ZT[:, :], A["zt"])
        L["fw1"] = load(FW1[0:33, 0:64], A["filt_w1"])
        L["fw2"] = load(FW1[0:64, 64:128], A["filt_w2"])

        t_v = {}

        def scaled(bank, t, w=T):
            i, s, rel = tmp()
            a = tt(DV, s[:, 0:w], bank.t[:, 0:w], RSTD[:, 0:w], ALU.mult, [t, t_rstd[0]] + rel)
            bank.rel = [a]
            return i, s, a

        def conv3(dst, j):
            b = mbank()
            t = ntile(b.t[:, 0:T], HN, range(16), b.rel)
            return conv3_end(dst, j, b, t)

        def conv3_end(dst, j, b, t):
            i, s, a = scaled(b, t)
            c = ts(DV, dst, s, vec("cw1", j), vec("cb", j), ALU.mult, ALU.add, [a, L["vec"]])
            d = stt(dst[:, 1:T], s[:, 0:T - 1], vec("cw0", j), dst[:, 1:T], ALU.mult, ALU.add, [c])
            d = stt(dst[:, 0:T - 1], s[:, 1:T], vec("cw2", j), dst[:, 0:T - 1], ALU.mult, ALU.add, [d])
            tmp_rel[i] = [d, c]
            return d

        def main_hyena():
            for j in range(24):
                dst = (V, X1, X2)[j // 8][:, j % 8, :]
                if j == 0:
                    b0 = mbank()
                    t0 = ntile(b0.t[:, 0:T], HN, range(16), b0.rel)
                    first_norm()
                    b1 = mbank()
                    t1 = ntile(b1.t[:, 0:T], HN, range(16), b1.rel)
                    b2 = mbank()
                    t2 = ntile(b2.t[:, 0:T], HN, range(16), b2.rel)
                    b3 = sbank()
                    t3 = ntile(b3.t[:, 0:T], HN, range(16), b3.rel, first_rstd)
                    t_v[0] = conv3_end(dst, 0, b0, t0)
                    yield
                elif j == 1:
                    t_v[1] = conv3_end(dst, 1, b1, t1)
                elif j == 2:
                    t_v[2] = conv3_end(dst, 2, b2, t2)
                elif j == 3:
                    t_v[3] = conv3_end(dst, 3, b3, t3)
                    yield
                else:
                    t_v[j] = conv3(dst, j)
                    if j == 6:
                        t_rtok[0] = rstd_tok(sbank())
                    yield

        def sine(dst, src, P, after):
            k, r = HA[0:P, 1, :], HA[0:P, 2, :]
            magic = 12582912.0
            a = ts(DV, k, src, 1.0 / (2.0 * math.pi), magic, ALU.mult, ALU.add, after)
            a = ts(DV, k, k, magic, None, ALU.subtract)
            c1 = 6.28125
            c2 = float(np.float32(2.0 * math.pi - c1).view(np.uint32) & 0xFFFFF000)
            c2 = float(np.array(int(c2), np.uint32).view(np.float32))
            c3 = 2.0 * math.pi - c1 - c2
            stt(r, k, -c1, src, ALU.mult, ALU.add)
            stt(r, k, -c2, r, ALU.mult, ALU.add)
            stt(r, k, -c3, r, ALU.mult, ALU.add)
            a = ts(DV, r, r, 3.1415925, -3.1415925, ALU.min, ALU.max)
            return act(dst, r, ACT.Sin, [a])

        def side_hyena_all():
            yield from side_filter()
            yield from side_hyena()

        def side_filter():
            b = sbank()
            t = mm(b.t[0:64, 0:T], FW1[0:33, 0:64], ZT[:, :], True, True, [L["fw1"], L["zt"]] + b.rel, inc=True)
            a = ts(DV, HA[:, 0, :], b.t[0:64, 0:T], vec("b1", 0, 64), vec("f1", 0, 64), ALU.add, ALU.mult,
                   [t, L["vec"]])
            b.rel = [a]
            s = sine(H2[:, :], HA[:, 0, :], 64, [a])
            yield
            b = sbank()
            t = mm(b.t[0:64, 0:T], FW1[0:64, 64:128], H2[:, :], True, True, [L["fw2"], s] + b.rel, inc=True)
            a = ts(DV, HA[:, 0, :], b.t[0:64, 0:T], vec("b2", 0, 64), vec("f2", 0, 64), ALU.add, ALU.mult,
                   [t, L["vec"]])
            b.rel = [a]
            t_v["h2"] = sine(H2[:, :], HA[:, 0, :], 64, [a])
            yield

        hy = {}

        def hyena_loads(o, qt, win_free, w3_free):
            hy["next"] = (load(WIN[:, :, :, :], A["win"][qt], win_free),
                          load(W3[:, :, :], A["filt_w3"][:, o, :, qt * 256:(qt + 1) * 256], w3_free))

        hyena_loads(0, 0, [], [])

        def flat2(x):
            return x.rearrange("p a n -> p (a n)")

        def flat4(x):
            return x[:, :, :, :].rearrange("p a b n -> p (a b n)")

        def side_hyena():
            t_kt = t_pr = t_um = t_z = t_inv = None
            fl = {"free": [], "ks": None}

            def filters(o, qt):
                t_win, t_w3 = hy["next"]
                for c in range(2):
                    b = sbank()
                    t = mm(b.t[:, :], H2[:, c * 128:(c + 1) * 128],
                           W3[:, :, :].rearrange("p a n -> p (a n)"), True, True,
                           [t_v["h2"], t_w3] + b.rel, inc=True)
                    w3_free = [t]
                    a = tt(DV, FW[:, c, :, :].rearrange("p a n -> p (a n)"), b.t[:, :],
                           WIN[:, c, :, :].rearrange("p a n -> p (a n)"), ALU.mult,
                           [t, t_win] + fl["free"])
                    b.rel = [a]
                    win_free = [a]
                    tt(GP, HSD[:, 0, c, :], FW[:, c, 0, :], FW[:, c, 1, :], ALU.add, [a, fl["ks"]])
                    t_hsd = tt(GP, HSD[:, 1, c, :], FW[:, c, 1, :], FW[:, c, 0, :], ALU.subtract)
                fl["free"] = [t_hsd]
                if (o, qt) != (1, 3):
                    hyena_loads(*divmod(o * 4 + qt + 1, 4), win_free, w3_free)
                fl["hsd"] = t_hsd
                yield

            yield from filters(0, 0)
            for o in range(2):
                for qt in range(4):
                    b = sbank()
                    for ct in range(2):
                        for c in range(2):
                            ua = tr(b.t[:, (c * 2 + ct) * 128:(c * 2 + ct + 1) * 128],
                                    V[:, 2 * qt + ct, :].rearrange("p (t a) -> p a t", a=2)[:, c, :], IDENT[:, :],
                                    [t_v[2 * qt + ct], L["ident"]] + b.rel, inc=(c == 1))
                    t_ut = cp(AC, flat4(UT), b.t[:, :], [ua, t_um])
                    b.rel = [t_ut]
                    for c in range(2):
                        b = sbank()
                        for ri in range(2):
                            t = mm(b.t[:, ri * 256:(ri + 1) * 256], DF[:, c, ri, :], HSD[:, ri, c, :], True, True,
                                   [fl["hsd"], L["df"]] + b.rel, inc=(ri == 1))
                        a = cp(AC, flat2(KT[:, c, :, :]), b.t[:, :], [t, t_kt])
                        b.rel = [a]
                    fl["ks"] = t
                    tt(GP, flat2(KS[:, 0, :, :]), flat2(KT[:, 0, :, :]), flat2(KT[:, 1, :, :]), ALU.add, [a, t_pr])
                    t_kt = tt(GP, flat2(KS[:, 1, :, :]), flat2(KT[:, 0, :, :]), flat2(KT[:, 1, :, :]), ALU.subtract)
                    yield
                    bu = [sbank(), sbank()]
                    for c in range(2):
                        for ri in range(2):
                            t_um = mm(bu[c].t[:, ri * 256:(ri + 1) * 256], DF[:, c, ri, :], flat2(UT[:, c, :, :]),
                                      True, True, [t_ut, L["df"]] + bu[c].rel, inc=(ri == 1))
                        if c == 0:
                            e = cp(AC, flat2(KT[:, 0, :, :]), bu[0].t[:, :], [t_um, t_kt])
                            bu[0].rel = [e]
                    tt(DV, flat2(UP[:, 0, :, :]), flat2(KT[:, 0, :, :]), bu[1].t[:, :], ALU.add, [e, t_um, t_inv])
                    a = tt(DV, flat2(UP[:, 1, :, :]), flat2(KT[:, 0, :, :]), bu[1].t[:, :], ALU.subtract)
                    bu[1].rel = [a]
                    yield
                    for f in range(2):
                        tt(DV, flat2(M1), flat2(UP[:, f, :, :]), flat2(KS[:, f, :, :]), ALU.mult, [t_kt, t_z])
                        tt(DV, Y[:, f, 0, :], M1[:, 0, :], M1[:, 1, :], ALU.add)
                        tt(DV, M1[:, 0, :], UP[:, f, 0, :], KS[:, f, 1, :], ALU.mult)
                        t_pr = tt(DV, M1[:, 1, :], UP[:, f, 1, :], KS[:, f, 0, :], ALU.mult)
                        t_y = tt(DV, Y[:, f, 1, :], M1[:, 0, :], M1[:, 1, :], ALU.subtract)
                    t_kt = t_pr
                    tt(GP, flat2(UP[:, 0, :, :]), flat2(Y[:, 0, :, :]), flat2(Y[:, 1, :, :]), ALU.add, [t_y])
                    t_z = tt(GP, flat2(UP[:, 1, :, :]), flat2(Y[:, 0, :, :]), flat2(Y[:, 1, :, :]), ALU.subtract)
                    yield
                    if (o, qt) != (1, 3):
                        yield from filters(*divmod(o * 4 + qt + 1, 4))
                    b = sbank()
                    for ct in range(2):
                        for c in range(2):
                            for ri in range(2):
                                k = ct * 256 + c * 128
                                t = mm(b.t[:, k:k + 128], UP[:, c, ri, ct * 128:(ct + 1) * 128],
                                       DG[:, ri, c, :], ri == 0, ri == 1, [t_z, L["dg"]] + b.rel,
                                       inc=(c == 1 and ri == 1))
                    t_inv = t

                    def times(x):
                        return x.rearrange("p (t a) -> p a t", a=2)

                    for ct in range(2):
                        j = 2 * qt + ct
                        i, s, rel = tmp()
                        s2 = s.rearrange("p (a t) -> p a t", a=2)
                        a = stt(s2, times(V[:, j, :]), vec("hb", o * 8 + j),
                                b.t[:, ct * 256:(ct + 1) * 256].rearrange("p (a t) -> p a t", a=2),
                                ALU.mult, ALU.add, [t] + rel)
                        if ct == 1:
                            b.rel = [a]
                        if o == 0:
                            t_v[j] = tt(DV, times(V[:, j, :]), s2, times(X1[:, j, :]), ALU.mult, [t_v[8 + j], a])
                            tmp_rel[i] = [t_v[j]]
                        else:
                            z = tt(DV, times(X2[:, j, :]), s2, times(X2[:, j, :]), ALU.mult, [t_v[16 + j], a])
                            tmp_rel[i] = [z]
                            split_later(None, YA, j, YAH[:, j, :], YAL[:, j, :], X2[:, j, :], [z])
                    yield

        YA = Act(YAH, YAL, 8)

        def silu_conv(dst, j, key):
            b = mbank()
            t = ntile(b.t[:, 0:T], HN, range(16), b.rel)
            i, s, rel = tmp()
            DV.wait(rel)
            t = conv3_end(s, j, b, t)

            def silu():
                a = act(dst, s, ACT.Silu, [t] + t_x1)
                tmp_rel[i] = [a]
                t_v[key] = a

            defer(silu)

        def main_qkvo():
            for j in range(16):
                silu_conv(QK[:, j, :], 24 + j, ("qk", j))
                yield
            b = mbank()
            t = ntile(b.t[:, 0:T], HN, range(16), b.rel)
            i, s, a = scaled(b, t)
            t_v["g"] = ts(DV, G16[:, :], s[0:16, :], vec("gbias", 0, 16), None, ALU.add)
            tmp_rel[i] = [t_v["g"]]
            yield
            for j in range(4):
                b, t = npair_tok(HN)
                for c in range(2):
                    a = act(VT[:, c, j * 256:(j + 1) * 256], b.t[:, c * T:(c + 1) * T], ACT.Copy,
                            [t, t_rtok[0]], scale=RTOK[:, c:c + 1])
                b.rel = [a]
                t_v["vt", 2 * j] = t_v["vt", 2 * j + 1] = a
                yield
                yield
            for j in range(8):
                b = mbank()
                t = ntile(b.t[:, 0:T], HN, range(16), b.rel)
                i, s, a = scaled(b, t)

                def sigmoid(j=j, i=i, s=s, a=a):
                    t_v["o", j] = act(O[:, j, :], s, ACT.Sigmoid, [a])
                    tmp_rel[i] = [t_v["o", j]]

                defer(sigmoid)
                yield
        speed = [1.0]

        def run(main, side, rate=1.0, skip=0):
            state = [-skip * rate, 0]

            def after_tile():
                state[1] += 1
                if state[1] % DEF == 0 and (lows or later):
                    step()
                state[0] += rate * speed[0] / 16.0
                if state[0] >= 1.0:
                    state[0] -= 1.0
                    next(side, None)

            pump[0] = after_tile
            for _ in main:
                pass
            flush()
            pump[0] = None

        RH, RQ, RA, RG, RN, DEF, RO = RATES
        side = side_hyena_all()
        run(main_hyena(), side, RH, 7)
        run(main_qkvo(), side, RQ)
        for _ in side:
            pass
        t_hy = [DV.last(), AC.last(), PE.last(), GP.last()]

        MIX = ar("MIX", [128, 16, T], 24)
        MSK = ar("MSK", [128, 2, 2, T], 40)
        WW = ar("WW", [128, 2, 2, T], 44)
        PP = ar("PP", [128, 2, 2, T], 48)
        EMB = ar("EMB", [128, 2, T], 52)
        RR = ar("RR", [128, 2, T], 54)
        ROWS = ar("ROWS", [4, 4, 2, T], 56)
        SEL = ar("SEL", [4, 4, 128], 81)
        NN = ar("NN", [128, 2, T], 83)
        GTT = ar("GTT", [128, 4, 4], 85)
        YBH = ar("YBH", [128, 8, T], 0, F32R)
        YBL = ar("YBL", [128, 8, T], 72, F32R)
        YB = Act(YBH, YBL, 8)

        def side_mlstm():
            t_msk = load(MSK[:, :, :, :], A["mmask"], t_hy)
            t_sel = load(SEL[:, :, :], A["sel4"], t_hy)
            a = t_v["g"]
            bi, bf = sbank(), sbank()
            for d in range(2):
                mm(bi.t[0:4, d * T:(d + 1) * T], IDENT[0:16, 8 * d:8 * d + 4], G16[:, :], True, True, [a] + bi.rel)
            for d in range(2):
                t = mm(bf.t[0:4, d * T:(d + 1) * T], IDENT[0:16, 8 * d + 4:8 * d + 8], G16[:, :], True, True,
                       bf.rel, inc=True)
            r = [ROWS[:, i, :, :] for i in range(4)]
            fl = [ROWS[:, i, :, :].rearrange("p a n -> p (a n)") for i in range(4)]
            a = cp(AC, fl[3], bf.t[0:4, :], [t])
            a = stt(fl[0], fl[3], -1.0, fl[3], ALU.mult, ALU.max, [a])
            a = act(fl[0], fl[0], ACT.Exp, [a], scale=-1.0)
            a = act(fl[0], fl[0], ACT.Ln, [a], bias=1.0)
            a = stt(fl[0], fl[3], 0.0, fl[0], ALU.min, ALU.subtract, [a])
            bf.rel = [a]
            yield
            on = ONES[0:4, 0:1].broadcast_to([4, T])
            for d in range(2):
                x = r[0][:, d, :] if d == 0 else r[0][:, d, ::-1]
                y = r[1][:, d, :] if d == 0 else r[1][:, d, ::-1]
                a = DV(lambda e, x=x, y=y: e.tensor_tensor_scan(y, on, x, 0.0, ALU.mult, ALU.add), [t_ones])
            a = tt(DV, fl[2], bi.t[0:4, :], fl[1], ALU.subtract)
            bi.rel = [a]
            yield
            for d in range(2):
                x = r[2][:, d, :] if d == 0 else r[2][:, d, ::-1]
                y = r[3][:, d, :] if d == 0 else r[3][:, d, ::-1]
                a = DV(lambda e, x=x, y=y: e.tensor_tensor_scan(y, x, x, 0.0, ALU.max, ALU.max))
            a = tt(DV, fl[0], fl[1], fl[3], ALU.add)
            t_em = act(fl[0], fl[0], ACT.Exp, [a], scale=-1.0)
            a = ts(DV, fl[3], fl[3], -1.0, None, ALU.mult, None, [t_em])
            t_nm = a
            yield
            b = sbank()
            for d in range(2):
                for c in range(2):
                    j = d * 2 + c
                    t = mm(b.t[:, 4 * j:4 * j + 4], r[2][:, d, c * 128:(c + 1) * 128], IDENT[0:4, 0:4], True, True,
                           [t_nm] + b.rel, inc=True)
            t_gtt = cp(DV, GTT[:, :, :].rearrange("p a b -> p (a b)"), b.t[:, 0:16], [t])
            b.rel = [t_gtt]
            yield
            def finish(h, nb, t_u):
                for v in range(2):
                    i, s, rel = tmp()
                    a = tt(DV, NN[:, v, :], nb[0].t[:, v * T:(v + 1) * T], RR[:, 0, :], ALU.mult, [t_u])
                    a = tt(DV, s, nb[1].t[:, v * T:(v + 1) * T], RR[:, 1, :], ALU.mult, rel)
                    tt(DV, s, s, NN[:, v, :], ALU.add)
                    j = 2 * h + v
                    z = tt(DV, s, s, O[:, j, :], ALU.mult, [t_v["o", j]])
                    split_later(i, YB, j, YBH[:, j, :], YBL[:, j, :], s, [z])
                nb[0].rel = nb[1].rel = [z]

            pe_last = None
            held = None
            t_rr = None
            for h in range(4):
                bs, bn, be = sbank(), sbank(), sbank()
                for c in range(2):
                    for k in range(2):
                        q, kk = QK[:, 2 * h + k, :], QK[:, 8 + 2 * h + k, c * 128:(c + 1) * 128]
                        t_s = mm(bs.t[:, c * T:(c + 1) * T], kk, q, k == 0, k == 1,
                                 [t_v["qk", 2 * h + k], t_v["qk", 8 + 2 * h + k]] + bs.rel, inc=(k == 1))
                t_n = mm(bn.t[:, :], SEL[:, h, :], fl[3], True, True, [t_nm, t_sel] + bn.rel, inc=True)
                t_e = mm(be.t[:, :], SEL[:, h, :], fl[0], True, True, [t_em] + be.rel, inc=True)
                t_emb = cp(AC, EMB[:, :, :].rearrange("p a n -> p (a n)"), be.t[:, :], [t_e, t_rr])
                be.rel = [t_emb]
                for d in range(2):
                    for c in range(2):
                        a = stt(WW[:, d, c, :], bn.t[:, d * T:(d + 1) * T], GTT[:, d * 2 + c, h:h + 1],
                                MSK[:, d, c, :], ALU.add, ALU.min, [t_n, t_gtt, t_msk])
                bn.rel = [a]
                a = act(WW[:, :, :, :].rearrange("p a b n -> p (a b n)"),
                        WW[:, :, :, :].rearrange("p a b n -> p (a b n)"), ACT.Exp, [a])
                if held:
                    finish(*held)
                yield
                for d in range(2):
                    p = stt(PP[:, d, :, :].rearrange("p b n -> p (b n)"), bs.t[:, :], 1.0 / 16.0,
                            WW[:, d, :, :].rearrange("p b n -> p (b n)"), ALU.mult, ALU.mult, [t_s, a, pe_last])
                bs.rel = [p]
                yield
                bd = sbank()
                nb = [sbank(), sbank()]
                for d in range(2):
                    cs = (0, 1) if d == 0 else (1, 0)
                    for n, c in enumerate(cs):
                        sl = slice(0, T) if n == 0 else (slice(128, T) if d == 0 else slice(0, 128))
                        o0 = d * T
                        t_d = mm(bd.t[:, o0 + sl.start:o0 + sl.stop], ONES[:, :], PP[:, d, c, sl],
                                 n == 0, n == 1, [p] + bd.rel, inc=(n == 1), skip=True)
                for d in range(2):
                    cs = (0, 1) if d == 0 else (1, 0)
                    for v in range(2):
                        for n, c in enumerate(cs):
                            sl = slice(0, T) if n == 0 else (slice(128, T) if d == 0 else slice(0, 128))
                            t_u = mm(nb[d].t[:, v * T + sl.start:v * T + sl.stop],
                                     VT[:, c, h * 256 + v * 128:h * 256 + (v + 1) * 128], PP[:, d, c, sl],
                                     n == 0, n == 1, [t_v["vt", 2 * h + v]] + nb[d].rel,
                                     inc=(n == 1), skip=True)
                pe_last = t_u
                rr = RR[:, :, :].rearrange("p a n -> p (a n)")
                tt(DV, rr, bd.t[:, :], EMB[:, :, :].rearrange("p a n -> p (a n)"), ALU.max, [t_d])
                a = stt(rr, bd.t[:, :], -1.0, rr, ALU.mult, ALU.max)
                t_rr = a
                bd.rel = [a]
                yield
                for d in range(2):
                    a = recip(RR[:, d, :], RR[:, d, :])
                held = (h, nb, t_u)
                yield
            finish(*held)
            yield

        def branch(x, first):
            for n in range(16):
                b = mbank()
                ntile(b.t[:, 0:T], HN, range(16), b.rel)
                yield
                t2 = ntile(b.t[:, T:2 * T], x, range(8), [])
                i, s, a = scaled(b, t2)
                if first:
                    g = []
                    defer(lambda g=g, s=s, a=a: g.append(act(s, s, ACT.Sigmoid, [a])))

                    def product(n=n, b=b, i=i, s=s, a=a, t2=t2, g=g):
                        z = tt(DV, MIX[:, n, :], s, b.t[:, T:2 * T], ALU.mult, g + [t2] + t_hy)
                        tmp_rel[i] = [z]
                        b.rel = [a, z]

                    defer(product)
                    yield
                    continue
                g = act(s, s, ACT.Sigmoid, [a])
                z = tt(DV, s, s, b.t[:, T:2 * T], ALU.mult, [g, t2])
                b.rel = [a, z]
                z = tt(DV, s, s, MIX[:, n, :], ALU.add)
                MX.t[n] = split(MXH[:, n, :], MXL[:, n, :], s, [z], t_ml)
                tmp_rel[i] = MX.t[n]
                yield

        side = side_mlstm()
        run(branch(YA, True), side, RA)
        for _ in side:
            pass
        t_ml = [DV.last(), AC.last(), PE.last()]
        t_xt = [load(XT[:, 4 * i:4 * i + 4, :], A["xT"][:, 4 * i:4 * i + 4, :], t_ml) for i in range(4)]
        MXH = ar("MXH", [128, 16, T], 8, F32R)
        MXL = ar("MXL", [128, 16, T], 44, F32R)
        MX = Act(MXH, MXL, 16)
        for _ in branch(YB, False):
            pass

        def residual(x, ks, bank_after, n, finish):
            b = mbank()
            t = ntile(b.t[:, 0:T], x, ks, b.rel)
            a = tt(DV, XT[:, n, :], b.t[:, 0:T], XT[:, n, :], ALU.add, [t] + bank_after)
            b.rel = [a]
            if finish:
                finish(n, a)

        def norm_after(gname):
            def f(n, a):
                make_hn(XT[:, n, :], n, vec(gname, n), [a], [hn_free[0]])
                add_sq(XT[:, n, :], n, 0, [a])
            return f

        hn_free = [None]

        hn_free[0] = PE.last()
        f = norm_after("norm2")
        for n in range(16):
            residual(MX, range(16), [t_xt[n // 4]], n, f)

        HDH = ar("HDH", [128, 22, T], 0, F32R)
        HDL = ar("HDL", [128, 22, T], 22, F32R)
        HD = Act(HDH, HDL, 22)
        SG = ar("SG", [128, 2, T], 44)

        def ffn(finish):
            used = [PE.last(), DV.last(), AC.last()]
            for half in range(2):
                for j in range(22):
                    b = mbank()
                    ntile(b.t[:, 0:T], HN, range(16), b.rel)
                    if half == 0 and j == 0:
                        finish_rstd(0)
                    t = ntile(b.t[:, T:2 * T], HN, range(16), [])
                    i, s, a = scaled(b, t)
                    sg = SG[:, j % 2, :]
                    g = act(sg, s, ACT.Silu, [a] + used)
                    z = tt(DV, s, b.t[:, T:2 * T], RSTD[:, :], ALU.mult, [g])
                    b.rel = [z]
                    z = tt(DV, s, s, sg, ALU.mult)
                    HD.t[j] = split(HDH[:, j, :], HDL[:, j, :], s, [z], used)
                    tmp_rel[i] = HD.t[j]
                hn_free[0] = PE.last()
                for n in range(16):
                    residual(HD, range(22), [], n, finish if half else None)
                used = [PE.last()]

        def x_two_norms(n, a):
            add_sq(XT[:, n, :], n, 0, [a])
            b = ts(DV, XT[:, n, :], XT[:, n, :], vec("normf", n), None, ALU.mult, None, [a, AC.last()])
            make_hn(XT[:, n, :], n, vec("attn", n), [b], [hn_free[0]])
            add_sq(XT[:, n, :], n, 1, [b], DV)

        ffn(x_two_norms)
        t_rf = [None]

        def second_norm():
            b0, t0 = sum_sq(0)
            t_rf[0], r = rsqrt_mean(RF[:, :], b0.t[:, 0:T], 2048.0, [t0])
            b0.rel = [r]
            b1, t1 = sum_sq(1)
            i, s, rel = tmp()
            a = tt(DV, s, RF[:, :], RF[:, :], ALU.mult, rel)
            a = tt(DV, s, s, b1.t[:, 0:T], ALU.mult, [t1])
            b1.rel = [a]
            t_ra, r = rsqrt_mean(RSTD[:, :], s, 2048.0, [a])
            tmp_rel[i] = [r]
            t_rstd[0] = tt(DV, RSTD[:, :], RSTD[:, :], RF[:, :], ALU.mult)

        t_b1 = [DV.last(), AC.last(), PE.last()]

        GQ = ar("GQ", [128, 4, T], 0)
        GK = ar("GK", [128, 4, T], 4)
        VTG = ar("VTG", [128, 2, 1024], 8)
        OG = ar("OG", [128, 8, T], 16)
        GG = ar("GG", [128, 4, T], 24)
        GB = ar("GB", [128, 4, T], 28)
        GE = ar("GE", [128, 4, T], 32)
        QE = ar("QE", [128, 4, T], 36)
        GE2 = [GE, ar("GE1", [128, 4, T], 48)]
        QE2 = [QE, ar("QE1", [128, 4, T], 52)]
        KE2 = [GG, ar("KE1", [128, 4, T], 56)]
        OSQ = ar("OSQ", [128, 2, 2 * T], 36)
        OR = ar("OR", [128, 2, T], 32)
        PT = ar("PT", [128, 2, 4, 128], 40)
        PT2 = ar("PT2", [128, 4, 128], 44)
        LM = at("LM", [128, 7, 128], mybir.dt.uint8, arena + 46 * KB)
        RST = ar("RST", [128, T], 47)
        LR = ar("LR", [16, T], 38)
        GW2 = ar("GW2", [16, 512], 36)
        MGH = ar("MGH", [128, 8, T], 48, F32R)
        MGL = ar("MGL", [128, 8, T], 56, F32R)
        NKC = ar("NKC", [128, 2, 2, T], 64)
        NKS = ar("NKS", [128, 2, 2, T], 68)
        NVT = ar("NVT", [128, 2, 2, 256], 72)
        NQA = ar("NQA", [128, 8, T], 76)
        AM = ar("AM", [128, 384], 84)
        MG = Act(MGH, MGL, 8)
        GT = ar("GT", [56, T], 85.5)
        GATE = ar("GATE", [128, 2, 24], 86.5)

        LM4 = ar("LM4", [128, 7, 128], 32, I32)
        t_lm = cp(DV, LM[:, :, :], LM4[:, :, :], [load(LM4[:, :, :], A["lmask"], t_b1)] + t_b1)
        t_rst = load(RST[:, :], A["reset"], t_b1)
        t_gw2 = load(GW2[:, :], A["gla_gate_w2"], t_b1)

        ready = []

        def conv4(dst, j):
            if j == 0:
                for n in range(3):
                    b = mbank()
                    ready.append((b, ntile(b.t[:, 0:T], HN, range(16), b.rel, second_norm if n == 1 else None)))
            if ready:
                b, t = ready.pop(0)
            else:
                b = mbank()
                t = ntile(b.t[:, 0:T], HN, range(16), b.rel)
            i, s, a = scaled(b, t)
            i2, y, rel = tmp()
            c = ts(DV, y, s, vec("gw3", j), None, ALU.mult, None, [a] + rel)
            for m in range(1, 4):
                d = stt(y[:, m:T], s[:, 0:T - m], vec(f"gw{3 - m}", j), y[:, m:T], ALU.mult, ALU.add, [c])
            tmp_rel[i] = [d]

            def silu():
                if dst is None:
                    t_v["v", j - 8] = act(y, y, ACT.Silu, [d])
                else:
                    t_v["g", j] = act(dst, y, ACT.Silu, [d] + t_b1)
                    tmp_rel[i2] = [t_v["g", j]]

            defer(silu)
            return i2, y

        def transpose_v(i2, y, j):
            f = t_v["v", j]
            b = sbank()
            for c in range(2):
                t = tr(b.t[:, c * 128:(c + 1) * 128], y[:, c * 128:(c + 1) * 128], IDENT[:, :], [f] + b.rel,
                       inc=True)
            tmp_rel[i2] = [t]
            for c in range(2):
                a = cp(DV, VTG[:, c, j * 128:(j + 1) * 128], b.t[:, c * 128:(c + 1) * 128], [t] + t_b1)
            b.rel = [a]
            t_v["vtg", j] = a

        for j in range(8):
            conv4((GQ if j < 4 else GK)[:, j % 4, :], j)
            if j == 4:
                t_rtok[0] = rstd_tok(sbank())
        b = mbank()
        t = ntile(b.t[:, 0:T], HN, range(16), b.rel)
        i, s, a = scaled(b, t)
        t_lr = cp(AC, LR[:, :], s[0:16, :], [a] + t_b1)
        t_gt = act(GT[32:56, :], s[32:56, :], ACT.Sigmoid, [a] + t_b1)
        tmp_rel[i] = [t_gt]

        def gates_turned():
            b = sbank()
            for c in range(2):
                t = tr(b.t[:, c * 24:(c + 1) * 24], GT[32:56, c * 128:(c + 1) * 128], IDENT[32:56, 32:56],
                       [t_gt] + b.rel, inc=(c == 1))
            t_v["gate"] = cp(DV, GATE[:, :, :].rearrange("p a n -> p (a n)"), b.t[:, 0:48], [t])
            b.rel = [t_v["gate"]]

        def flat(x):
            return x[:, :, :].rearrange("p a n -> p (a n)")

        def side_gla():
            bz = [sbank(), sbank()]
            for h in range(4):
                t = mm(bz[h // 2].t[:, (h % 2) * T:(h % 2 + 1) * T], GW2[:, h * 128:(h + 1) * 128], LR[:, :],
                       True, True, [t_lr, t_gw2] + bz[h // 2].rel, inc=True)
            t_gq = ts(GP, flat(GQ), flat(GQ), 128.0 ** -0.5, None, ALU.mult, None, [t_v["g", j] for j in range(4)])
            for h in range(4):
                a = ts(DV, GG[:, h, :], bz[h // 2].t[:, (h % 2) * T:(h % 2 + 1) * T], vec("gb", h), None, ALU.add,
                       None, [t])
            bz[0].rel = bz[1].rel = [a]
            a = stt(flat(GE), flat(GG), -1.0, flat(GG), ALU.mult, ALU.max)
            yield
            a = act(flat(GE), flat(GE), ACT.Exp, [a], scale=-1.0)
            a = act(flat(GE), flat(GE), ACT.Ln, [a], bias=1.0)
            yield
            bb = [sbank(), sbank()]
            for c in range(2):
                for h in range(4):
                    t = mm(bb[c].t[:, h * 128:(h + 1) * 128], GK[:, h, c * 128:(c + 1) * 128],
                           GQ[:, h, c * 128:(c + 1) * 128], True, True, [t_gq, t_v["g", 4 + h]] + bb[c].rel,
                           inc=(h == 3))
            a = stt(flat(GG), flat(GG), 0.0, flat(GE), ALU.min, ALU.subtract, [a])
            yield
            a = ts(DV, flat(GG), flat(GG), 1.0 / 16.0, None, ALU.mult)
            for h in range(4):
                a = DV(lambda e, h=h: e.tensor_tensor_scan(GB[:, h, :], RST[:, :], GG[:, h, :], 0.0, ALU.mult,
                                                           ALU.add), [t_rst])
            t_gb = a
            yield
            for c in range(2):
                a = tt(DV, PT[:, c, :, :], bb[c].t[:, :].rearrange("p (a n) -> p a n", a=4),
                       IDENT[:, :].unsqueeze(1).broadcast_to([128, 4, 128]), ALU.mult, [t])
                bb[c].rel = [a]
            free = [None, None]

            t_free = [None, None]
            ready = [None, None]

            def prep(lv):
                p = lv % 2
                ge, qe, ke = GE2[p], QE2[p], KE2[p]
                w = 1 << lv
                g = flat(GB).rearrange("p (n a w) -> p n a w", a=2, w=w)
                e4 = flat(ge).rearrange("p (n a w) -> p n a w", a=2, w=w)
                n = 1024 // (2 * w)
                end = g[:, :, 0, w - 1:w].broadcast_to([128, n, w])
                a0 = tt(DV, e4[:, :, 0, :], end, g[:, :, 0, :], ALU.subtract, [t_free[p]])
                if w < 64:
                    a = tt(GP, e4[:, :, 1, :], g[:, :, 1, :], end, ALU.subtract, [t_gb, t_free[p]])
                else:
                    a = cp(GP, e4[:, :, 1, :], g[:, :, 1, :], [t_gb, t_free[p]])
                yield
                a = act(flat(ge), flat(ge), ACT.Exp, [a0, a])
                yield
                q = tt(DV, flat(qe), flat(GQ), flat(ge), ALU.mult, [a, t_gq, free[p]])
                k = tt(DV, flat(ke), flat(GK), flat(ge), ALU.mult, [a, free[p]])
                t_free[p] = q
                ready[p] = (q, k)

            yield from prep(0)
            for lv in range(7):
                nxt = prep(lv + 1) if lv < 6 else iter(())
                next(nxt, None)
                q, k = ready[lv % 2]
                qe, ke = QE2[lv % 2], KE2[lv % 2]
                bb = [sbank(), sbank()]
                for c in range(2):
                    for h in range(4):
                        t = mm(bb[c].t[:, h * 128:(h + 1) * 128], ke[:, h, c * 128:(c + 1) * 128],
                               qe[:, h, c * 128:(c + 1) * 128], True, True, [k, q] + bb[c].rel,
                               inc=(h == 3))
                free[lv % 2] = t
                yield
                next(nxt, None)
                yield
                next(nxt, None)
                yield
                for c in range(2):
                    m = LM[:, lv, :].unsqueeze(1).broadcast_to([128, 4, 128])
                    t_pt = DV(lambda e, c=c, m=m, src=bb[c].t: e.copy_predicated(
                        PT[:, c, :, :], m, src[:, :].rearrange("p (a n) -> p a n", a=4)), [t, t_lm])
                    bb[c].rel = [t_pt]
                yield
            speed[0] = RO / RG
            ge, qe = GE2[1], QE2[1]
            for h in range(4):
                last2 = GB[:, h, 191:192]
                last1 = GB[:, h, 127:128]
                last0 = GB[:, h, 63:64]
                cp(DV, ge[:, h, 128:192], GB[:, h, 128:192], [free[1], t_free[1]])
                ts(DV, ge[:, h, 192:256], GB[:, h, 192:256], last2, None, ALU.add)
                ts(DV, ge[:, h, 64:128], GB[:, h, 64:128], last1, -1.0, ALU.subtract, ALU.mult)
                ts(DV, ge[:, h, 0:64], GB[:, h, 0:64], last0, -1.0, ALU.subtract, ALU.mult)
                a = ts(DV, ge[:, h, 0:64], ge[:, h, 0:64], last1, None, ALU.add)
            yield
            a = act(flat(ge), flat(ge), ACT.Exp, [a])
            yield
            q = tt(GP, qe[:, :, 128:256], GQ[:, :, 128:256], ge[:, :, 128:256], ALU.mult, [a])
            a = tt(DV, ge[:, :, 0:128], GK[:, :, 0:128], ge[:, :, 0:128], ALU.mult, [a])
            yield
            b = sbank()
            for h in range(4):
                t = mm(b.t[:, h * 128:(h + 1) * 128], ge[:, h, 0:128], qe[:, h, 128:256], True, True,
                       [a, q] + b.rel, inc=(h == 3))
            p = cp(AC, flat(PT2), b.t[:, :], [t])
            b.rel = [p]
            t_ends = [t, p, free[0], free[1], t_free[0], t_free[1], ready[0][1], ready[1][1], a]
            yield

            def outs(h):
                b = sbank()
                w = h % 2
                for v in range(2):
                    cs = slice(h * 256 + v * 128, h * 256 + (v + 1) * 128)
                    o = v * T
                    mm(b.t[:, o:o + 128], VTG[:, 0, cs], PT[:, 0, h, :], True, True,
                       [p, t_pt, t_v["vtg", 2 * h + v]] + b.rel)
                    mm(b.t[:, o + 128:o + 256], VTG[:, 0, cs], PT2[:, h, :], True, False)
                    t = mm(b.t[:, o + 128:o + 256], VTG[:, 1, cs], PT[:, 1, h, :], False, True, inc=(v == 1))
                a = act(OSQ[:, w, :], b.t[:, :], ACT.Square, [t, osq_free[w]] + t_ends)
                return b, a

            def rms(h, b, a):
                w = h % 2
                b2 = sbank()
                for v in range(2):
                    t = mm(b2.t[:, 0:T], ONES[:, :], OSQ[:, w, v * T:(v + 1) * T], v == 0, v == 1, [a] + b2.rel,
                           inc=(v == 1))
                osq_free[w] = t
                ra, rr = rsqrt_mean(OR[:, w, :], b2.t[:, 0:T], 256.0, [t, or_free[w]] + t_ends)
                b2.rel = [rr]
                return b, ra

            def gated_out(h, b, ra):
                w = h % 2
                for v in range(2):
                    i, s, rel = tmp()
                    j = 2 * h + v
                    a = tt(DV, s, b.t[:, v * T:(v + 1) * T], OR[:, w, :], ALU.mult, [ra] + rel)
                    z = stt(s, s, vec("gng", v), OG[:, j, :], ALU.mult, ALU.mult, [t_v["og", j]])
                    split_later(i, MG, j, MGH[:, j, :], MGL[:, j, :], s, [z], t_ends)
                b.rel = or_free[w] = [a]
                or_free[w] = a

            osq_free = [None, None]
            or_free = [None, None]
            o1, o2 = {}, {}
            for h in range(6):
                while h < 4 and (("og", 2 * h + 1) not in t_v or ("vtg", 2 * h + 1) not in t_v):
                    yield
                if h >= 2:
                    gated_out(h - 2, *o2[h - 2])
                if h < 4:
                    o1[h] = outs(h)
                yield
                if 1 <= h < 5:
                    o2[h - 1] = rms(h - 1, *o1[h - 1])
                yield

        def plain(dst, after=()):
            b = mbank()
            t = ntile(b.t[:, 0:T], HN, range(16), b.rel)
            a = tt(DV, dst, b.t[:, 0:T], RSTD[:, :], ALU.mult, [t, t_rstd[0]] + list(after))
            b.rel = [a]
            return a

        def main_second(side):
            held = None
            for j in range(8):
                new = conv4(None, 8 + j)
                if held:
                    transpose_v(*held)
                held = (*new, j)
                for n in (2 * j, 2 * j + 1):
                    t_v["xf", n] = tt(GP, XT[:, n, :], XT[:, n, :], RF[:, :], ALU.mult, [t_rf[0]], chain=False)
                yield
            for j in range(8):
                b = mbank()
                t = ntile(b.t[:, 0:T], HN, range(16), b.rel)
                i, s, a = scaled(b, t)

                def silu(j=j, i=i, s=s, a=a):
                    t_v["og", j] = act(OG[:, j, :], s, ACT.Silu, [a])
                    tmp_rel[i] = [t_v["og", j]]

                defer(silu)
                if j == 0:
                    transpose_v(*held)
                    gates_turned()
                yield
            for name, dst in (("ks", NKS), ("kc", NKC)):
                for m in range(2):
                    for g in range(2):
                        t_v[name, m, g] = plain(dst[:, m, g, :], t_b1)
                        yield
            for m in range(2):
                b, t = npair_tok(HN)
                for c in range(2):
                    a = ts(DV, NVT[:, m, c, :], b.t[:, c * T:(c + 1) * T],
                           RTOK[:, c:c + 1], None, ALU.mult, None, [t, t_rtok[0]] + t_b1)
                b.rel = [a]
                t_v["vs", m, 0] = t_v["vs", m, 1] = a
                yield
                yield
            for m in range(2):
                while ("cb", m) not in t_v:
                    next(side)
                b = mbank()
                x = CB[:, m, :, :, :].rearrange("p a b n -> p a (b n)")
                for l in range(32):
                    t = raw_product(b.t[0:30, 0:128], x, l, t_v["cb", m], l == 0, l == 31, b.rel if l == 0 else ())
                a = act(HIDT[0:30, m, :], b.t[0:30, 0:128], ACT.Silu, [t])
                b.rel = [a]
                t_v["hidt", m] = a
                yield
            for j in range(8):
                t_v["nq", j] = plain(NQA[:, j, :], t_b1)
                yield
            for n in range(16):
                b = mbank()
                t = ntile(b.t[:, 0:T], MG, range(8), b.rel)
                z = tt(DV, XT[:, n, :], XT[:, n, :], b.t[:, 0:T], ALU.add, [t, t_v["xf", n]])
                b.rel = [z]
                t_v["h", n] = z
                yield

        MNH = ar("MNH", [128, 8, T], 0, F32R)
        MNL = ar("MNL", [128, 8, T], 8, F32R)
        CB = ar("CB", [128, 2, 32, 2, 15], 16)
        HIDT = ar("HIDT", [32, 2, 128], 84 + 1.5)
        PCT = ar("PCT", [16, 8, 2, 128], 24)
        PTS = ar("PTS", [128, 2, 2, 384], 16)
        SS = ar("SS", [128, 3, 2, 384], 32)
        NB = ar("NB", [128, 2, 2, 2 * T], 0)
        CW2 = ar("CW2", [128, 2, 128], 42)
        HID = ar("HID", [128, 2, 32], 43)
        POS = ar("POS", [128, 2, 32], 43.25)
        KCN = ar("KCN", [128, 32], 43.5)
        VCN = ar("VCN", [16, 2, 128], 44)
        PC = ar("PC", [128, 16, 16], 45)
        PC2 = ar("PC2", [128, 16, 16], 46)
        CM = ar("CM", [128, 2, 2, 16], 47)
        SMALL = ar("SMALL", [128, 16, 4], 47.25)
        SQQ = ar("SQQ", [128, 2 * T], 22)
        GKQ = ar("GKQ", [128, 4], 86.75)
        RQ = ar("RQ", [128, 16], 41.5)
        STAT = ar("STAT", [128, 3, 4, 4], 47.5)
        MN = Act(MNH, MNL, 8)

        def head_norm(ring, x2, gname, after):
            n = x2.shape[-1]
            k = ring["n"] % 2
            ring["n"] += 1
            sq, rn = NB[:, k, 0, 0:n], NB[:, k, 1, 0:n]
            a = act(sq, x2, ACT.Square, list(after) + [ring["sq", k], ring["rn", k]])
            yield
            b = sbank()
            t = mm(b.t[:, 0:n], ONES[:, :], sq, True, True, [a] + b.rel, inc=True)
            ring["sq", k] = t
            rr = act(rn, b.t[:, 0:n], ACT.Sqrt, [t, ring["rn", k]], bias=EPSC[:, 0:1],
                     scale=1.0 / 128.0)
            b.rel = [rr]
            yield
            h = (n + 1) // 2
            for u in range(2):
                z = recip(rn[:, u * h:min(n, (u + 1) * h)], rn[:, u * h:min(n, (u + 1) * h)], [rr])
            z = stt(x2, x2, GKQ[:, gname:gname + 1], rn, ALU.mult, ALU.mult)
            ring["rn", k] = z
            ring["z"] = z
            yield

        def blocks(m, t_pos):
            for g in range(2):
                win = NKC[:, m, g, :].rearrange("p (n l) -> p l n", l=16)
                for half in range(2):
                    o = CB[:, m, half * 16:(half + 1) * 16, g, :]
                    i1 = POS[:, m, half * 16:(half + 1) * 16].unsqueeze(2).broadcast_to([128, 16, 15])
                    st = tt(DV, o, win[:, :, half:half + 15], i1, ALU.add, [t_v["kc", m, g], t_pos])
            t_v["cb", m] = [st]

        def side_nsa():
            t_gl = [DV.last(), AC.last(), PE.last(), GP.last()]
            t_v["gla"] = t_gl
            yield
            yield
            for E in (DV, AC, GP):
                E.wait(t_gl)
            t_pos = load(POS[:, :, :], A["posT"], t_gl)
            t_cw2 = load(CW2[:, :, :], A["cmp_w2"])
            t_cm = load(CM[:, :, :, :], A["cmask"])
            for i, gn in enumerate(("ksg", "kwg", "kcg")):
                tt(DV, GKQ[:, i:i + 1], vec(gn), vec("qg"), ALU.mult)
            ring = {"n": 0, ("sq", 0): None, ("sq", 1): None, ("rn", 0): None, ("rn", 1): None}

            def norms(jobs):
                live = []
                jobs = list(jobs)
                while jobs or live:
                    for g in list(live):
                        if next(g, live) is live:
                            live.remove(g)
                    if jobs and all(x in t_v for x in jobs[0][-1]) and len(live) < 2:
                        x2, gn, keys = jobs.pop(0)
                        g = head_norm(ring, x2, gn, [t_v[x] for x in keys])
                        next(g)
                        live.append(g)
                    yield

            yield from norms((NKS[:, m, :, :].rearrange("p a n -> p (a n)"), gn, [("ks", m, 0), ("ks", m, 1)])
                             for m, gn in ((0, 0), (1, 1)))
            t_kk = ring["z"]
            while ("kc", 1, 1) not in t_v:
                yield
            blocks(0, t_pos)
            blocks(1, t_pos)
            yield
            while ("hidt", 1) not in t_v:
                yield
            yield
            b = sbank()
            for m in range(2):
                t = tr(b.t[:, m * 32:m * 32 + 30], HIDT[0:30, m, :], IDENT[0:30, 0:30],
                       [t_v["hidt", m]] + b.rel, inc=(m == 1))
            a = cp(DV, HID[:, :, 0:30], b.t[:, 0:64].rearrange("p (m n) -> p m n", m=2)[:, :, 0:30], [t])
            b.rel = [a]
            yield
            b = sbank()
            t = mm(b.t[:, 0:30], CW2[:, 0, :], HID[:, 0, 0:30], True, True, [a, t_cw2] + b.rel, inc=True)
            c0 = cp(DV, KCN[:, 0:30], b.t[:, 0:30], [t])
            b.rel = [c0]
            b = sbank()
            for g in range(2):
                t = mm(b.t[0:15, g * 128:(g + 1) * 128], HID[:, 1, 15 * g:15 * g + 15], CW2[:, 1, :], True, True,
                       b.rel, inc=(g == 1))
            t_vcn = cp(DV, VCN[0:15, :, :].rearrange("p a n -> p (a n)"), b.t[0:15, 0:256], [t])
            b.rel = [t_vcn]
            t_v["kcn"] = c0
            yield from norms([(KCN[:, 0:30], 2, ["kcn"])])
            t_kcn = ring["z"]

            t_pct = {}

            def compressed(g):
                b = sbank()
                for h in range(4 * g, 4 * g + 4):
                    for c in range(2):
                        o = ((h % 4) * 2 + c) * 16
                        t = mm(b.t[:, o:o + 15], NQA[:, h, c * 128:(c + 1) * 128],
                               KCN[:, 15 * g:15 * g + 15], True, True, [t_q[h], t_kcn] + b.rel,
                               inc=(c == 1))
                r = slice(8 * g, 8 * g + 8)
                pc, pc2, sma = PC[:, r, :], PC2[:, r, :], SMALL[:, r, :]
                pc4 = pc.rearrange("p (h c) n -> p h c n", c=2)
                a = tt(DV, pc[:, :, 0:15], b.t[:, 0:128].rearrange("p (r n) -> p r n", n=16)[:, :, 0:15],
                       RQ[:, r].unsqueeze(2).broadcast_to([128, 8, 15]), ALU.mult, [t])
                b.rel = [a]
                for c in range(2):
                    a = tt(DV, pc4[:, :, c, 0:15], pc4[:, :, c, 0:15],
                           CM[:, 0, c, 0:15].unsqueeze(1).broadcast_to([128, 4, 15]), ALU.add, [t_cm])
                DV(lambda e: e.tensor_reduce(sma[:, :, 0], pc[:, :, 0:15], AX.X, ALU.max))
                a = tt(DV, pc[:, :, 0:15], pc[:, :, 0:15], sma[:, :, 0:1].broadcast_to([128, 8, 15]), ALU.subtract)
                a = act(pc2[:, :, 0:15], pc[:, :, 0:15], ACT.Exp, [a])
                yield
                DV(lambda e: e.tensor_reduce(sma[:, :, 1], pc2[:, :, 0:15], AX.X, ALU.add), [a])
                recip(sma[:, :, 2], sma[:, :, 1])
                sm = sma.rearrange("p (h c) n -> p h c n", c=2)
                for c in range(2):
                    gt = GATE[:, c, 12 * g:12 * g + 12].rearrange("p (h r) -> p h r", r=3)
                    tt(DV, sm[:, :, c, 3], sm[:, :, c, 2], gt[:, :, 0], ALU.mult, [t_v["gate"]])
                a = tt(DV, pc2[:, :, 0:15], pc2[:, :, 0:15], sma[:, :, 3:4].broadcast_to([128, 8, 15]), ALU.mult)
                p4 = pc2.rearrange("p (h c) n -> p h c n", c=2)
                for c in range(2):
                    a = tt(DV, p4[:, :, c, 0:15], p4[:, :, c, 0:15],
                           CM[:, 1, c, 0:15].unsqueeze(1).broadcast_to([128, 4, 15]), ALU.mult)
                yield
                for q in (2 * g, 2 * g + 1):
                    b = sbank()
                    for m in range(4):
                        hc = 4 * q + m
                        t = tr(b.t[0:15, m * 128:(m + 1) * 128], PC2[:, hc, 0:15], IDENT[:, :], [a] + b.rel,
                               inc=(m == 3))
                    c0 = cp(AC, PCT[0:15, 2 * q:2 * q + 2, :, :].rearrange("p a b n -> p (a b n)"),
                            b.t[0:15, :], [t])
                    b.rel = [c0]
                    t_pct[2 * q] = t_pct[2 * q + 1] = c0
                    yield

            t_q = {}

            def query_norms():
                for j in range(0, 8, 2):
                    while ("nq", j + 1) not in t_v:
                        yield
                    sq = SQQ[:, :]
                    a = act(sq, NQA[:, j:j + 2, :].rearrange("p a n -> p (a n)"), ACT.Square,
                            [t_v["nq", j], t_v["nq", j + 1], ring["sq", 0], t_v["hidt", 1]])
                    yield
                    b = sbank()
                    for i in range(4):
                        t = mm(b.t[:, i:i + 1], sq[:, i * 128:(i + 1) * 128], ONES[:, 0:1], True, True,
                               [a] + b.rel, inc=(i == 3))
                    ring["sq", 0] = t
                    yield
                    rq = RQ[:, 2 * j:2 * j + 4]
                    a = act(rq, b.t[:, 0:4], ACT.Sqrt, [t], bias=EPSC[:, 1:2], scale=1.0)
                    b.rel = [a]
                    t_q[j] = t_q[j + 1] = recip(rq, rq, [a])
                    yield

            qn = query_norms()

            t_am = t_amask

            def scores(h):
                out = []
                for m in range(2):
                    b = sbank()
                    g = h // 4
                    for c in range(2):
                        n = 128 * (c + 1)
                        o = 128 * c
                        t = mm(b.t[:, o:o + n], NQA[:, h, c * 128:(c + 1) * 128], NKS[:, m, g, 0:n], True, True,
                               [t_kk, t_q[h]] + b.rel, inc=(c == 1))
                    out.append((b, t))
                return out

            ss_free = [None, None, None]
            pts_free = [None, None]

            def soft(h, bt, key):
                w = h % 3
                s = SS[:, w, :, :]
                st = STAT[:, w, :, :]
                for m, (b, t) in enumerate(bt):
                    for c in range(2):
                        x = slice(128 * c, 128 + 256 * c)
                        a = stt(s[:, m, x], b.t[:, x], RQ[:, 2 * h + c:2 * h + c + 1], AM[:, x], ALU.mult, ALU.add,
                                [t, t_am, ss_free[w]])
                    b.rel = [a]
                xs = [s[:, :, 0:128], s[:, :, 128:384]]
                for c in range(2):
                    a = DV(lambda e, x=xs[c], o=st[:, 2 * c:2 * c + 2, 0]: e.tensor_reduce(
                        o, x, AX.X, ALU.max, negate=True))
                yield
                for c in range(2):
                    for m in range(2):
                        x = xs[c][:, m, :]
                        q = 2 * c + m
                        e1 = act(x, x, ACT.Exp, [a], bias=st[:, q, 0:1], accum=st[:, q, 1:2])
                yield
                recip(st[:, :, 2], st[:, :, 1], [e1])
                for c in range(2):
                    a = tt(DV, st[:, 2 * c:2 * c + 2, 3], st[:, 2 * c:2 * c + 2, 2],
                           GATE[:, c, 3 * h + 1:3 * h + 3], ALU.mult)
                for c in range(2):
                    n = 128 * (c + 1)
                    p = tt(DV, xs[c], xs[c], st[:, 2 * c:2 * c + 2, 3:4].broadcast_to([128, 2, n]), ALU.mult, [a])
                key[h] = p

            def turnp(h, a):
                w = h % 2
                out = []
                for m in range(2):
                    b = sbank()
                    for k in range(3):
                        t = tr(b.t[:, k * 128:(k + 1) * 128], SS[:, h % 3, m, k * 128:(k + 1) * 128], IDENT[:, :],
                               [a] + b.rel, inc=(k == 2))
                    a2 = cp(AC if m else DV, PTS[:, w, m, :], b.t[:, 0:384], [t, pts_free[w]])
                    b.rel = [a2]
                    out.append(a2)
                ss_free[h % 3] = t
                return out

            def values(h, pp):
                w = h % 2
                b = sbank()
                g = h // 4
                mm(b.t[:, 0:T], VCN[0:15, g, :], PCT[0:15, h, :, :].rearrange("p a n -> p (a n)"), True, False,
                   [t_vcn, t_pct[h]] + b.rel, skip=True)
                for m in range(2):
                    mm(b.t[:, 0:T], NVT[:, m, 0, g * 128:(g + 1) * 128], PTS[:, w, m, 0:256], False, False,
                       [pp[m], t_v["vs", m, g]], skip=True)
                    t = mm(b.t[:, 128:T], NVT[:, m, 1, g * 128:(g + 1) * 128], PTS[:, w, m, 256:384], False, m == 1,
                           inc=(m == 1), skip=True)
                pts_free[w] = t
                hi = cp(AC, MNH[:, h, :], b.t[:, 0:T], [t, t_kcn])
                lo = tt(DV, MNL[:, h, :], b.t[:, 0:T], f32(MNH[:, h, :]), ALU.subtract, [hi])
                b.rel = [lo]
                MN.t[h] = [hi, lo]

            soft_t, turn_t = {}, {}

            def heads():
                for h in range(11):
                    while h < 8 and h not in t_q:
                        yield
                    if h >= 3:
                        while h - 3 not in t_pct:
                            yield
                        values(h - 3, turn_t[h - 3])
                        yield
                    if 2 <= h < 10:
                        turn_t[h - 2] = turnp(h - 2, soft_t[h - 2])
                    yield
                    if h < 8:
                        yield from soft(h, scores(h), soft_t)
                        yield

            def comp():
                for g in range(2):
                    while 4 * g + 3 not in t_q:
                        yield
                    yield from compressed(g)

            live = [qn, comp(), heads()]
            while live:
                for g in list(live):
                    if next(g, live) is live:
                        live.remove(g)
                yield

        def side_second():
            yield from side_gla()
            speed[0] = RN / RG
            yield from side_nsa()

        t_amask = load(AM[:, :], A["amask"], t_b1)
        side = side_second()
        run(main_second(side), side, RG)
        for _ in side:
            pass
        hn_free[0] = PE.last()
        f = norm_after("ffn")
        for n in range(16):
            residual(MN, range(8), [t_v["h", n]], n, f)

        out_tickets = []

        def store(n, a):
            s = out_sem[n % 4]
            SP.wait([a])
            SP.todo.append(lambda e, n=n, s=s: e.dma_start(out[:, n, :], XT[:, n, :]).then_inc(s, 16))
            out_tickets.append((s, 16 * (n // 4 + 1)))

        out_sem = [sem(f"s_out{i}") for i in range(4)]
        ffn(store)
        SP.wait(out_tickets[-4:])
        assert tile_at[0] == len(order) * RU, (tile_at[0], len(order) * RU)

        block = ctx.enter_context(nc.Block())

        @block.sync
        def _(e):
            SP.play(e)

        @block.gpsimd
        def _(e):
            GP.play(e)

        @block.scalar
        def _(e):
            AC.play(e)

        @block.vector
        def _(e):
            DV.play(e)

        @block.tensor
        def _(e):
            PE.play(e)


def tiles(w, kt=None):
    K, N = w.shape
    t = w.reshape(K // 128, 128, N // 128, 128).transpose(2, 0, 1, 3)
    return t.reshape(-1, 128, 128)


def pairs(w):
    K, N = w.shape
    return w.reshape(K // 128, 128, N // 256, 2, 128).transpose(2, 0, 3, 1, 4).reshape(-1, 128, 128)


def units(t):
    return np.ascontiguousarray(t.reshape(-1, RU, 128, 128).transpose(0, 2, 1, 3)).reshape(-1, 128, RU * 128)


def gated(w, b):
    ta = tiles(w).reshape(-1, w.shape[0] // 128, 128, 128)
    tb = tiles(b).reshape(-1, b.shape[0] // 128, 128, 128)
    return units(np.concatenate([ta, tb], axis=1).reshape(-1, 128, 128))


def down(w):
    t = tiles(w).reshape(16, 2, 22, 128, 128).transpose(1, 0, 2, 3, 4)
    return units(t.reshape(-1, 128, 128))


def padded(w, n=128):
    return np.pad(w, ((0, 0), (0, n - w.shape[1])))


def cols(v):
    return np.ascontiguousarray(v.reshape(-1, 128).T)


def consts():
    L = 256
    f = np.float64
    t = np.arange(L, dtype=f)[:, None]
    m = np.arange(L, dtype=f)[None, :]
    ang = 2.0 * np.pi * (m + 0.5) * t / 512.0
    C, S = np.cos(ang), np.sin(ang)
    c = {}
    half = np.stack([C, S])[:, :, 0:128].reshape(2, 128, 2, 128)
    c["df"] = half.transpose(1, 2, 0, 3).astype(np.float32)
    c["dg"] = (half * np.array([1.0, -1.0]).reshape(2, 1, 1, 1) / 256.0).transpose(3, 0, 2, 1).astype(np.float32)
    tl = np.linspace(0.0, 1.0, L, dtype=np.float32)[:, None]
    om = (np.float32(2.0 * math.pi) * np.arange(L, dtype=np.float32) / np.float32(L)).astype(np.float32)
    fr = np.linspace(1e-4, 15, 16, dtype=np.float32)
    an = (om[:, None] * fr[None, :]).astype(np.float32).astype(f)
    z = np.concatenate([tl, np.cos(an), -np.sin(an)], axis=1).astype(np.float32)
    c["zt"] = np.ascontiguousarray(z.reshape(128, 2, 33).transpose(1, 0, 2).reshape(256, 33).T)
    d = np.linspace(math.log(1e-2) / 1.5, math.log(1e-2) / 0.3, 1024, dtype=np.float32)
    win = np.exp((-tl * np.abs(d)[None, :]).astype(f)).astype(np.float32)
    wb = win.copy()
    wb[0] = 0.0
    w2 = np.stack([win, wb], axis=1).reshape(128, 2, 2, 4, 256)
    c["win"] = w2.transpose(3, 0, 1, 2, 4)
    p = np.arange(128)
    j = np.arange(L)
    mk = np.zeros((128, 2, 2, L), np.float32)
    for h in range(2):
        s = (h * 128 + p)[:, None]
        mk[:, 0, h] = np.where(s <= j[None, :], 0.0, NEG)
        mk[:, 1, h] = np.where(s >= j[None, :], 0.0, NEG)
    c["mmask"] = mk
    sel = np.zeros((4, 4, 128), np.float32)
    for h in range(4):
        sel[h, h] = 1.0
    c["sel4"] = sel
    lm = np.zeros((128, 7, 128), np.int32)
    s, q = p[:, None], p[None, :]
    for lv in range(7):
        w = 1 << lv
        lm[:, lv] = (s // (2 * w) == q // (2 * w)) & (s // w % 2 == 0) & (q // w % 2 == 1)
    c["lmask"] = lm
    r = np.ones((128, L), np.float32)
    r[:, ::64] = 0.0
    c["reset"] = r
    cm = np.zeros((128, 2, 2, 16), np.float32)
    for h in range(2):
        ok = (16 * np.arange(16)[None, :] + 31) <= (h * 128 + p)[:, None]
        cm[:, 0, h] = np.where(ok, 0.0, NEG)
        cm[:, 1, h] = ok
    c["cmask"] = cm
    am = np.zeros((128, 384), np.float32)
    dm = np.where(q <= s, 0.0, NEG)
    am[:, 0:128] = dm
    am[:, 256:384] = dm
    c["amask"] = am
    c["ident"] = np.eye(128, dtype=np.float32)
    return {k: np.ascontiguousarray(v) for k, v in c.items()}


def kernel(**inputs):
    import concourse.bacc as bacc
    from concourse.bass_utils import run_bass_kernel_spmd as launch

    x = {k: np.asarray(v) for k, v in inputs.items()}
    one = {k: (v[0] if k != "norm_f_w" else v) for k, v in x.items()}
    a = consts()
    w = one["w_in"]
    a["w_in_a"] = units(np.concatenate([tiles(w[:, 0:5120]), tiles(padded(w[:, 7168:7184])),
                                        pairs(w[:, 5120:6144]), tiles(w[:, 6144:7168])]))
    a["w_ga"] = gated(w[:, 7184:9232], one["w_branch_a"])
    a["w_gb"] = gated(w[:, 9232:11280], one["w_branch_b"])
    a["w_out"] = units(tiles(one["w_out"]))
    gu = one["w_gate_up"]
    a["w_gu"] = gated(gu[:, 0:5632], gu[:, 5632:])
    a["w_dn"] = down(one["w_down"])
    w = one["w_in_2"]
    a["w_in2"] = units(np.concatenate([tiles(m) for m in (
        w[:, 0:1024], padded(np.concatenate([padded(w[:, 2048:2064], 32), w[:, 5648:5672]], axis=1)), w[:, 1024:2048], w[:, 2064:3088], w[:, 4624:4880],
        w[:, 5136:5392], w[:, 4112:4624])] + [
            pairs(w[:, 4880:5136]), pairs(w[:, 5392:5648]), tiles(w[:, 3088:4112])]))
    a["w_cmp"] = units(np.concatenate([one["cmp_k_w1_2"].reshape(32, 128, 128),
                                       one["cmp_v_w1_2"].reshape(32, 128, 128)]))
    a["cmp_w2"] = np.ascontiguousarray(np.stack([one["cmp_k_w2_2"], one["cmp_v_w2_2"]], axis=1))
    a["posT"] = np.ascontiguousarray(np.stack([one["cmp_k_pos_2"].T, one["cmp_v_pos_2"].T], axis=1))
    w = one["w_out_2"]
    a["w_out2"] = units(np.concatenate([tiles(w[0:1024]), tiles(w[1024:2048])]))
    a["w_gu2"] = gated(one["w_gate_2"], one["w_up_2"])
    a["w_dn2"] = down(one["w_down_2"])
    a["filt_w1"] = np.ascontiguousarray(one["filt_w1"])
    a["filt_w2"] = np.ascontiguousarray(one["filt_w2"])
    a["filt_w3"] = np.ascontiguousarray(one["filt_w3"].reshape(64, 2, 2, 1024))
    a["gla_gate_w2"] = np.ascontiguousarray(one["gla_gate_w2_2"])
    a["xT"] = np.ascontiguousarray(x["x"][0].T.reshape(16, 128, 256).transpose(1, 0, 2))

    v = np.zeros((128, NVEC), np.float32)

    def put(name, m):
        n, k = VECS[name]
        v[0:m.shape[0], n:n + k] = m

    put("norm1", cols(one["norm1_w"]))
    put("norm2", cols(one["norm2_w"]))
    put("normf", cols(one["norm_f_w"]))
    put("attn", cols(one["attn_norm_g_2"]))
    put("ffn", cols(one["ffn_norm_g_2"]))
    for i in range(3):
        put(f"cw{i}", cols(one["conv_w"][i]))
    put("cb", cols(one["conv_b"]))
    put("hb", cols(one["hyena_bias"].reshape(-1)))
    for i in range(4):
        put(f"gw{i}", cols(one["gla_conv_w_2"][i]))
    put("gb", cols(one["gla_gate_b_2"]))
    put("gng", cols(one["gla_norm_g_2"]))
    put("qg", cols(one["nsa_q_norm_g_2"]))
    put("kcg", cols(one["nsa_kc_norm_g_2"]))
    put("ksg", cols(one["nsa_ks_norm_g_2"]))
    put("kwg", cols(one["nsa_kw_norm_g_2"]))
    put("f1", one["filt_freq1"].reshape(64, 1))
    put("b1", one["filt_b1"].reshape(64, 1))
    put("f2", one["filt_freq2"].reshape(64, 1))
    put("b2", one["filt_b2"].reshape(64, 1))
    put("gbias", one["mlstm_gate_bias"].reshape(16, 1))
    a["vecs"] = v

    nc = bacc.Bacc("TRN2", target_bir_lowering=False, num_devices=1)
    arrays, aps = {}, {}
    for k, m in a.items():
        arrays[f"in_{k}"] = m
        aps[k] = nc.dram_tensor(f"in_{k}", m.shape, mybir.dt.from_np(m.dtype), kind="ExternalInput").ap()
    out = nc.dram_tensor("out_x", (128, 16, 256), F32, kind="ExternalOutput").ap()
    build(nc, aps, out)
    r = launch(nc, [arrays], core_ids=[0])
    got = r.results[0]["out_x"]
    return np.ascontiguousarray(got.transpose(1, 0, 2).reshape(2048, 256).T).reshape(1, 256, 2048)
```
